# Optimizing a Trainium2 kernel written in Bass

```python
import jax, jax.numpy as jnp
from jax import lax
import numpy as np

D_MODEL = 1024
BATCH = 1
SEQ = 256
DEPTH = 2

CHUNK = 64
Q_BLOCK = 128
N_MIXERS = 2
EPS = 1e-6
A_HEADS = 8
A_LAT = 128
IDX_HEADS = 8
IDX_DIM = 64
TOPK_MAX = 256
A_Q_COLS = A_HEADS * A_LAT
A_IN_COLS = A_Q_COLS + A_LAT + IDX_HEADS * IDX_DIM + IDX_DIM + IDX_HEADS
B_HEADS = D_MODEL // 256
B_DK = D_MODEL // B_HEADS
B_DV = 2 * B_DK
B_IN_COLS = 2 * D_MODEL + 2 * (B_HEADS * B_DV)
ROPE_BASE = 10000.0
D_FF = 2816
CONV_W = 3
N_A = (DEPTH + N_MIXERS - 1) // N_MIXERS
N_B = DEPTH // N_MIXERS


def rms_norm(x, g):
    xf = x.astype(jnp.float32)
    y = xf * lax.rsqrt(jnp.mean(xf * xf, axis=-1, keepdims=True) + EPS)
    return (y * g.astype(jnp.float32)).astype(x.dtype)

def dsa_mixer(h, w_in, q_g, k_g, iq_g, ik_g, w_out):
    bsz, seq, _ = h.shape
    topk = min(TOPK_MAX, seq // 4)
    proj = h @ w_in
    o1 = A_Q_COLS
    o2 = o1 + A_LAT
    o3 = o2 + IDX_HEADS * IDX_DIM
    o4 = o3 + IDX_DIM
    q = proj[..., :o1].reshape(bsz, seq, A_HEADS, A_LAT)
    c = proj[..., o1:o2]
    qi = proj[..., o2:o3].reshape(bsz, seq, IDX_HEADS, IDX_DIM)
    ki = rms_norm(proj[..., o3:o4], ik_g)
    wi = proj[..., o4:] * (IDX_HEADS ** -0.5 * IDX_DIM ** -0.5)
    q = rms_norm(q, q_g) * (A_LAT ** -0.5)
    k = rms_norm(c, k_g)
    qi = rms_norm(qi, iq_g)

    nb = seq // Q_BLOCK

    def to_blocks(a):
        return a.reshape(bsz, nb, Q_BLOCK, *a.shape[2:]).swapaxes(0, 1)

    t_blk = jnp.arange(seq, dtype=jnp.int32).reshape(nb, Q_BLOCK)
    key_pos = jnp.arange(seq, dtype=jnp.int32)
    gather = jax.vmap(lambda a, idx: a[idx])

    def block(args):
        qb, qib, wb, tb = args
        limit = (tb // CHUNK + 1) * CHUNK
        admissible = key_pos[None, :] < limit[:, None]
        rel = jax.nn.relu(jnp.einsum('bqhd,bsd->bqhs', qib, ki).astype(jnp.float32))
        score = jnp.einsum('bqhs,bqh->bqs', rel, wb.astype(jnp.float32))
        score = jnp.where(admissible[None], score, -jnp.inf)
        _, idx = lax.top_k(score, topk)
        valid = idx < limit[None, :, None]
        k_sel = gather(k, idx)
        v_sel = gather(c, idx)
        logits = jnp.einsum('bqhd,bqkd->bqhk', qb, k_sel).astype(jnp.float32)
        logits = jnp.where(valid[:, :, None, :], logits, -jnp.inf)
        p = jax.nn.softmax(logits, axis=-1).astype(v_sel.dtype)
        return jnp.einsum('bqhk,bqkd->bqhd', p, v_sel)

    o = lax.map(block, (to_blocks(q), to_blocks(qi), to_blocks(wi), t_blk))
    o = o.swapaxes(0, 1).reshape(bsz, seq, A_Q_COLS)
    return o @ w_out

def rotary(x):
    seq, d = x.shape[1], x.shape[-1]
    inv = 1.0 / (ROPE_BASE ** (jnp.arange(0, d, 2, dtype=jnp.float32) / d))
    ang = jnp.arange(seq, dtype=jnp.float32)[:, None] * inv[None, :]
    cos = jnp.cos(ang)[None, :, None, :]
    sin = jnp.sin(ang)[None, :, None, :]
    xf = x.astype(jnp.float32)
    x1, x2 = xf[..., : d // 2], xf[..., d // 2:]
    return jnp.concatenate([x1 * cos - x2 * sin, x1 * sin + x2 * cos], axis=-1)

def retention_mixer(h, w_in, out_g, w_out):
    bsz, seq, _ = h.shape
    nc = seq // CHUNK
    proj = h @ w_in
    dq = B_HEADS * B_DK
    dv = B_HEADS * B_DV
    q = rotary(proj[..., :dq].reshape(bsz, seq, B_HEADS, B_DK))
    k = rotary(proj[..., dq:2 * dq].reshape(bsz, seq, B_HEADS, B_DK)) * (B_DK ** -0.5)
    v = proj[..., 2 * dq:2 * dq + dv].reshape(bsz, seq, B_HEADS, B_DV).astype(jnp.float32)
    g = proj[..., 2 * dq + dv:]

    log_gamma = jnp.log1p(-(2.0 ** (-5.0 - jnp.arange(B_HEADS, dtype=jnp.float32))))
    pos = jnp.arange(CHUNK, dtype=jnp.float32)
    diff = pos[:, None] - pos[None, :]
    decay_intra = jnp.where(diff[None] >= 0,
                            jnp.exp(jnp.maximum(diff, 0.0)[None] * log_gamma[:, None, None]), 0.0)
    xi = jnp.exp((pos + 1.0)[:, None] * log_gamma[None, :])
    zeta = jnp.exp((CHUNK - 1.0 - pos)[:, None] * log_gamma[None, :])
    gamma_c = jnp.exp(CHUNK * log_gamma)

    qc = q.reshape(bsz, nc, CHUNK, B_HEADS, B_DK)
    kc = k.reshape(bsz, nc, CHUNK, B_HEADS, B_DK)
    vc = v.reshape(bsz, nc, CHUNK, B_HEADS, B_DV)
    s = jnp.einsum('bnqhd,bnkhd->bnhqk', qc, kc) * decay_intra[None, None]
    intra = jnp.einsum('bnhqk,bnkhe->bnqhe', s, vc)

    def step(state, inp):
        qn, kn, vn = inp
        cross = jnp.einsum('bqhd,bhde->bqhe', qn, state) * xi[None, :, :, None]
        state = state * gamma_c[None, :, None, None] + jnp.einsum(
            'bkhd,bkhe->bhde', kn * zeta[None, :, :, None], vn)
        return state, cross

    state0 = jnp.zeros((bsz, B_HEADS, B_DK, B_DV), jnp.float32)
    _, cross = lax.scan(step, state0, (qc.swapaxes(0, 1), kc.swapaxes(0, 1), vc.swapaxes(0, 1)))
    ret = (intra + cross.swapaxes(0, 1)).reshape(bsz, seq, B_HEADS, B_DV)
    ret = rms_norm(ret, out_g.reshape(B_HEADS, B_DV)).reshape(bsz, seq, dv)
    y = ret * jax.nn.silu(g.astype(jnp.float32))
    return y.astype(h.dtype) @ w_out

def conv_ffn(h, w_up, conv_w, conv_b, w_down):
    seq = h.shape[1]
    u = h @ w_up
    up = jnp.pad(u, ((0, 0), (CONV_W - 1, 0), (0, 0)))
    u = sum(up[:, j:j + seq] * conv_w[j] for j in range(CONV_W)) + conv_b
    a, b = u[..., :D_FF], u[..., D_FF:]
    return (jax.nn.silu(a) * b) @ w_down

def first_inputs(seed: int = 0) -> dict:
    key = jax.random.key(seed)
    ks = jax.random.split(key, 16)

    def nrm(k, shape, scale):
        return jax.random.normal(k, shape, jnp.float32) * scale

    return {
        'x': nrm(ks[0], (BATCH, SEQ, D_MODEL), 1.0),
        'norm_mix_g': 1.0 + nrm(ks[1], (DEPTH, D_MODEL), 0.02),
        'norm_ffn_g': 1.0 + nrm(ks[2], (DEPTH, D_MODEL), 0.02),
        'a_w_in': nrm(ks[3], (N_A, D_MODEL, A_IN_COLS), D_MODEL ** -0.5),
        'a_q_g': 1.0 + nrm(ks[4], (N_A, A_LAT), 0.02),
        'a_k_g': 1.0 + nrm(ks[5], (N_A, A_LAT), 0.02),
        'a_iq_g': 1.0 + nrm(ks[6], (N_A, IDX_DIM), 0.02),
        'a_ik_g': 1.0 + nrm(ks[7], (N_A, IDX_DIM), 0.02),
        'a_w_out': nrm(ks[8], (N_A, A_Q_COLS, D_MODEL), A_Q_COLS ** -0.5),
        'b_w_in': nrm(ks[9], (N_B, D_MODEL, B_IN_COLS), D_MODEL ** -0.5),
        'b_out_g': 1.0 + nrm(ks[10], (N_B, B_HEADS * B_DV), 0.02),
        'b_w_out': nrm(ks[11], (N_B, B_HEADS * B_DV, D_MODEL), (B_HEADS * B_DV) ** -0.5),
        'f_w_up': nrm(ks[12], (DEPTH, D_MODEL, 2 * D_FF), D_MODEL ** -0.5),
        'f_conv_w': nrm(ks[13], (DEPTH, CONV_W, 2 * D_FF), CONV_W ** -0.5),
        'f_conv_b': nrm(ks[14], (DEPTH, 2 * D_FF), 0.01),
        'f_w_down': nrm(ks[15], (DEPTH, D_FF, D_MODEL), D_FF ** -0.5),
    }

def first_block(x, norm_mix_g, norm_ffn_g, a_w_in, a_q_g, a_k_g, a_iq_g, a_ik_g, a_w_out,
              b_w_in, b_out_g, b_w_out, f_w_up, f_conv_w, f_conv_b, f_w_down):
    for i in range(DEPTH):
        h = rms_norm(x, norm_mix_g[i])
        j = i // N_MIXERS
        if i % N_MIXERS == 0:
            x = x + dsa_mixer(h, a_w_in[j], a_q_g[j], a_k_g[j], a_iq_g[j], a_ik_g[j], a_w_out[j])
        else:
            x = x + retention_mixer(h, b_w_in[j], b_out_g[j], b_w_out[j])
        x = x + conv_ffn(rms_norm(x, norm_ffn_g[i]), f_w_up[i], f_conv_w[i], f_conv_b[i], f_w_down[i])
    return x


DEPTH_2 = 1

D_INNER = 2 * D_MODEL
SSD_HEAD_DIM = 64
SSD_HEADS = D_INNER // SSD_HEAD_DIM
SSD_GROUPS = 4
SSD_HEADS_PER_GROUP = SSD_HEADS // SSD_GROUPS
SSD_STATE = 128
CONV_WIDTH = 4
CHUNK_2 = 128
XBC_WIDTH = D_INNER + 2 * SSD_GROUPS * SSD_STATE
DT_MIN = 0.001
DT_MAX = 0.1
POOL_WINDOWS = (2, 4, 8, 16)
POOL_GROUPS = len(POOL_WINDOWS)
POOL_WIDTH = D_MODEL
POOL_GROUP_WIDTH = POOL_WIDTH // POOL_GROUPS
N_BRANCHES = 2
D_FF_2 = 4 * D_MODEL
N_MOD = 6
NORM_EPS = 1e-5
IN_SPLITS = (D_INNER,
             D_INNER + XBC_WIDTH,
             D_INNER + XBC_WIDTH + SSD_HEADS,
             D_INNER + XBC_WIDTH + SSD_HEADS + POOL_WIDTH)
IN_COLS = IN_SPLITS[-1] + N_BRANCHES * D_MODEL


def rmsnorm(x, w, eps=NORM_EPS):
    x32 = x.astype(jnp.float32)
    y = x32 * lax.rsqrt(jnp.mean(x32 * x32, axis=-1, keepdims=True) + eps)
    return y.astype(x.dtype) * w

def causal_depthwise_conv(u, w, b):
    k_width = w.shape[0]
    seq = u.shape[1]
    up = jnp.pad(u, ((0, 0), (k_width - 1, 0), (0, 0)))
    out = b
    for k in range(k_width):
        out = out + up[:, k:k + seq] * w[k]
    return out

def segsum_decay(a_cs):
    q = a_cs.shape[-1]
    seg = a_cs[..., :, None] - a_cs[..., None, :]
    mask = jnp.tril(jnp.ones((q, q), dtype=bool))
    return jnp.exp(jnp.where(mask, seg, -jnp.inf))

def ssd_chunked_scan(xdt, dtA, bmat, cmat):
    b, seq, _, p = xdt.shape
    g, hg, n, q = SSD_GROUPS, SSD_HEADS_PER_GROUP, SSD_STATE, CHUNK_2
    nc = seq // q
    x = xdt.astype(jnp.float32).reshape(b, nc, q, g, hg, p)
    a = dtA.astype(jnp.float32).reshape(b, nc, q, g, hg).transpose(0, 3, 4, 1, 2)
    bc = bmat.astype(jnp.float32).reshape(b, nc, q, g, n)
    cc = cmat.astype(jnp.float32).reshape(b, nc, q, g, n)
    a_cs = jnp.cumsum(a, axis=-1)
    scores = jnp.einsum('bclgn,bcsgn->bgcls', cc, bc)
    mmat = scores[:, :, None] * segsum_decay(a_cs)
    y_diag = jnp.einsum('bghcls,bcsghp->bclghp', mmat, x)
    decay_states = jnp.exp(a_cs[..., -1:] - a_cs)
    states = jnp.einsum('bcsgn,bghcs,bcsghp->bcghpn', bc, decay_states, x)
    chunk_decay = jnp.exp(a_cs[..., -1])

    def step(h, inp):
        s_c, d_c = inp
        return h * d_c[..., None, None] + s_c, h

    h0 = jnp.zeros((b, g, hg, p, n), jnp.float32)
    _, prev = lax.scan(step, h0, (jnp.moveaxis(states, 1, 0), jnp.moveaxis(chunk_decay, 3, 0)))
    prev = jnp.moveaxis(prev, 0, 1)
    y_off = jnp.einsum('bclgn,bcghpn,bghcl->bclghp', cc, prev, jnp.exp(a_cs))
    return (y_diag + y_off).reshape(b, seq, SSD_HEADS, p)

def causal_multiscale_pool(u, pool_w, pool_scale):
    b, seq, _ = u.shape
    gw = POOL_GROUP_WIDTH
    u32 = u.astype(jnp.float32)
    cs = jnp.concatenate([jnp.zeros((b, 1, POOL_WIDTH), jnp.float32), jnp.cumsum(u32, axis=1)], axis=1)
    count = jnp.arange(1, seq + 1, dtype=jnp.float32)[:, None]
    outs = []
    for gi, win in enumerate(POOL_WINDOWS):
        csg = cs[:, :, gi * gw:(gi + 1) * gw]
        start = jnp.concatenate([jnp.zeros((b, win - 1, gw), jnp.float32), csg[:, :seq - win + 1]], axis=1)
        mean = (csg[:, 1:] - start) / jnp.minimum(count, float(win))
        outs.append(mean - u32[..., gi * gw:(gi + 1) * gw])
    pooled = jnp.stack(outs, axis=2).astype(u.dtype)
    y = jnp.einsum('blgc,gcd->blgd', pooled, pool_w).reshape(b, seq, POOL_WIDTH)
    return y * pool_scale

def hybrid_mixer(h, w_in, conv_w, conv_b, dt_bias, a_log, d_skip, ssd_norm_w,
                 w_branch_ssd, pool_w, pool_scale, w_branch_pool, w_out):
    b, seq, _ = h.shape
    proj = h @ w_in
    z, xbc, dt_raw, u_pool, gate_logits = jnp.split(proj, IN_SPLITS, axis=-1)
    xbc = jax.nn.silu(causal_depthwise_conv(xbc, conv_w, conv_b))
    xs, bmat, cmat = jnp.split(xbc, (D_INNER, D_INNER + SSD_GROUPS * SSD_STATE), axis=-1)
    xs = xs.reshape(b, seq, SSD_HEADS, SSD_HEAD_DIM)
    bmat = bmat.reshape(b, seq, SSD_GROUPS, SSD_STATE)
    cmat = cmat.reshape(b, seq, SSD_GROUPS, SSD_STATE)
    dt = jax.nn.softplus(dt_raw.astype(jnp.float32) + dt_bias.astype(jnp.float32))
    a_cont = -jnp.exp(a_log.astype(jnp.float32))
    x32 = xs.astype(jnp.float32)
    y = ssd_chunked_scan(x32 * dt[..., None], dt * a_cont, bmat, cmat)
    y = y + d_skip.astype(jnp.float32)[:, None] * x32
    y = y.reshape(b, seq, D_INNER).astype(h.dtype) * jax.nn.silu(z)
    y = rmsnorm(y.reshape(b, seq, SSD_GROUPS, D_INNER // SSD_GROUPS),
                ssd_norm_w.reshape(SSD_GROUPS, D_INNER // SSD_GROUPS))
    y_ssd = y.reshape(b, seq, D_INNER) @ w_branch_ssd
    y_pool = causal_multiscale_pool(u_pool, pool_w, pool_scale) @ w_branch_pool
    g_ssd, g_pool = jnp.split(jax.nn.sigmoid(gate_logits), N_BRANCHES, axis=-1)
    return (g_ssd * y_ssd + g_pool * y_pool) @ w_out

def second_inputs(seed: int = 0) -> dict:
    key = jax.random.key(seed)
    ks = jax.random.split(key, 24)
    f32 = jnp.float32
    nrm = lambda k, shape, s: jax.random.normal(k, shape, f32) * s
    dt0 = jnp.exp(jax.random.uniform(ks[6], (DEPTH_2, SSD_HEADS), f32)
                  * (np.log(DT_MAX) - np.log(DT_MIN)) + np.log(DT_MIN))
    return {
        "x": nrm(ks[0], (BATCH, SEQ, D_MODEL), 1.0),
        "c": nrm(ks[1], (BATCH, D_MODEL), 1.0),
        "w_ada": nrm(ks[2], (DEPTH_2, D_MODEL, N_MOD * D_MODEL), D_MODEL ** -0.5),
        "b_ada": nrm(ks[3], (DEPTH_2, N_MOD * D_MODEL), 0.01),
        "norm_mix_w": 1.0 + nrm(ks[4], (DEPTH_2, D_MODEL), 0.05),
        "w_in": nrm(ks[5], (DEPTH_2, D_MODEL, IN_COLS), D_MODEL ** -0.5),
        "conv_w": nrm(ks[7], (DEPTH_2, CONV_WIDTH, XBC_WIDTH), CONV_WIDTH ** -0.5),
        "conv_b": nrm(ks[8], (DEPTH_2, XBC_WIDTH), 0.01),
        "dt_bias": dt0 + jnp.log(-jnp.expm1(-dt0)),
        "a_log": jnp.log(jax.random.uniform(ks[9], (DEPTH_2, SSD_HEADS), f32, 1.0, 16.0)),
        "d_skip": 1.0 + nrm(ks[10], (DEPTH_2, SSD_HEADS), 0.1),
        "ssd_norm_w": 1.0 + nrm(ks[11], (DEPTH_2, D_INNER), 0.05),
        "w_branch_ssd": nrm(ks[12], (DEPTH_2, D_INNER, D_MODEL), D_INNER ** -0.5),
        "pool_w": nrm(ks[13], (DEPTH_2, POOL_GROUPS, POOL_GROUP_WIDTH, POOL_GROUP_WIDTH), POOL_GROUP_WIDTH ** -0.5),
        "pool_scale": 1.0 + nrm(ks[14], (DEPTH_2, POOL_WIDTH), 0.1),
        "w_branch_pool": nrm(ks[15], (DEPTH_2, POOL_WIDTH, D_MODEL), POOL_WIDTH ** -0.5),
        "w_out": nrm(ks[16], (DEPTH_2, D_MODEL, D_MODEL), D_MODEL ** -0.5),
        "norm_mlp_w": 1.0 + nrm(ks[17], (DEPTH_2, D_MODEL), 0.05),
        "w_up": nrm(ks[18], (DEPTH_2, D_MODEL, D_FF_2), D_MODEL ** -0.5),
        "w_down": nrm(ks[19], (DEPTH_2, D_FF_2, D_MODEL), D_FF_2 ** -0.5),
        "norm_final_w": 1.0 + nrm(ks[20], (D_MODEL,), 0.05),
    }

def second_block(x, c, w_ada, b_ada, norm_mix_w, w_in, conv_w, conv_b, dt_bias, a_log, d_skip,
              ssd_norm_w, w_branch_ssd, pool_w, pool_scale, w_branch_pool, w_out,
              norm_mlp_w, w_up, w_down, norm_final_w):
    for i in range(DEPTH_2):
        mod = (jax.nn.silu(c) @ w_ada[i] + b_ada[i])[:, None, :]
        shift_m, scale_m, gate_m, shift_f, scale_f, gate_f = jnp.split(mod, N_MOD, axis=-1)
        h = rmsnorm(x, norm_mix_w[i]) * (1.0 + scale_m) + shift_m
        x = x + gate_m * hybrid_mixer(h, w_in[i], conv_w[i], conv_b[i], dt_bias[i], a_log[i],
                                      d_skip[i], ssd_norm_w[i], w_branch_ssd[i], pool_w[i],
                                      pool_scale[i], w_branch_pool[i], w_out[i])
        h = rmsnorm(x, norm_mlp_w[i]) * (1.0 + scale_f) + shift_f
        x = x + gate_f * (jnp.square(jax.nn.relu(h @ w_up[i])) @ w_down[i])
    return rmsnorm(x, norm_final_w)


def setup_inputs(seed=0):
    out = dict(first_inputs(seed))
    for name, value in second_inputs(seed + 1).items():
        if name != "x":
            out[name + "_2"] = value
    return out


def reference(
    x, norm_mix_g, norm_ffn_g, a_w_in, a_q_g, a_k_g, a_iq_g, a_ik_g, a_w_out, b_w_in, b_out_g,
    b_w_out, f_w_up, f_conv_w, f_conv_b, f_w_down, c_2, w_ada_2, b_ada_2, norm_mix_w_2, w_in_2,
    conv_w_2, conv_b_2, dt_bias_2, a_log_2, d_skip_2, ssd_norm_w_2, w_branch_ssd_2, pool_w_2,
    pool_scale_2, w_branch_pool_2, w_out_2, norm_mlp_w_2, w_up_2, w_down_2, norm_final_w_2,
):
    x = first_block(
        x, norm_mix_g, norm_ffn_g, a_w_in, a_q_g, a_k_g, a_iq_g, a_ik_g, a_w_out, b_w_in,
        b_out_g, b_w_out, f_w_up, f_conv_w, f_conv_b, f_w_down,
    )
    return second_block(
        x, c_2, w_ada_2, b_ada_2, norm_mix_w_2, w_in_2, conv_w_2, conv_b_2, dt_bias_2, a_log_2,
        d_skip_2, ssd_norm_w_2, w_branch_ssd_2, pool_w_2, pool_scale_2, w_branch_pool_2,
        w_out_2, norm_mlp_w_2, w_up_2, w_down_2, norm_final_w_2,
    )


_drawn_inputs = setup_inputs


def setup_inputs(seed=0):
    import zlib

    import numpy as np

    out = dict(_drawn_inputs(seed))
    spreads = {}
    factors = {'a_q_g': 8.0,
     'a_k_g': 7.49,
     'b_out_g': 5.631,
     'f_conv_b': 4.674,
     'b_ada_2': 3.62,
     'norm_mix_w_2': 2.911,
     'conv_b_2': 36.677,
     'd_skip_2': 156.948,
     'ssd_norm_w_2': 5.224,
     'norm_mlp_w_2': 3.694}
    for name, (base, spread) in spreads.items():
        noise = np.random.default_rng([zlib.crc32(name.encode()), seed]).standard_normal(out[name].shape)
        drawn = base * np.exp(spread * noise) if base else spread * noise
        out[name] = __import__('jax').numpy.asarray(drawn.astype(out[name].dtype))
    for name, factor in factors.items():
        out[name] = (out[name] * factor).astype(out[name].dtype)
    return out
```

```python
from contextlib import ExitStack

import numpy as np

import concourse.bass as bass
from concourse import mybir

F32 = mybir.dt.float32
F32R = mybir.dt.float32r
BF16 = mybir.dt.bfloat16
ALU = mybir.AluOpType
ACT = mybir.ActivationFunctionType
AX = mybir.AxisListType

P = 128
SEQ, DM = 256, 1024
NT = DM // P
NB = SEQ // P
FF_PAIRS = 2816 // P
MLP_TILES = 4 * DM // P
HEADS_A, LAT, IDX_DIM, TOPK = 8, 128, 64, 64
HEADS_B = 4
GROUPS, GROUP_HEADS, SSD_HEADS, SSD_P = 4, 8, 32, 64
EPS_A, EPS_B = 1e-6, 1e-5
MASKED, TAKEN = -3.0e38, -3.3e38
SEEN = 384

ARENA = 9180
RING = 6
SLAB = 8 * P
S_AIN = 0
S_AOUT = S_AIN + 14
S_FFN0 = S_AOUT + NT
S_B = S_FFN0 + 3 * FF_PAIRS
S_BOUT = S_B + 12 * HEADS_B
S_FFN1 = S_BOUT + 2 * NT
S_DT = S_FFN1 + 3 * FF_PAIRS
S_GRP = S_DT + 1
S_GATE = S_GRP + 12 * GROUPS
S_POOL = S_GATE + 2 * NT
S_MERGE = S_POOL + 2
S_WOUT = S_MERGE + 3 * NT
S_MLP = S_WOUT + NT
SLABS = S_MLP + 2 * MLP_TILES
ADA_TILES = 6 * NT

_widths = [
    ("mix_g0", NT), ("ffn_g0", NT), ("mix_g1", NT), ("ffn_g1", NT), ("q_g", 1), ("k_g", 1), ("iq_g", 1), ("ik_g", 1),
    ("ffn0", 8 * FF_PAIRS), ("ffn1", 8 * FF_PAIRS), ("out_g", 16), ("b_ada", 48), ("mix_w", NT),
    ("grp", 38 * GROUPS), ("dt_bias", 1), ("a_log", 1), ("pool_scale", NT), ("mlp_w", NT), ("final_w", NT),
]
COL, PARAMS = {}, 0
for _name, _w in _widths:
    COL[_name] = PARAMS
    PARAMS += _w
_widths = [("ident", P), ("ones", P), ("halves", 2), ("dup", P), ("cos", SEQ), ("sin", SEQ), ("decay", HEADS_B * SEEN),
           ("admit", SEEN), ("tri", SEEN), ("ramp", 4 * 16)]
CC, CONSTS = {}, 0
for _name, _w in _widths:
    CC[_name] = CONSTS
    CONSTS += _w


def val(base, it=None, step=0):
    return base if it is None else it * step + base


class Steps:

    def __init__(self, eng, sem):
        self.eng, self.sem, self.n, self.it, self.per = eng, sem, 0, None, 0

    def __call__(self, ins):
        ins.then_inc(self.sem, 1)
        self.n += 1
        self.eng.wait_ge(self.sem, val(self.n, self.it, self.per))

    def enter(self, it, per):
        self.it, self.per, self.start = it, per, self.n

    def leave(self, turns):
        assert self.n - self.start == self.per, (self.n - self.start, self.per)
        self.n, self.it, self.per = self.start + self.per * turns, None, 0


def build(nc, x, stream, ada, c_rows, params, consts, out):
    ctx = ExitStack()
    with ctx:
        def sb(name, shape, dt=F32):
            return ctx.enter_context(nc.sbuf_tensor(name, shape, dt))

        def sem(name):
            return ctx.enter_context(nc.semaphore(name))

        w_raw = sb("w_raw", [P, RING, SLAB])
        w_hi = sb("w_hi", [P, RING, SLAB], F32R)
        w_lo = sb("w_lo", [P, RING, SLAB], F32R)
        a_hi, a_lo = sb("a_hi", [P, NT, SEQ], F32R), sb("a_lo", [P, NT, SEQ], F32R)
        b_hi, b_lo = sb("b_hi", [P, 2 * NT, SEQ], F32R), sb("b_lo", [P, 2 * NT, SEQ], F32R)
        c_hi, c_lo = sb("c_hi", [P, NT, SEQ], F32R), sb("c_lo", [P, NT, SEQ], F32R)
        res = sb("res", [P, NT, SEQ])
        sq = sb("sq", [P, NT, SEQ])
        inv = sb("inv", [P, SEQ])
        inv_tok = sb("inv_tok", [P, NB])
        par, con = sb("par", [P, PARAMS]), sb("con", [P, CONSTS])
        tri = sb("tri", [P, SEEN], BF16)
        ident_b = sb("ident_b", [P, P], BF16)
        rs_var, rs_root, rs_y, rs_t = (sb(f"rs_{n}", [P, 24]) for n in ("var", "root", "y", "t"))
        diag = sb("diag", [P, 4, P])
        mod = sb("mod", [P, 48])
        eff_scale = sb("eff_scale", [P, 2, NT])
        arena = sb("arena", [P, ARENA])
        ps = ctx.enter_context(nc.psum_tensor("ps", [P, 8, 512], F32))

        top = [0]

        def area(*shape):
            n = int(np.prod(shape))
            piece = arena[:, top[0]:top[0] + n]
            top[0] += n
            assert top[0] <= ARENA, top[0]
            names = " ".join(f"d{i}" for i in range(len(shape)))
            if len(shape) == 1:
                return piece
            return piece.rearrange(f"p ({names}) -> p {names}", **{f"d{i}": s for i, s in enumerate(shape)})

        def const(name, n, rows=P, at=0):
            return con[0:rows, CC[name] + at:CC[name] + at + n]

        def pcol(name, at=0, rows=P, n=1):
            return par[0:rows, COL[name] + at:COL[name] + at + n]

        ident, ones = const("ident", P), const("ones", P)

        small_in, x_in = sem("small_in"), sem("x_in")
        w_landed = [sem(f"w_landed{i}") for i in range(RING)]
        w_hi_ready, w_lo_ready = sem("w_hi_ready"), sem("w_lo_ready")
        w_used = sem("w_used")
        turned = sem("turned")
        res_ready = sem("res_ready")
        a_hi_ready, a_ready = sem("a_hi_ready"), sem("a_ready")
        sq_ready, sum_ready = sem("sq_ready"), sem("sum_ready")
        var_ready, root_ready = sem("var_ready"), sem("root_ready")
        diag_ready, spread_ready, inv_ready = sem("diag_ready"), sem("spread_ready"), sem("inv_ready")
        vec_step, act_step = sem("vec_step"), sem("act_step")
        const_ready = sem("const_ready")
        RS = [0, 3, 4, 9, 10, 15, 16]
        RS_KEYS, RS_Q, RS_RET, RS_SSD = 1, 2, 5, 11

        def sum_bank(v):
            return 3 if v % 2 else 7


        def split_hi(act, s, it=None, ds=0):
            act.wait_ge(w_landed[s % RING], val(16 * (s // RING + 1), it, 16 * ds // RING))
            if s >= RING:
                act.wait_ge(w_used, val(s - RING + 1, it, ds))
            act.activation(w_hi[:, s % RING], w_raw[:, s % RING], ACT.Copy).then_inc(w_hi_ready, 1)

        def split_lo(dve, s, it=None, ds=0):
            dve.wait_ge(w_hi_ready, val(s + 1, it, ds))
            dve.tensor_tensor(w_lo[:, s % RING], w_raw[:, s % RING], w_hi[:, s % RING].bitcast(F32),
                              ALU.subtract).then_inc(w_lo_ready, 1)

        def slab_ready(pe, s, it=None, ds=0):
            pe.wait_ge(w_lo_ready, val(s + 1, it, ds))

        def mm3(pe, o, wh, wl, xh, xl, start, stop, shared=False):
            pe.matmul(o, wh, xh, start=start, stop=False, skip_group_check=shared)
            pe.matmul(o, wh, xl, start=False, stop=False, skip_group_check=shared)
            return pe.matmul(o, wl, xh, start=False, stop=stop, skip_group_check=shared)

        def slab_gemm(pe, s, o, hi, lo, it=None, ds=0, first=True, last=True, each=None):
            slab_ready(pe, s, it, ds)
            for k in range(NT):
                if each:
                    each(k)
                t = slice(k * P, (k + 1) * P)
                mm = mm3(pe, o, w_hi[:, s % RING, t], w_lo[:, s % RING, t], hi[:, k], lo[:, k],
                         first and k == 0, last and k == NT - 1)
            mm.then_inc(w_used, 1)

        def down_slab(pe, s, hi, lo, first, last, it=None, ds=0):
            slab_ready(pe, s, it, ds)
            for m in range(NT):
                t = slice(m * P, (m + 1) * P)
                o = ps[:, m // 2, (m % 2) * SEQ:(m % 2 + 1) * SEQ]
                mm = mm3(pe, o, w_hi[:, s % RING, t], w_lo[:, s % RING, t], hi, lo,
                         first and m % 2 == 0, last, shared=True)
            mm.then_inc(w_used, 1)

        def sum_squares(pe, v, k):
            pe.wait_ge(sq_ready, NT * v + k + 1)
            for b in range(NB):
                mm = pe.matmul(ps[:, sum_bank(v), b:b + 1], sq[:, k, b * P:(b + 1) * P], ones[:, 0:1],
                               start=(k == 0 and b == 0), stop=(k == NT - 1), skip_group_check=True)
            if k == NT - 1:
                mm.then_inc(sum_ready, 1)

        def operand_and_sums(pe, v):
            def each(k):
                pe.wait_ge(a_ready, NT * v + k + 1)
                sum_squares(pe, v, k)
            return each

        def spread_inv(pe, v):
            pe.wait_ge(diag_ready, v + 1)
            pe.matmul(ps[:, sum_bank(v), SEQ:2 * SEQ], ones, diag[:, 0:2].rearrange("p b t -> p (b t)"),
                      start=True, stop=True).then_inc(spread_ready, 1)

        def act_root(act, r, n, it=None):
            act.wait_ge(var_ready, val(r + 1, it, 1))
            act.activation(rs_root[:, 0:n], rs_var[:, 0:n], ACT.Sqrt).then_inc(root_ready, 1)

        def rsqrt(dve, step, r, n, o, it=None):
            dve.wait_ge(root_ready, val(r + 1, it, 1))
            step(dve.reciprocal(rs_y[:, 0:n], rs_root[:, 0:n]))
            step(dve.scalar_tensor_tensor(out=rs_t[:, 0:n], in0=rs_y[:, 0:n], scalar=-0.5, in1=rs_y[:, 0:n],
                                          op0=ALU.mult, op1=ALU.mult))
            step(dve.tensor_tensor(rs_t[:, 0:n], rs_t[:, 0:n], rs_var[:, 0:n], ALU.mult))
            step(dve.scalar_tensor_tensor(out=o, in0=rs_t[:, 0:n], scalar=1.5, in1=rs_y[:, 0:n],
                                          op0=ALU.add, op1=ALU.mult))

        def act_inv(act, v):
            act_root(act, RS[v], NB)
            act.wait_ge(spread_ready, v + 1)
            act.activation(inv[:, :], ps[:, sum_bank(v), SEQ:2 * SEQ], ACT.Copy).then_inc(inv_ready, 1)

        def vec_inv(dve, step, v, eps):
            dve.wait_ge(sum_ready, v + 1)
            dve.tensor_scalar(rs_var[:, 0:NB], ps[:, sum_bank(v), 0:NB], 1.0 / DM, eps, ALU.mult, ALU.add).then_inc(var_ready, 1)
            rsqrt(dve, step, RS[v], NB, inv_tok[:, :])
            step(dve.tensor_scalar(diag[:, 0], ident, inv_tok[:, 0:1], None, ALU.mult))
            dve.tensor_scalar(diag[:, 1], ident, inv_tok[:, 1:2], None, ALU.mult).then_inc(diag_ready, 1)

        def act_prep(act, v, m, g):
            act.wait_ge(res_ready, NT * v + m + 1)
            act.activation(a_hi[:, m], res[:, m], ACT.Copy, scale=pcol(g, m)).then_inc(a_hi_ready, 1)
            square(act, v, m)

        def square(act, v, m):
            act.wait_ge(res_ready, NT * v + m + 1)
            act.activation(sq[:, m], res[:, m], ACT.Square).then_inc(sq_ready, 1)

        def vec_prep(dve, v, m, g):
            dve.wait_ge(a_hi_ready, NT * v + m + 1)
            dve.scalar_tensor_tensor(out=a_lo[:, m], in0=res[:, m], scalar=pcol(g, m), in1=a_hi[:, m].bitcast(F32),
                                     op0=ALU.mult, op1=ALU.subtract).then_inc(a_ready, 1)

        def hi_ahead(act, s, it=None, ds=0):
            if s < SLABS:
                split_hi(act, s, it, ds)

        def lo_ahead(dve, s, it=None, ds=0):
            if s < SLABS:
                split_lo(dve, s, it, ds)

        def out_pe(pe, s0, two, hi, lo, taken, base, each=(None, None)):
            for m in range(NT):
                if m >= 4:
                    pe.wait_ge(taken, base + m - 3)
                o = ps[:, 4 + (m + 2) % 4, 0:SEQ]
                if two:
                    slab_gemm(pe, s0 + 2 * m, o, hi, lo, last=False, each=None if m else each[0])
                    slab_gemm(pe, s0 + 2 * m + 1, o, hi[:, NT:2 * NT], lo[:, NT:2 * NT], first=False, each=None if m else each[1])
                else:
                    slab_gemm(pe, s0 + m, o, hi, lo, each=None if m else each[0])

        def out_act(act, s0, per, v, g):
            for m in range(NT):
                for s in range(s0 + per * m, s0 + per * (m + 1)):
                    hi_ahead(act, s + 3)
                act_prep(act, v, m, g)

        def out_vec(dve, s0, per, v, g):
            for m in range(NT):
                for s in range(s0 + per * m, s0 + per * (m + 1)):
                    lo_ahead(dve, s + 3)
                dve.wait_ge(w_used, s0 + per * (m + 1))
                dve.tensor_tensor(res[:, m], res[:, m], ps[:, 4 + (m + 2) % 4, 0:SEQ], ALU.add).then_inc(res_ready, 1)
                if m:
                    vec_prep(dve, v, m - 1, g)
            vec_prep(dve, v, NT - 1, g)

        ADA_PARTS = 4
        top[0] = ARENA - 2 * DM - ADA_PARTS * ADA_TILES
        ada_raw, cond_row, ada_part = area(DM), area(DM), area(ADA_TILES, ADA_PARTS)
        cond_in, cond_ready, mod_ready = sem("cond_in"), sem("cond_ready"), sem("mod_ready")
        ada_landed, pool_step = sem("ada_landed"), sem("pool_step")

        def modulation_pool(pool, step):
            pool.wait_ge(cond_ready, 1)
            pool.dma_start(ada_raw, ada[0]).then_inc(ada_landed, 16)

            def dot(i, it=None):
                pool.wait_ge(ada_landed, val(16 * (i + 1), it, 16))
                step(pool.tensor_tensor(ada_raw, ada_raw, cond_row, ALU.mult))
                n = DM // 2
                while n > ADA_PARTS:
                    step(pool.tensor_tensor(ada_raw[:, 0:n], ada_raw[:, 0:n], ada_raw[:, n:2 * n], ALU.add))
                    n //= 2
                o = ada_part[:, i] if it is None else ada_part[:, bass.ds(it, 1)].rearrange("p a n -> p (a n)")
                step(pool.tensor_tensor(o, ada_raw[:, 0:n], ada_raw[:, n:2 * n], ALU.add))

            with pool.Fori(0, ADA_TILES - 1) as it:
                step.enter(it, 9)
                dot(0, it)
                pool.dma_start(ada_raw, ada[bass.ds(it + 1, 1)].rearrange("a p n -> (a p) n")).then_inc(ada_landed, 16)
            step.leave(ADA_TILES - 1)
            dot(ADA_TILES - 1)
            for n in (2, 1):
                step(pool.tensor_tensor(ada_part[:, :, 0:n], ada_part[:, :, 0:n], ada_part[:, :, n:2 * n], ALU.add))
            pool.tensor_tensor(mod[:, :], ada_part[:, :, 0], pcol("b_ada", n=ADA_TILES), ALU.add).then_inc(mod_ready, 1)

        top[0] = 0
        x_tok = area(NB, DM)
        top[0] = 0
        q_f = area(HEADS_A, SEQ)
        c_f, kw_f, qi_f = area(SEQ), area(SEQ), area(4, SEQ)
        k_n, ki_n, ki_dup, c_tok = area(SEQ), area(SEQ), area(SEQ), area(NB, LAT)
        key_gain = area(2)
        rel = area(2, 512)
        w_idx = area(NB, HEADS_A)
        score, work, pick = area(SEEN), area(SEEN), area(SEEN)
        best = area(8)
        logit, prob, prob_t = area(2, SEEN), area(2, SEEN), area(2, SEEN)
        peak, low, mass, share = area(2, 2), area(2, 2), area(2, 2), area(2, 2)
        q_scale = area(NB, HEADS_A)
        q_part = [slice(0, P), slice(P, SEEN)]
        a_out_f = sem("a_out_f")
        key_sq, key_sum = sem("key_sq"), sem("key_sum")
        q_sq, q_sum = sem("q_sq"), sem("q_sum")
        key_diag, key_spread, key_norm, dup_done, dup_ready = (sem(n) for n in ("key_diag", "key_spread", "key_norm", "dup_done", "dup_ready"))
        c_turned, c_tok_ready = sem("c_turned"), sem("c_tok_ready")
        idx_ready, rel_ready, rel_used = sem("idx_ready"), sem("rel_ready"), sem("rel_used")
        logit_ready, logit_used, low_ready = sem("logit_ready"), sem("logit_used"), sem("low_ready")
        exp_ready, prob_ready, prob_turned, prob_t_ready = sem("exp_ready"), sem("prob_ready"), sem("prob_turned"), sem("prob_t_ready")
        o_ready, o_hi_ready, o_lo_ready = sem("o_ready"), sem("o_hi_ready"), sem("o_lo_ready")

        IDX = [(1, [0, 2]), (1, [1, 3]), (1, [4, 6]), (1, [5, 7]), (0, [0, 2, 4, 6]), (0, [1, 3, 5, 7])]

        def attention_pe(pe):
            pe.wait_ge(small_in, 32)
            pe.wait_ge(x_in, 16)
            for m in range(NT):
                for b in range(NB):
                    mm = pe.transpose(ps[:, m // 2, (m % 2) * SEQ + b * P:(m % 2) * SEQ + (b + 1) * P],
                                      x_tok[:, b, m * P:(m + 1) * P], ident)
                if m % 2:
                    mm.then_inc(turned, 1)
            pe.wait_ge(res_ready, NT)
            slab_gemm(pe, 0, ps[:, 0, 0:SEQ], a_hi, a_lo, each=operand_and_sums(pe, 0))
            slab_gemm(pe, 1, ps[:, 1, 0:SEQ], a_hi, a_lo)
            spread_inv(pe, 0)
            for s in range(2, 6):
                if s >= 4:
                    pe.wait_ge(a_out_f, s - 3)
                slab_gemm(pe, s, ps[:, s % 4, 0:SEQ], a_hi, a_lo)
            def key_sums(n):
                pe.wait_ge(key_sq, n + 1)
                for b in range(NB):
                    t = slice(b * P, (b + 1) * P)
                    if n == 0:
                        mm = pe.matmul(ps[:, 6, b:b + 1], sq[:, 0, t], ones[:, 0:1], start=True, stop=True)
                    elif n == 1:
                        pe.matmul(ps[:, 6, 2 + b:3 + b], sq[0:IDX_DIM, 1, t], ones[0:IDX_DIM, 0:1], start=True, stop=True)
                        mm = pe.matmul(ps[:, 5, 8 * b:8 + 8 * b], kw_f[64:72, t], con[64:72, CC["ident"] + 64:CC["ident"] + 72],
                                       start=True, stop=True)
                    else:
                        h = 2 * (n - 2)
                        mm = pe.matmul(ps[:, 6, 4 + 8 * b + h:6 + 8 * b + h], sq[:, n, t], const("halves", 2), start=True, stop=True)
                return mm
            for n in range(6):
                mm = key_sums(n)
            mm.then_inc(key_sum, 1)
            pe.wait_ge(a_out_f, 1)
            for b in range(NB):
                mm = pe.transpose(ps[:, 7, b * P:(b + 1) * P], c_f[:, b * P:(b + 1) * P], ident)
            mm.then_inc(c_turned, 1)

            def q_slab(h):
                s = 6 + h
                pe.wait_ge(a_out_f, s - 3)
                slab_gemm(pe, s, ps[:, s % 4, 0:SEQ], a_hi, a_lo)

            def q_sums(h):
                pe.wait_ge(q_sq, h + 1)
                for b in range(NB):
                    mm = pe.matmul(ps[:, 6, 64 + 8 * b + h:65 + 8 * b + h], sq[:, h, b * P:(b + 1) * P], ones[:, 0:1],
                                   start=True, stop=True)
                if h == HEADS_A - 1:
                    mm.then_inc(q_sum, 1)

            def index_batch(n):
                b, heads = IDX[n]
                if n >= 2:
                    pe.wait_ge(rel_ready, n - 1)
                w = 512 // len(heads)
                for i, h in enumerate(heads):
                    r = slice(64 * (h % 2), 64 * (h % 2) + 64)
                    mm = pe.matmul(ps[:, 4 + n % 2, i * w:(i + 1) * w], qi_f[r, h // 2, b * P:(b + 1) * P],
                                   ki_dup[r, 0:w], start=True, stop=True)
                mm.then_inc(idx_ready, 1)

            q_slab(0)
            pe.wait_ge(key_diag, 1)
            pe.matmul(ps[:, 5, :], ones, diag[:, :, :].rearrange("p b t -> p (b t)"), start=True, stop=True).then_inc(key_spread, 1)
            q_slab(1)
            pe.wait_ge(key_norm, 1)
            pe.matmul(ps[:, 4, 0:SEQ], const("dup", P, IDX_DIM), ki_n[0:IDX_DIM, :], start=True, stop=True).then_inc(dup_done, 1)
            pe.wait_ge(dup_ready, 1)
            for n in range(6):
                index_batch(n)
                if n < 5:
                    q_slab(2 + n)
            q_slab(7)
            pe.wait_ge(w_used, 6)
            for h in range(HEADS_A):
                q_sums(h)
            def logits(h):
                if h >= 2:
                    pe.wait_ge(logit_used, 2 * h - 2)
                pe.matmul(ps[:, h % 2, 0:P], q_f[:, h, 0:P], k_n[:, 0:P], start=True, stop=True)
                pe.matmul(ps[:, h % 2, P:SEEN], q_f[:, h, P:SEQ], k_n[:, :], start=True, stop=True).then_inc(logit_ready, 1)

            def turn(h):
                pe.wait_ge(prob_ready, h + 1)
                if h >= 2:
                    pe.wait_ge(prob_t_ready, h - 1)
                for i, c in enumerate([0, 1, 2]):
                    mm = pe.transpose(ps[:, 2 + h % 2, i * P:(i + 1) * P], prob[:, h % 2, c * P:(c + 1) * P], ident)
                mm.then_inc(prob_turned, 1)

            def weigh(h):
                pe.wait_ge(prob_t_ready, h + 1)
                if h >= 2:
                    pe.wait_ge(o_lo_ready, h - 1)
                o = ps[:, 4 + h % 2, :]
                pe.matmul(o[:, 0:P], c_tok[:, 0], prob_t[:, h % 2, 0:P], start=True, stop=True)
                pe.matmul(o[:, P:SEQ], c_tok[:, 0], prob_t[:, h % 2, P:SEQ], start=True, stop=False)
                pe.matmul(o[:, P:SEQ], c_tok[:, 1], prob_t[:, h % 2, SEQ:SEEN], start=False, stop=True).then_inc(o_ready, 1)

            pe.wait_ge(a_out_f, 14)
            pe.wait_ge(c_tok_ready, 1)
            for h in range(HEADS_A + 2):
                if h < HEADS_A:
                    logits(h)
                if 0 <= h - 1 < HEADS_A:
                    turn(h - 1)
                if 0 <= h - 2 < HEADS_A:
                    weigh(h - 2)
            pe.wait_ge(o_lo_ready, HEADS_A)
            out_pe(pe, S_AOUT, False, b_hi, b_lo, res_ready, NT)

        def attention_act(act):
            for s in range(3):
                split_hi(act, s)
            act.wait_ge(small_in, 32)
            act.activation(tri[:, :], const("tri", SEEN), ACT.Copy).then_inc(const_ready, 1)
            act.activation(ident_b[:, :], ident, ACT.Copy).then_inc(const_ready, 1)
            for m in range(NT):
                act_prep(act, 0, m, "mix_g0")
            split_hi(act, 3)
            act_root(act, RS[0], NB)
            split_hi(act, 4)
            act.wait_ge(spread_ready, 1)
            act.activation(inv[:, :], ps[:, 7, SEQ:2 * SEQ], ACT.Copy).then_inc(inv_ready, 1)
            for n in range(6):
                split_hi(act, 5 + n)
                act.wait_ge(a_out_f, n + 1)
                if n == 1:
                    act.activation(sq[0:IDX_DIM, 1], kw_f[0:IDX_DIM, :], ACT.Square).then_inc(key_sq, 1)
                else:
                    act.activation(sq[:, n], c_f if n == 0 else qi_f[:, n - 2], ACT.Square).then_inc(key_sq, 1)
            act_root(act, RS_KEYS, 20)
            act.wait_ge(c_turned, 1)
            act.activation(c_tok[:, :, :].rearrange("p b d -> p (b d)"), ps[:, 7, 0:SEQ], ACT.Copy).then_inc(c_tok_ready, 1)

            def q_squares(h):
                act.wait_ge(a_out_f, 7 + h)
                if h == 0:
                    act.wait_ge(key_sum, 1)
                act.activation(sq[:, h], q_f[:, h], ACT.Square).then_inc(q_sq, 1)

            def relu(n):
                act.wait_ge(idx_ready, n + 1)
                if n >= 2:
                    act.wait_ge(rel_used, n - 1)
                act.activation(rel[:, n % 2], ps[:, 4 + n % 2, :], ACT.Relu).then_inc(rel_ready, 1)

            split_hi(act, 11)
            act.wait_ge(dup_done, 1)
            act.activation(ki_dup, ps[:, 4, 0:SEQ], ACT.Copy).then_inc(dup_ready, 1)
            for n in range(6):
                if n < 5:
                    split_hi(act, 12 + n)
                relu(n)
            for h in range(HEADS_A):
                q_squares(h)
            act_root(act, RS_Q, 2 * HEADS_A)

            def exps(h):
                act.wait_ge(low_ready, h + 1)
                if h >= 2:
                    act.wait_ge(prob_turned, h - 1)
                for b in range(NB):
                    act.activation(prob[:, h % 2, q_part[b]], logit[:, h % 2, q_part[b]], ACT.Exp, bias=low[:, h % 2, b:b + 1],
                                   scale=q_scale[:, b, h:h + 1], accum_out=mass[:, h % 2, b:b + 1]).then_inc(exp_ready, 1)

            def turned_copy(h):
                act.wait_ge(prob_turned, h + 1)
                if h >= 2:
                    act.wait_ge(o_ready, h - 1)
                act.activation(prob_t[:, h % 2], ps[:, 2 + h % 2, 0:SEEN], ACT.Copy).then_inc(prob_t_ready, 1)

            def out_hi(h):
                act.wait_ge(o_ready, h + 1)
                act.activation(b_hi[:, h], ps[:, 4 + h % 2, 0:SEQ], ACT.Copy).then_inc(o_hi_ready, 1)

            for h in range(HEADS_A + 2):
                if h < HEADS_A:
                    exps(h)
                if 0 <= h - 1 < HEADS_A:
                    turned_copy(h - 1)
                if 0 <= h - 2 < HEADS_A:
                    out_hi(h - 2)
            out_act(act, S_AOUT, 1, 1, "ffn_g0")
            act.wait_ge(cond_in, 16)
            act.activation(cond_row, cond_row, ACT.Silu).then_inc(cond_ready, 1)

        def attention_vec(dve, step):
            for s in range(3):
                split_lo(dve, s)
            dve.wait_ge(small_in, 32)
            step(dve.tensor_tensor(key_gain[:, 0:1], pcol("q_g"), pcol("k_g"), ALU.mult))
            step(dve.tensor_tensor(key_gain[:, 1:2], pcol("iq_g"), pcol("ik_g"), ALU.mult))
            for j in range(NT // 2):
                dve.wait_ge(turned, j + 1)
                dve.tensor_copy(res[:, 2 * j:2 * j + 2].rearrange("p m t -> p (m t)"), ps[:, j, :]).then_inc(res_ready, 2)
                if j:
                    vec_prep(dve, 0, 2 * j - 2, "mix_g0")
                    vec_prep(dve, 0, 2 * j - 1, "mix_g0")
            vec_prep(dve, 0, NT - 2, "mix_g0")
            vec_prep(dve, 0, NT - 1, "mix_g0")
            split_lo(dve, 3)
            vec_inv(dve, step, 0, EPS_A)
            split_lo(dve, 4)
            dve.wait_ge(inv_ready, 1)
            tiles = [c_f, kw_f, *(qi_f[:, i] for i in range(4)), *(q_f[:, h] for h in range(HEADS_A))]

            def evict(s):
                dve.wait_ge(w_used, s + 1)
                dve.tensor_tensor(tiles[s], ps[:, s % 4, 0:SEQ], inv[:, :], ALU.mult).then_inc(a_out_f, 1)

            for s in range(6):
                split_lo(dve, 5 + s)
                evict(s)
            dve.wait_ge(key_sum, 1)
            step(dve.tensor_scalar(rs_var[:, 0:2], ps[:, 6, 0:2], 1.0 / LAT, EPS_A, ALU.mult, ALU.add))
            dve.tensor_scalar(rs_var[:, 2:20], ps[:, 6, 2:20], 1.0 / IDX_DIM, EPS_A, ALU.mult, ALU.add).then_inc(var_ready, 1)
            rsqrt(dve, step, RS_KEYS, 20, rs_root[:, 0:20])
            step(dve.scalar_tensor_tensor(
                out=w_idx[:, :, :].rearrange("p b h -> p (b h)"), in0=rs_root[:, 4:20], scalar=float((HEADS_A * IDX_DIM) ** -0.5),
                in1=ps[:, 5, 0:16], op0=ALU.mult, op1=ALU.mult))
            for i in range(3):
                step(dve.tensor_scalar(diag[:, i], ident, rs_root[:, i:i + 1], None, ALU.mult))
            dve.tensor_scalar(diag[:, 3], ident, rs_root[:, 3:4], None, ALU.mult).then_inc(key_diag, 1)
            dve.wait_ge(key_spread, 1)
            step(dve.scalar_tensor_tensor(out=k_n, in0=c_f, scalar=key_gain[:, 0:1], in1=ps[:, 5, 0:SEQ], op0=ALU.mult, op1=ALU.mult))
            dve.scalar_tensor_tensor(out=ki_n[0:IDX_DIM, :], in0=kw_f[0:IDX_DIM, :], scalar=key_gain[0:IDX_DIM, 1:2],
                                     in1=ps[0:IDX_DIM, 5, SEQ:512], op0=ALU.mult, op1=ALU.mult).then_inc(key_norm, 1)
            split_lo(dve, 11)
            evict(6)
            evict(7)
            for n, (b, heads) in enumerate(IDX):
                if n < 5:
                    split_lo(dve, 12 + n)
                if n < 4:
                    evict(8 + n)
                dve.wait_ge(rel_ready, n + 1)
                w = 512 // len(heads)
                for i, h in enumerate(heads):
                    ins = dve.scalar_tensor_tensor(
                        out=score[:, q_part[b]], in0=rel[:, n % 2, i * w:(i + 1) * w], scalar=w_idx[:, b, h:h + 1],
                        in1=const("admit", SEEN)[:, q_part[b]] if h == 0 else score[:, q_part[b]], op0=ALU.mult, op1=ALU.add)
                    if i < len(heads) - 1:
                        step(ins)
                    else:
                        ins.then_inc(rel_used, 1)
                        dve.wait_ge(rel_used, n + 1)
            evict(12)
            evict(13)
            for b in range(NB):
                for r in range(TOPK // 8):
                    src = (score if r == 0 else work)[:, q_part[b]]
                    step(dve.max(best, src))
                    step(dve.match_replace(work[:, q_part[b]], best, src, TAKEN))
            step(dve.tensor_scalar(pick, work, (MASKED + TAKEN) / 2, -1e30, ALU.is_gt, ALU.mult))
            dve.wait_ge(q_sum, 1)
            dve.tensor_scalar(rs_var[:, 0:16], ps[:, 6, 64:80], 1.0 / LAT, EPS_A, ALU.mult, ALU.add).then_inc(var_ready, 1)
            rsqrt(dve, step, RS_Q, 16, rs_root[:, 0:16])
            step(dve.tensor_scalar(q_scale[:, :, :].rearrange("p b h -> p (b h)"), rs_root[:, 0:16], float(LAT ** -0.5), None, ALU.mult))

            def maxima(h):
                dve.wait_ge(logit_ready, h + 1)
                for b in range(NB):
                    if h >= 2:
                        dve.wait_ge(exp_ready, 2 * h - 2)
                    dve.tensor_tensor_reduce(logit[:, h % 2, q_part[b]], ps[:, h % 2, q_part[b]], pick[:, q_part[b]], 1.0, -3.4e38,
                                             ALU.add, ALU.max, peak[:, h % 2, b:b + 1]).then_inc(logit_used, 1)
                dve.wait_ge(logit_used, 2 * h + 2)
                dve.scalar_tensor_tensor(out=low[:, h % 2], in0=peak[:, h % 2], scalar=-1.0, in1=q_scale[:, :, h],
                                         op0=ALU.mult, op1=ALU.mult).then_inc(low_ready, 1)

            def shares(h):
                dve.wait_ge(exp_ready, 2 * h + 2)
                step(dve.reciprocal(share[:, h % 2], mass[:, h % 2]))
                step(dve.tensor_scalar(prob[:, h % 2, q_part[0]], prob[:, h % 2, q_part[0]], share[:, h % 2, 0:1], None, ALU.mult))
                dve.tensor_scalar(prob[:, h % 2, q_part[1]], prob[:, h % 2, q_part[1]], share[:, h % 2, 1:2], None, ALU.mult).then_inc(prob_ready, 1)

            def out_lo(h):
                dve.wait_ge(o_hi_ready, h + 1)
                dve.tensor_tensor(b_lo[:, h], ps[:, 4 + h % 2, 0:SEQ], b_hi[:, h].bitcast(F32), ALU.subtract).then_inc(o_lo_ready, 1)

            for h in range(HEADS_A + 2):
                if h < HEADS_A:
                    maxima(h)
                    shares(h)
                if 0 <= h - 2 < HEADS_A:
                    out_lo(h - 2)
            out_vec(dve, S_AOUT, 1, 1, "ffn_g0")

        top[0] = 0
        up, conv = area(2, 2, SEQ), area(2, 2, SEQ)
        gate, glu = area(2, SEQ), area(2, SEQ)
        ffn_sems = [{n: sem(f"ffn{i}_{n}") for n in ("up_out", "tap", "conv", "gate", "glu", "hi", "operand")} for i in range(2)]

        def ffn_pe(pe, L, s0, v):
            f = ffn_sems[L]

            def up_pair(p, s, it=None, ds=0, each=None):
                for half in range(2):
                    if p >= 2:
                        pe.wait_ge(f["up_out"], val(2 * (p - 2) + half + 1, it, 4))
                    slab_gemm(pe, s + half, ps[:, 6 - 2 * (p % 2) + half, 0:SEQ], a_hi, a_lo, it, ds, each=each if half == 0 else None)

            def down(p, s, it=None, ds=0):
                pe.wait_ge(f["operand"], val(p + 1, it, 2))
                down_slab(pe, s, b_hi[:, p % 2], b_lo[:, p % 2], p == 0, p == FF_PAIRS - 1, it, ds)

            up_pair(0, s0, each=operand_and_sums(pe, v))
            spread_inv(pe, v)
            up_pair(1, s0 + 2)
            pe.wait_ge(inv_ready, v + 1)
            down(0, s0 + 4)
            with pe.Fori(0, (FF_PAIRS - 2) // 2) as it:
                for u in range(2):
                    up_pair(2 + u, s0 + 5 + 3 * u, it, 6)
                    down(1 + u, s0 + 7 + 3 * u, it, 6)
            down(FF_PAIRS - 1, s0 + 3 * FF_PAIRS - 1)

        def ffn_act(act, L, s0, v, next_gain):
            f = ffn_sems[L]

            def prm(p, j, it):
                c = COL[f"ffn{L}"] + 8 * p + j
                return par[:, c:c + 1] if it is None else par[:, bass.ds(it * 16 + c, 1)]

            def tap(p, half, it=None):
                act.wait_ge(f["up_out"], val(2 * p + half + 1, it, 4))
                if p >= 2:
                    act.wait_ge(f["glu"], val(p - 1, it, 2))
                act.activation(conv[:, p % 2, half], up[:, p % 2, half], ACT.Identity, bias=prm(p, 6 + half, it),
                               scale=prm(p, 3 * half + 2, it)).then_inc(f["tap"], 1)

            def silu(p, it=None):
                act.wait_ge(f["conv"], val(2 * p + 1, it, 4))
                act.activation(gate[:, p % 2], conv[:, p % 2, 0], ACT.Silu).then_inc(f["gate"], 1)

            def hi(p, done, it=None):
                act.wait_ge(f["glu"], val(p + 1, it, 2))
                if p >= 2:
                    act.wait_ge(w_used, val(done, it, 6))
                act.activation(b_hi[:, p % 2], glu[:, p % 2], ACT.Copy).then_inc(f["hi"], 1)

            def pair(p, s, it=None):
                ds = 0 if it is None else 6
                hi_ahead(act, s + 3, it, ds)
                if p == 0:
                    act_inv(act, v)
                hi_ahead(act, s + 4, it, ds)
                tap(p, 0, it)
                if p:
                    hi_ahead(act, s + 5, it, ds)
                tap(p, 1, it)
                silu(p, it)
                hi(p, s - 6 + 3, it)

            pair(0, s0)
            pair(1, s0 + 2)
            with act.Fori(0, (FF_PAIRS - 4) // 2) as it:
                for u in range(2):
                    pair(2 + u, s0 + 5 + 3 * u, it)
            for p in range(FF_PAIRS - 2, FF_PAIRS):
                pair(p, s0 + 3 * p - 1)
            hi_ahead(act, s0 + 3 * FF_PAIRS - 1 + 3)
            for m in range(NT):
                if next_gain:
                    act_prep(act, v + 1, m, next_gain)
                else:
                    square(act, v + 1, m)

        def ffn_vec(dve, step, L, s0, v, next_gain):
            f = ffn_sems[L]

            def prm(p, j, it):
                c = COL[f"ffn{L}"] + 8 * p + j
                return par[:, c:c + 1] if it is None else par[:, bass.ds(it * 16 + c, 1)]

            def evict(p, half, s, it, ds):
                dve.wait_ge(w_used, val(s + half + 1, it, ds))
                dve.tensor_tensor(up[:, p % 2, half], ps[:, 6 - 2 * (p % 2) + half, 0:SEQ], inv[:, :], ALU.mult).then_inc(f["up_out"], 1)

            def taps(p, half, it):
                dve.wait_ge(f["tap"], val(2 * p + half + 1, it, 4))
                t = conv[:, p % 2, half]
                u = up[:, p % 2, half]
                step(dve.scalar_tensor_tensor(out=t[:, 1:SEQ], in0=u[:, 0:SEQ - 1], scalar=prm(p, 3 * half + 1, it),
                                              in1=t[:, 1:SEQ], op0=ALU.mult, op1=ALU.add))
                dve.scalar_tensor_tensor(out=t[:, 2:SEQ], in0=u[:, 0:SEQ - 2], scalar=prm(p, 3 * half, it),
                                         in1=t[:, 2:SEQ], op0=ALU.mult, op1=ALU.add).then_inc(f["conv"], 1)

            def pair(p, s, it=None):
                ds = 0 if it is None else 6
                lo_ahead(dve, s + 3, it, ds)
                if p == 0:
                    vec_inv(dve, step, v, EPS_A)
                    dve.wait_ge(inv_ready, v + 1)
                evict(p, 0, s, it, ds)
                lo_ahead(dve, s + 4, it, ds)
                taps(p, 0, it)
                evict(p, 1, s, it, ds)
                taps(p, 1, it)
                dve.wait_ge(f["conv"], val(2 * p + 2, it, 4))
                dve.wait_ge(f["gate"], val(p + 1, it, 2))
                dve.tensor_tensor(glu[:, p % 2], gate[:, p % 2], conv[:, p % 2, 1], ALU.mult).then_inc(f["glu"], 1)
                if p:
                    lo_ahead(dve, s + 5, it, ds)
                dve.wait_ge(f["hi"], val(p + 1, it, 2))
                dve.tensor_tensor(b_lo[:, p % 2], glu[:, p % 2], b_hi[:, p % 2].bitcast(F32), ALU.subtract).then_inc(f["operand"], 1)

            pair(0, s0)
            pair(1, s0 + 2)
            with dve.Fori(0, (FF_PAIRS - 4) // 2) as it:
                step.enter(it, 4)
                for u in range(2):
                    pair(2 + u, s0 + 5 + 3 * u, it)
            step.leave((FF_PAIRS - 4) // 2)
            for p in range(FF_PAIRS - 2, FF_PAIRS):
                pair(p, s0 + 3 * p - 1)
            lo_ahead(dve, s0 + 3 * FF_PAIRS - 1 + 3)
            add_down(dve, s0 + 3 * FF_PAIRS, v + 1, next_gain)

        def add_down(dve, used, v, g):
            dve.wait_ge(w_used, used)
            for j in range(NT // 2):
                dve.tensor_tensor(res[:, 2 * j:2 * j + 2].rearrange("p m t -> p (m t)"), res[:, 2 * j:2 * j + 2].rearrange("p m t -> p (m t)"),
                                  ps[:, j, :], ALU.add).then_inc(res_ready, 2)
                if g and j:
                    vec_prep(dve, v, 2 * j - 2, g)
                    vec_prep(dve, v, 2 * j - 1, g)
            if g:
                vec_prep(dve, v, NT - 2, g)
                vec_prep(dve, v, NT - 1, g)

        HEAD = 12
        top[0] = 0
        cos_i, sin_i = area(SEQ), area(SEQ)
        q_rot, k_rot = area(2, SEQ), area(2, SEQ)
        v_tok = area(NB, 512)
        g_b = area(4, SEQ)
        decayed = area(SEEN)
        turn_t = area(4, SEQ)
        inv_r = area(SEQ)
        y_n, y_b = area(2, SEQ), area(4, SEQ)
        g_taken, ret_taken = sem("g_taken"), sem("ret_taken")
        rot_ready, qk_ready, decayed_ready, v_ready = (sem(n) for n in ("rot_ready", "qk_ready", "decayed_ready", "v_ready"))
        ret_ready, ret_sq, ret_sum, ret_diag, ret_spread, ret_inv = (sem(n) for n in ("ret_ready", "ret_sq", "ret_sum", "ret_diag", "ret_spread", "ret_inv"))
        g_silu, y_ready, y_hi, y_operand = sem("g_silu"), sem("y_ready"), sem("y_hi"), sem("y_operand")

        def retention_pe(pe):
            def v_slab(s, i, it):
                slab_ready(pe, s, it, HEAD)
                for kk in range(2):
                    k = 2 * i + kk
                    w = slice(kk * 512, (kk + 1) * 512)
                    for b in range(NB):
                        t = slice(b * P, (b + 1) * P)
                        mm = mm3(pe, ps[:, 4 + b, :], a_hi[:, k, t], a_lo[:, k, t], w_hi[:, s % RING, w], w_lo[:, s % RING, w],
                                 k == 0, k == NT - 1)
                mm.then_inc(w_used, 1)

            def scores(it):
                pe.wait_ge(rot_ready, val(2, it, 2))
                for b in range(NB):
                    for d in range(2):
                        mm = pe.matmul(ps[:, 7, b * SEQ:b * SEQ + SEQ - b * P], k_rot[:, d, b * P:(b + 1) * P], q_rot[:, d, b * P:SEQ],
                                       start=(d == 0), stop=(d == 1))
                mm.then_inc(qk_ready, 1)

            def weigh(it):
                pe.wait_ge(decayed_ready, val(1, it, 1))
                pe.wait_ge(v_ready, val(2, it, 2))
                for e in range(4):
                    o = ps[:, 4 + e // 2, (e % 2) * SEQ:(e % 2 + 1) * SEQ]
                    c = slice(e * P, (e + 1) * P)
                    pe.matmul(o[:, 0:P], v_tok[:, 0, c], decayed[:, 0:P], start=True, stop=True)
                    pe.matmul(o[:, P:SEQ], v_tok[:, 0, c], decayed[:, P:SEQ], start=True, stop=False)
                    pe.matmul(o[:, P:SEQ], v_tok[:, 1, c], decayed[:, SEQ:SEEN], start=False, stop=True).then_inc(ret_ready, 1)

            def sums(it):
                pe.wait_ge(ret_sq, val(2, it, 2))
                for b in range(NB):
                    for e in range(4):
                        mm = pe.matmul(ps[:, 7, 400 + b:401 + b], sq[:, e, b * P:(b + 1) * P], ones[:, 0:1], start=(e == 0), stop=(e == 3))
                mm.then_inc(ret_sum, 1)

            def head(it, s=S_B):
                for j in range(12):
                    own = s + j
                    if j == 0:
                        pe.wait_ge(g_taken, val(1, it, 4))
                    if j == 4:
                        pe.wait_ge(ret_taken, val(1, it, 4))
                    if 4 <= j < 8:
                        v_slab(own, j - 4, it)
                    else:
                        slab_gemm(pe, own, ps[:, j % 4, 0:SEQ], a_hi, a_lo, it, HEAD)
                    if j == 6:
                        scores(it)
                    if j == 8:
                        weigh(it)
                    if j == 9:
                        sums(it)
                pe.wait_ge(ret_diag, val(1, it, 1))
                pe.matmul(ps[:, 7, 0:SEQ], ones, diag[:, 2:4].rearrange("p b t -> p (b t)"), start=True, stop=True).then_inc(ret_spread, 1)

            for k in range(NT):
                sum_squares(pe, 2, k)
            spread_inv(pe, 2)
            pe.wait_ge(a_ready, NT * 3)
            with pe.Fori(0, HEADS_B) as it:
                head(it)

            def tile_of(n):
                def each(k):
                    pe.wait_ge(y_operand, n + k + 1)
                return each
            out_pe(pe, S_BOUT, True, b_hi, b_lo, res_ready, 3 * NT, (tile_of(0), tile_of(NT)))

        def retention_act(act):
            act_inv(act, 2)
            with act.Fori(0, HEADS_B) as it:
                def silu(n):
                    act.wait_ge(g_taken, val(2 + n, it, 4))
                    act.activation(g_b[:, n], g_b[:, n], ACT.Silu).then_inc(g_silu, 1)

                for j in range(12):
                    s = S_B + j
                    split_hi(act, s + 3, it, HEAD)
                    if j == 7:
                        act.wait_ge(w_used, val(s + 1, it, HEAD))
                        for b in range(NB):
                            act.activation(v_tok[:, b], ps[:, 4 + b, :], ACT.Copy, scale=inv_tok[:, b:b + 1]).then_inc(v_ready, 1)
                    if j == 9:
                        for i in range(2):
                            act.wait_ge(ret_ready, val(2 * i + 2, it, 4))
                            act.activation(sq[:, 2 * i:2 * i + 2].rearrange("p m t -> p (m t)"), ps[:, 4 + i, :], ACT.Square).then_inc(ret_sq, 1)
                    if j == 10:
                        act_root(act, RS_RET, NB, it)
                for n in range(4):
                    silu(n)
                act.wait_ge(ret_spread, val(1, it, 1))
                act.activation(inv_r, ps[:, 7, 0:SEQ], ACT.Copy).then_inc(ret_inv, 1)
                for e in range(4):
                    act.wait_ge(y_ready, val(e + 1, it, 4))
                    act.activation(b_hi[:, bass.ds(it * 4 + e, 1)].rearrange("p a t -> p (a t)"), y_b[:, e], ACT.Copy).then_inc(y_hi, 1)
            out_act(act, S_BOUT, 2, 3, "ffn_g1")

        def retention_vec(dve, step):
            vec_inv(dve, step, 2, EPS_A)
            dve.wait_ge(inv_ready, 3)
            dve.tensor_tensor(cos_i, const("cos", SEQ), inv[:, :], ALU.mult).then_inc(g_taken, 1)
            dve.tensor_tensor(sin_i, const("sin", SEQ), inv[:, :], ALU.mult).then_inc(ret_taken, 1)
            dve.wait_ge(ret_taken, 1)
            with dve.Fori(0, HEADS_B) as it:
                step.enter(it, 9)

                def rotary(o, bank, used):
                    dve.wait_ge(w_used, val(used, it, HEAD))
                    for n, (x_h, table) in enumerate([(0, cos_i), (1, sin_i), (0, sin_i), (1, cos_i)]):
                        ins = dve.tensor_tensor(turn_t[:, n], ps[:, bank + x_h, 0:SEQ], table, ALU.mult)
                    step(ins)
                    step(dve.tensor_tensor(o[:, 0], turn_t[:, 0], turn_t[:, 1], ALU.subtract))
                    dve.tensor_tensor(o[:, 1], turn_t[:, 2], turn_t[:, 3], ALU.add).then_inc(rot_ready, 1)

                for j in range(12):
                    s = S_B + j
                    split_lo(dve, s + 3, it, HEAD)
                    if j == 1:
                        rotary(q_rot, 0, s + 1)
                    if j == 3:
                        dve.wait_ge(rot_ready, val(1, it, 2))
                        rotary(k_rot, 2, s + 1)
                    if j == 7:
                        dve.wait_ge(qk_ready, val(1, it, 1))
                        dve.tensor_tensor(decayed, ps[:, 7, 0:SEEN], con[:, bass.ds(it * SEEN + CC["decay"], SEEN)],
                                          ALU.mult).then_inc(decayed_ready, 1)
                    if j == 10:
                        dve.wait_ge(ret_sum, val(1, it, 1))
                        dve.tensor_scalar(rs_var[:, 0:NB], ps[:, 7, 400:402], 1.0 / 512, EPS_A, ALU.mult, ALU.add).then_inc(var_ready, 1)
                        rsqrt(dve, step, RS_RET, NB, rs_root[:, 0:NB], it)
                        step(dve.tensor_scalar(diag[:, 2], ident, rs_root[:, 0:1], None, ALU.mult))
                        dve.tensor_scalar(diag[:, 3], ident, rs_root[:, 1:2], None, ALU.mult).then_inc(ret_diag, 1)
                    if j >= 8:
                        dve.wait_ge(w_used, val(s + 1, it, HEAD))
                        dve.tensor_tensor(g_b[:, j - 8], ps[:, j - 8, 0:SEQ], inv[:, :], ALU.mult).then_inc(g_taken, 1)
                dve.wait_ge(ret_inv, val(1, it, 1))

                def y_lo(e):
                    dve.wait_ge(y_hi, val(e + 1, it, 4))
                    o = bass.ds(it * 4 + e, 1)
                    dve.tensor_tensor(b_lo[:, o].rearrange("p a t -> p (a t)"), y_b[:, e],
                                      b_hi[:, o].bitcast(F32).rearrange("p a t -> p (a t)"), ALU.subtract).then_inc(y_operand, 1)

                for e in range(4):
                    dve.scalar_tensor_tensor(out=y_n[:, e % 2], in0=ps[:, 4 + e // 2, (e % 2) * SEQ:(e % 2 + 1) * SEQ],
                                             scalar=par[:, bass.ds(it * 4 + COL["out_g"] + e, 1)], in1=inv_r,
                                             op0=ALU.mult, op1=ALU.mult).then_inc(ret_taken, 1)
                    dve.wait_ge(ret_taken, val(2 + e, it, 4))
                    dve.wait_ge(g_silu, val(e + 1, it, 4))
                    dve.tensor_tensor(y_b[:, e], y_n[:, e % 2], g_b[:, e], ALU.mult).then_inc(y_ready, 1)
                    if e:
                        y_lo(e - 1)
                y_lo(3)
            step.leave(HEADS_B)
            out_vec(dve, S_BOUT, 2, 3, "ffn_g1")

        top[0] = ARENA - 4 * SEQ
        scaled, normed = area(2, SEQ), area(2, SEQ)
        scaled_ready = sem("scaled_ready")
        MOD = {4: ("mix_w", 0), 5: ("mlp_w", 3 * NT)}

        def mod_act(act, v):
            act.wait_ge(mod_ready, 1)
            for m in range(NT):
                n = NT * (v - 4) + m
                act.wait_ge(scaled_ready, n + 1)
                act.activation(a_hi[:, m], scaled[:, m % 2], ACT.Identity, bias=mod[:, MOD[v][1] + m:MOD[v][1] + m + 1],
                               scale=eff_scale[:, v - 4, m:m + 1]).then_inc(a_hi_ready, 1)

        def mod_vec(dve, step, v):
            gain, col = MOD[v]
            dve.wait_ge(mod_ready, 1)
            step(dve.scalar_tensor_tensor(out=eff_scale[:, v - 4], in0=mod[:, col + NT:col + 2 * NT], scalar=1.0, in1=pcol(gain, n=NT),
                                          op0=ALU.add, op1=ALU.mult))
            vec_inv(dve, step, v, EPS_B)
            dve.wait_ge(inv_ready, v + 1)

            def low(m):
                dve.wait_ge(a_hi_ready, NT * v + m + 1)
                dve.tensor_tensor(a_lo[:, m], normed[:, m % 2], a_hi[:, m].bitcast(F32), ALU.subtract).then_inc(a_ready, 1)

            for m in range(NT):
                if m >= 2:
                    dve.wait_ge(a_ready, NT * v + m - 1)
                dve.tensor_tensor(scaled[:, m % 2], res[:, m], inv[:, :], ALU.mult).then_inc(scaled_ready, 1)
                dve.wait_ge(scaled_ready, NT * (v - 4) + m + 1)
                step(dve.tensor_scalar(normed[:, m % 2], scaled[:, m % 2], eff_scale[:, v - 4, m:m + 1], mod[:, col + m:col + m + 1],
                                       ALU.mult, ALU.add))
                if m:
                    low(m - 1)
            low(NT - 1)

        def ready(s, base):
            def wait_on(pe):
                def each(k):
                    pe.wait_ge(s, base + k + 1)
                return each
            return wait_on

        GRP = 12
        top[0] = 0
        u_f = area(NT, SEQ)
        cv = area(6, SEQ)
        z_s = area(4, SEQ)
        inv_s = area(SEQ)
        tail = top[0]
        x_tok2 = area(NB, 512)
        pick_h = area(GROUP_HEADS, P)
        seen = area(2, SEEN)
        cb = area(SEEN)
        cum = area(SEEN)
        dt_f = area(SEQ)
        dt_tok, neg_cum = area(NB, GROUP_HEADS), area(NB, GROUP_HEADS)
        root_s = area(NB)
        neg_a = area(1)
        end = top[0]
        top[0] = tail + 2 * 512
        dt_x, dt_e, dt_z = area(SEQ), area(SEQ), area(SEQ)
        assert top[0] <= tail + 1024 + GROUP_HEADS * P
        top[0] = tail
        gates = area(2 * NT, SEQ)
        top[0] = 0
        merged = area(2, SEQ)
        part = area(2, 2, SEQ)
        win = [cv[:, 0:2], cv[:, 2:4]]

        dt_x_ready, dt_e_ready, decay_a, dt_ready = sem("dt_x_ready"), sem("dt_e_ready"), sem("decay_a"), sem("dt_ready")
        tap_done, conv_done, act_done, z_done, u_done = (sem(n) for n in ("tap_done", "conv_done", "act_done", "z_done", "u_done"))
        cb_ready, cb_copied, own_ready, own_copied = sem("cb_ready"), sem("cb_copied"), sem("own_ready"), sem("own_copied")
        pick_ready, x_turned, x_tok_ready = sem("pick_ready"), sem("x_turned"), sem("x_tok_ready")
        cum_ready, exp_done, seen_ready, y_done = sem("cum_ready"), sem("exp_done"), sem("seen_ready"), sem("y_done")
        yz_ready, ysq_ready, ysum_ready, ydiag_ready, yspread_ready, inv_s_ready = (
            sem(n) for n in ("yz_ready", "ysq_ready", "ysum_ready", "ydiag_ready", "yspread_ready", "inv_s_ready"))
        yn_ready, yhi_ready, yssd_ready = sem("yn_ready"), sem("yhi_ready"), sem("yssd_ready")
        gate_ready, pooled_ready, pooled_hi, pooled_operand = (sem(n) for n in ("gate_ready", "pooled_ready", "pooled_hi", "pooled_operand"))
        pw_ready, pw_hi, pw_operand = sem("pw_ready"), sem("pw_hi"), sem("pw_operand")
        parts_ready, merged_ready, merged_hi, merged_operand = (sem(n) for n in ("parts_ready", "merged_ready", "merged_hi", "merged_operand"))

        def ssd_pe(pe):
            for k in range(NT):
                sum_squares(pe, 4, k)
            spread_inv(pe, 4)
            slab_gemm(pe, S_DT, ps[:, 4, 0:SEQ], a_hi, a_lo, each=ready(a_ready, 4 * NT)(pe))
            pe.sem_inc(z_done, 1)
            pe.sem_inc(u_done, 1)
            with pe.Fori(0, GROUPS) as it:
                def slab(j):
                    if j < 2:
                        pe.wait_ge(z_done, val(1, it, 4))
                    elif j < 4:
                        pe.wait_ge(u_done, val(1, it, 2))
                    elif j < 10:
                        pe.wait_ge(conv_done, val(j - 3, it, 6))
                    else:
                        pe.wait_ge(z_done, val(j - 8, it, 4))
                    slab_gemm(pe, S_GRP + j, ps[:, j % 4, 0:SEQ], a_hi, a_lo, it, GRP)

                for j in range(4):
                    slab(j)
                pe.wait_ge(dt_x_ready, 1)
                pe.wait_ge(act_done, val(2, it, 6))
                for b in range(NB):
                    mm = pe.matmul(ps[:, 4, b * SEQ:b * SEQ + SEQ - b * P], cv[:, 0, b * P:(b + 1) * P], cv[:, 1, b * P:SEQ],
                                   start=True, stop=True)
                mm.then_inc(cb_ready, 1)
                for j in range(4, 6):
                    slab(j)
                pe.wait_ge(cb_copied, val(1, it, 1))
                pe.wait_ge(dt_ready, 2)
                sel = con[0:SSD_HEADS, bass.ds(it * GROUP_HEADS + CC["ident"], GROUP_HEADS)]
                for n, src in enumerate([dt_f, cum]):
                    for b in range(NB):
                        c = 400 + GROUP_HEADS * (2 * n + b)
                        mm = pe.matmul(ps[:, 4, c:c + GROUP_HEADS], src[0:SSD_HEADS, b * P:(b + 1) * P], sel, start=True, stop=True)
                mm.then_inc(own_ready, 1)
                for j in range(6, 8):
                    slab(j)
                pe.wait_ge(act_done, val(6, it, 6))
                for b in range(NB):
                    for t in range(4):
                        mm = pe.transpose(ps[:, 5 + b, t * P:(t + 1) * P], cv[:, 2 + t, b * P:(b + 1) * P], ident)
                    mm.then_inc(x_turned, 1)
                for j in range(8, 10):
                    slab(j)

                def spread_cum(j):
                    if j == 0:
                        pe.wait_ge(pick_ready, val(1, it, 1))
                    if j < 2:
                        pe.wait_ge(x_tok_ready, val(j + 1, it, 2))
                    else:
                        pe.wait_ge(exp_done, val(2 * j - 2, it, 16))
                    o = ps[:, 5 + j % 2, :]
                    pe.matmul(o[:, P:SEQ], pick_h[0:SSD_HEADS, j], cum[0:SSD_HEADS, P:SEQ], start=True, stop=True)
                    for i, c in enumerate([0, SEQ]):
                        pe.matmul(o[:, c:c + P], pick_h[0:SSD_HEADS, j], cum[0:SSD_HEADS, c:c + P], start=True, stop=False)
                        mm = pe.matmul(o[:, c:c + P], ident_b[:, :], tri[:, 0:P], start=False, stop=True)
                    mm.then_inc(cum_ready, 1)

                def head(j):
                    pe.wait_ge(seen_ready, val(j + 1, it, 8))
                    if j == 4:
                        pe.wait_ge(own_copied, val(1, it, 1))
                    o = ps[SSD_P * (j % 2):SSD_P * (j % 2) + SSD_P, 7 if j < 4 else 4, (j // 2 % 2) * SEQ:(j // 2 % 2 + 1) * SEQ]
                    c = slice(j * SSD_P, (j + 1) * SSD_P)
                    pe.matmul(o[:, 0:P], x_tok2[:, 0, c], seen[:, j % 2, 0:P], start=True, stop=True)
                    pe.matmul(o[:, P:SEQ], x_tok2[:, 0, c], seen[:, j % 2, P:SEQ], start=True, stop=False)
                    pe.matmul(o[:, P:SEQ], x_tok2[:, 1, c], seen[:, j % 2, SEQ:SEEN], start=False, stop=True).then_inc(y_done, 1)

                for j in range(GROUP_HEADS + 1):
                    if j < GROUP_HEADS:
                        spread_cum(j)
                    if j:
                        head(j - 1)
                slab(10)
                pe.wait_ge(ysq_ready, val(4, it, 4))
                for b in range(NB):
                    for t in range(4):
                        mm = pe.matmul(ps[:, 5, b:b + 1], sq[:, t, b * P:(b + 1) * P], ones[:, 0:1], start=(t == 0), stop=(t == 3))
                mm.then_inc(ysum_ready, 1)
                slab(11)
                pe.wait_ge(ydiag_ready, val(1, it, 1))
                pe.matmul(ps[:, 6, 0:SEQ], ones, diag[:, 2:4].rearrange("p b t -> p (b t)"), start=True, stop=True).then_inc(yspread_ready, 1)

            for m in range(2 * NT):
                if m < 2:
                    pe.wait_ge(z_done, 1 + 4 * GROUPS)
                elif m < 4:
                    pe.wait_ge(u_done, 1 + 2 * GROUPS)
                else:
                    pe.wait_ge(gate_ready, m - 3)
                slab_gemm(pe, S_GATE + m, ps[:, m % 4, 0:SEQ], a_hi, a_lo)
            pe.wait_ge(pooled_operand, GROUPS)
            pe.wait_ge(yssd_ready, 4 * GROUPS)
            for a in range(2):
                s = S_POOL + a
                slab_ready(pe, s)
                for n in range(4):
                    for k in range(2):
                        t = slice((2 * n + k) * P, (2 * n + k + 1) * P)
                        i = 4 * a + 2 * (n // 2) + k
                        mm = mm3(pe, ps[:, 4 + 2 * a + n // 2, (n % 2) * SEQ:(n % 2 + 1) * SEQ], w_hi[:, s % RING, t], w_lo[:, s % RING, t],
                                 c_hi[:, i], c_lo[:, i], k == 0, k == 1)
                mm.then_inc(w_used, 1)
            pe.wait_ge(gate_ready, 2 * NT)
            pe.wait_ge(pw_operand, NT)
            pe.sem_inc(parts_ready, 2)
            with pe.Fori(0, NT // 2) as it:
                for u in range(2):
                    pe.wait_ge(parts_ready, val(u + 1, it, 2))
                    s = S_MERGE + 3 * u
                    slab_gemm(pe, s, ps[:, 2 * u, 0:SEQ], b_hi, b_lo, it, 6, last=False)
                    slab_gemm(pe, s + 1, ps[:, 2 * u, 0:SEQ], b_hi[:, NT:2 * NT], b_lo[:, NT:2 * NT], it, 6, first=False)
                    slab_gemm(pe, s + 2, ps[:, 2 * u + 1, 0:SEQ], a_hi, a_lo, it, 6)
            out_pe(pe, S_WOUT, False, c_hi, c_lo, res_ready, 5 * NT, (ready(merged_operand, 0)(pe),))

        def ssd_act(act):
            act_inv(act, 4)
            mod_act(act, 4)
            hi_ahead(act, S_DT + 3)
            act.wait_ge(dt_x_ready, 1)
            act.activation(dt_e[0:SSD_HEADS, :], dt_e[0:SSD_HEADS, :], ACT.Exp, scale=-1.0).then_inc(dt_e_ready, 1)
            act.activation(neg_a[0:SSD_HEADS, :], pcol("a_log", 0, SSD_HEADS), ACT.Exp).then_inc(decay_a, 1)
            with act.Fori(0, GROUPS) as it:
                def prm(t, j):
                    return par[:, bass.ds(it * 38 + COL["grp"] + 5 * t + j, 1)]

                def silu(t):
                    act.wait_ge(conv_done, val(t + 1, it, 6))
                    act.activation(cv[:, t], cv[:, t], ACT.Silu).then_inc(act_done, 1)

                def used(j):
                    act.wait_ge(w_used, val(S_GRP + j + 1, it, GRP))

                for j in range(10):
                    split_hi(act, S_GRP + j + 3, it, GRP)
                    if j < 6:
                        used(j)
                        act.activation(cv[:, j], ps[:, j % 4, 0:SEQ], ACT.Identity, bias=prm(j, 4), scale=prm(j, 3)).then_inc(tap_done, 1)
                    if 1 <= j < 7:
                        silu(j - 1)
                    if j == 4:
                        act.wait_ge(cb_ready, val(1, it, 1))
                        act.activation(cb, ps[:, 4, 0:SEEN], ACT.Copy).then_inc(cb_copied, 1)
                    if j >= 6:
                        used(j)
                        act.activation(z_s[:, j - 6], ps[:, j % 4, 0:SEQ], ACT.Silu).then_inc(z_done, 1)
                for j in range(GROUP_HEADS):
                    act.wait_ge(cum_ready, val(j + 1, it, 8))
                    if j == 0:
                        act.wait_ge(own_copied, val(1, it, 1))
                    if j >= 2:
                        act.wait_ge(y_done, val(j - 1, it, 8))
                    for b in range(NB):
                        c = slice(0, SEQ) if b == 0 else slice(SEQ, SEEN)
                        act.activation(seen[:, j % 2, c], ps[:, 5 + j % 2, c], ACT.Exp, bias=neg_cum[:, b, j:j + 1]).then_inc(exp_done, 1)
                for t in range(4):
                    act.wait_ge(yz_ready, val(t + 1, it, 4))
                    act.activation(sq[:, t], z_s[:, t], ACT.Square).then_inc(ysq_ready, 1)
                for j in range(10, 12):
                    split_hi(act, S_GRP + j + 3, it, GRP)
                    if j == 11:
                        act_root(act, RS_SSD, NB, it)
                    used(j)
                    act.activation(u_f[:, bass.ds(it * 2 + j - 10, 1)].rearrange("p a t -> p (a t)"), ps[:, j % 4, 0:SEQ],
                                   ACT.Copy).then_inc(u_done, 1)
                act.wait_ge(yspread_ready, val(1, it, 1))
                act.activation(inv_s, ps[:, 6, 0:SEQ], ACT.Copy).then_inc(inv_s_ready, 1)
                for t in range(4):
                    act.wait_ge(yn_ready, val(t + 1, it, 4))
                    act.activation(b_hi[:, bass.ds(it * 4 + t, 1)].rearrange("p a t -> p (a t)"), cv[:, 2 + t], ACT.Copy).then_inc(yhi_ready, 1)

            for m in range(2 * NT):
                hi_ahead(act, S_GATE + m + 3)
                act.wait_ge(w_used, S_GATE + m + 1)
                act.activation(gates[:, m], ps[:, m % 4, 0:SEQ], ACT.Sigmoid).then_inc(gate_ready, 1)
                if m % 4 == 3:
                    g = m // 4
                    act.wait_ge(pooled_ready, g + 1)
                    act.activation(c_hi[:, 2 * g:2 * g + 2], win_of(g), ACT.Copy).then_inc(pooled_hi, 1)
            for a in range(2):
                hi_ahead(act, S_POOL + a + 3)
                act.wait_ge(w_used, S_POOL + a + 1)
                for n in range(4):
                    act.activation(sq[:, 4 * a + n], ps[:, 4 + 2 * a + n // 2, (n % 2) * SEQ:(n % 2 + 1) * SEQ], ACT.Copy,
                                   scale=pcol("pool_scale", 4 * a + n)).then_inc(pw_ready, 1)
                act.wait_ge(pw_ready, 4 * a + 4)
                act.activation(a_hi[:, 4 * a:4 * a + 4], sq[:, 4 * a:4 * a + 4], ACT.Copy).then_inc(pw_hi, 1)
            with act.Fori(0, NT // 2) as it:
                for u in range(2):
                    for n in range(3):
                        split_hi(act, S_MERGE + 3 * u + n + 3, it, 6)
                    act.wait_ge(merged_ready, val(u + 1, it, 2))
                    act.activation(c_hi[:, bass.ds(it * 2 + u, 1)].rearrange("p a t -> p (a t)"), merged[:, u], ACT.Copy).then_inc(merged_hi, 1)
            for m in range(NT):
                hi_ahead(act, S_WOUT + m + 3)
                square(act, 5, m)

        def win_of(g):
            return win[g % 2]

        def ssd_vec(dve, step):
            mod_vec(dve, step, 4)
            lo_ahead(dve, S_DT + 3)
            h = slice(0, SSD_HEADS)
            dve.wait_ge(w_used, S_DT + 1)
            step(dve.tensor_scalar(dt_x[h], ps[h, 4, 0:SEQ], pcol("dt_bias", 0, SSD_HEADS), None, ALU.add))
            dve.scalar_tensor_tensor(out=dt_e[h], in0=dt_x[h], scalar=-1.0, in1=dt_x[h], op0=ALU.mult, op1=ALU.max).then_inc(dt_x_ready, 1)
            dve.wait_ge(dt_e_ready, 1)
            step(dve.tensor_scalar(dt_z[h], dt_e[h], 2.0, None, ALU.add))
            step(dve.reciprocal(dt_z[h], dt_z[h]))
            step(dve.tensor_tensor(dt_z[h], dt_z[h], dt_e[h], ALU.mult))
            step(dve.tensor_tensor(dt_e[h], dt_z[h], dt_z[h], ALU.mult))
            step(dve.tensor_scalar(dt_f[h], dt_e[h], 1.0 / 15, None, ALU.mult))
            for n in range(13, 1, -2):
                step(dve.scalar_tensor_tensor(out=dt_f[h], in0=dt_f[h], scalar=1.0 / n, in1=dt_e[h], op0=ALU.add, op1=ALU.mult))
            step(dve.scalar_tensor_tensor(out=dt_f[h], in0=dt_f[h], scalar=1.0, in1=dt_z[h], op0=ALU.add, op1=ALU.mult))
            step(dve.tensor_scalar(dt_f[h], dt_f[h], 2.0, None, ALU.mult))
            step(dve.scalar_tensor_tensor(out=dt_f[h], in0=dt_x[h], scalar=0.0, in1=dt_f[h], op0=ALU.max, op1=ALU.add))
            dve.wait_ge(decay_a, 1)
            step(dve.tensor_scalar(dt_x[h], dt_f[h], neg_a[h, 0:1], -1.0, ALU.mult, ALU.mult))
            step(dve.memset(dt_e[h], 1.0))
            dve.tensor_tensor_scan(cum[h, 0:SEQ], dt_e[h], dt_x[h], 0.0, ALU.mult, ALU.add).then_inc(dt_ready, 1)
            dve.wait_ge(dt_ready, 1)
            dve.tensor_copy(cum[h, SEQ:SEEN], cum[h, P:SEQ]).then_inc(dt_ready, 1)
            dve.wait_ge(dt_ready, 2)

            with dve.Fori(0, GROUPS) as it:
                step.enter(it, 22)

                def prm(c):
                    return par[:, bass.ds(it * 38 + COL["grp"] + c, 1)]

                dve.tensor_copy(pick_h[h], con[h, bass.ds(it * GROUP_HEADS + CC["ident"], GROUP_HEADS)].unsqueeze(2)
                                .broadcast_to((SSD_HEADS, GROUP_HEADS, P))).then_inc(pick_ready, 1)
                for j in range(10):
                    split_lo(dve, S_GRP + j + 3, it, GRP)
                    if j < 6:
                        dve.wait_ge(tap_done, val(j + 1, it, 6))
                        for n in range(1, 4):
                            ins = dve.scalar_tensor_tensor(out=cv[:, j, n:SEQ], in0=ps[:, j % 4, 0:SEQ - n], scalar=prm(5 * j + 3 - n),
                                                           in1=cv[:, j, n:SEQ], op0=ALU.mult, op1=ALU.add)
                            if n < 3:
                                step(ins)
                        ins.then_inc(conv_done, 1)
                    if j == 7:
                        dve.wait_ge(own_ready, val(1, it, 1))
                        step(dve.tensor_copy(dt_tok.rearrange("p b h -> p (b h)"), ps[:, 4, 400:416]))
                        dve.tensor_scalar(neg_cum.rearrange("p b h -> p (b h)"), ps[:, 4, 416:432], -1.0, None, ALU.mult).then_inc(own_copied, 1)
                    if j == 8:
                        for b in range(NB):
                            dve.wait_ge(x_turned, val(b + 1, it, 2))
                            dve.tensor_tensor(x_tok2[:, b].rearrange("p (h d) -> p h d", h=GROUP_HEADS),
                                              ps[:, 5 + b, :].rearrange("p (h d) -> p h d", h=GROUP_HEADS),
                                              dt_tok[:, b].unsqueeze(2).broadcast_to((P, GROUP_HEADS, SSD_P)), ALU.mult).then_inc(x_tok_ready, 1)

                def skip_and_gate(t):
                    dve.wait_ge(y_done, val(4 * (t // 2) + 4, it, 8))
                    dve.wait_ge(z_done, val(t + 2, it, 4))
                    step(dve.scalar_tensor_tensor(out=cv[:, 2 + t], in0=cv[:, 2 + t], scalar=prm(30 + t),
                                                  in1=ps[:, 4 if t // 2 else 7, (t % 2) * SEQ:(t % 2 + 1) * SEQ], op0=ALU.mult, op1=ALU.add))
                    dve.tensor_tensor(z_s[:, t], cv[:, 2 + t], z_s[:, t], ALU.mult).then_inc(yz_ready, 1)

                dve.wait_ge(cb_copied, val(1, it, 1))
                for j in range(GROUP_HEADS):
                    dve.wait_ge(exp_done, val(2 * j + 2, it, 16))
                    dve.tensor_tensor(seen[:, j % 2], seen[:, j % 2], cb, ALU.mult).then_inc(seen_ready, 1)
                    if j >= 6:
                        skip_and_gate(j - 6)
                skip_and_gate(2)
                skip_and_gate(3)
                split_lo(dve, S_GRP + 13, it, GRP)
                dve.wait_ge(ysum_ready, val(1, it, 1))
                dve.tensor_scalar(rs_var[:, 0:NB], ps[:, 5, 0:NB], 1.0 / 512, EPS_B, ALU.mult, ALU.add).then_inc(var_ready, 1)
                split_lo(dve, S_GRP + 14, it, GRP)
                rsqrt(dve, step, RS_SSD, NB, root_s, it)
                step(dve.tensor_scalar(diag[:, 2], ident, root_s[:, 0:1], None, ALU.mult))
                dve.tensor_scalar(diag[:, 3], ident, root_s[:, 1:2], None, ALU.mult).then_inc(ydiag_ready, 1)
                dve.wait_ge(inv_s_ready, val(1, it, 1))

                def y_lo(t):
                    dve.wait_ge(yhi_ready, val(t + 1, it, 4))
                    o = bass.ds(it * 4 + t, 1)
                    dve.tensor_tensor(b_lo[:, o].rearrange("p a t -> p (a t)"), cv[:, 2 + t], b_hi[:, o].bitcast(F32).rearrange("p a t -> p (a t)"),
                                      ALU.subtract).then_inc(yssd_ready, 1)

                for t in range(4):
                    dve.scalar_tensor_tensor(out=cv[:, 2 + t], in0=z_s[:, t], scalar=prm(34 + t), in1=inv_s,
                                             op0=ALU.mult, op1=ALU.mult).then_inc(yn_ready, 1)
                    if t:
                        y_lo(t - 1)
                y_lo(3)
            step.leave(GROUPS)

            dve.wait_ge(u_done, 1 + 2 * GROUPS)
            dve.wait_ge(yssd_ready, 4 * GROUPS)

            def pool(g):
                u = u_f[:, 2 * g:2 * g + 2]
                cur = u
                for i in range(g + 1):
                    nxt = win[i % 2]
                    dve.tensor_copy(nxt[:, :, 0:2 ** i], cur[:, :, 0:2 ** i])
                    step(dve.tensor_tensor(nxt[:, :, 2 ** i:SEQ], cur[:, :, 2 ** i:SEQ], cur[:, :, 0:SEQ - 2 ** i], ALU.add))
                    cur = nxt
                for t in range(2):
                    ins = dve.tensor_tensor(cur[:, t, 0:16], cur[:, t, 0:16], const("ramp", 16, at=16 * g), ALU.mult)
                step(ins)
                dve.scalar_tensor_tensor(out=cur, in0=cur, scalar=0.5 ** (g + 1), in1=u, op0=ALU.mult, op1=ALU.subtract).then_inc(pooled_ready, 1)
                dve.wait_ge(pooled_ready, g + 1)

            def pooled_lo(g):
                dve.wait_ge(pooled_hi, g + 1)
                dve.tensor_tensor(c_lo[:, 2 * g:2 * g + 2], win_of(g), c_hi[:, 2 * g:2 * g + 2].bitcast(F32), ALU.subtract).then_inc(pooled_operand, 1)
                dve.wait_ge(pooled_operand, g + 1)

            for m in range(2 * NT):
                lo_ahead(dve, S_GATE + m + 3)
                if m % 4 == 2:
                    pool(m // 4)
                if m % 4 == 3:
                    pooled_lo(m // 4)
            for a in range(2):
                lo_ahead(dve, S_POOL + a + 3)
                dve.wait_ge(pw_hi, a + 1)
                dve.tensor_tensor(a_lo[:, 4 * a:4 * a + 4], sq[:, 4 * a:4 * a + 4], a_hi[:, 4 * a:4 * a + 4].bitcast(F32),
                                  ALU.subtract).then_inc(pw_operand, 4)
            with dve.Fori(0, NT // 2) as it:
                step.enter(it, 0)
                for u in range(2):
                    for n in range(3):
                        split_lo(dve, S_MERGE + 3 * u + n + 3, it, 6)
                    dve.wait_ge(w_used, val(S_MERGE + 3 * u + 3, it, 6))
                    dve.tensor_tensor(part[:, u, 0], ps[:, 2 * u, 0:SEQ], gates[:, bass.ds(it * 2 + u, 1)].rearrange("p a t -> p (a t)"), ALU.mult)
                    dve.tensor_tensor(part[:, u, 1], ps[:, 2 * u + 1, 0:SEQ], gates[:, bass.ds(it * 2 + NT + u, 1)].rearrange("p a t -> p (a t)"),
                                      ALU.mult).then_inc(parts_ready, 1)
                    dve.wait_ge(parts_ready, val(u + 3, it, 2))
                    dve.tensor_tensor(merged[:, u], part[:, u, 0], part[:, u, 1], ALU.add).then_inc(merged_ready, 1)
                    dve.wait_ge(merged_hi, val(u + 1, it, 2))
                    o = bass.ds(it * 2 + u, 1)
                    dve.tensor_tensor(c_lo[:, o].rearrange("p a t -> p (a t)"), merged[:, u], c_hi[:, o].bitcast(F32).rearrange("p a t -> p (a t)"),
                                      ALU.subtract).then_inc(merged_operand, 1)
            step.leave(NT // 2)
            for m in range(NT):
                lo_ahead(dve, S_WOUT + m + 3)
                dve.wait_ge(w_used, S_WOUT + m + 1)
                dve.scalar_tensor_tensor(out=res[:, m], in0=ps[:, 4 + (m + 2) % 4, 0:SEQ], scalar=mod[:, 2 * NT + m:2 * NT + m + 1], in1=res[:, m],
                                         op0=ALU.mult, op1=ALU.add).then_inc(res_ready, 1)

        top[0] = 0
        relu, hidden = area(3, SEQ), area(3, SEQ)
        normal = area(NT, SEQ)
        result = area(NB, DM)
        relu_ready, hidden_ready, hidden_hi, hidden_operand = (
            sem(n) for n in ("relu_ready", "hidden_ready", "hidden_hi", "hidden_operand"))
        normal_ready, normal_turned, block_0_ready, block_1_ready, stored = (
            sem(n) for n in ("normal_ready", "normal_turned", "block_0_ready", "block_1_ready", "stored"))
        MLP_TURNS = (MLP_TILES - 5) // 3

        def up_at(n):
            return S_MLP + (n if n < 2 else 2 * n - 2)

        def down_at(n):
            return S_MLP + (2 * n + 3 if n < MLP_TILES - 2 else MLP_TILES + n)

        def mlp_pe(pe):
            def up_tile(n, it=None, each=None):
                slab_gemm(pe, up_at(n), ps[:, 4 + n % 3, 0:SEQ], a_hi, a_lo, it, 6, each=each)

            def down(n, it=None):
                pe.wait_ge(hidden_operand, val(n + 1, it, 3))
                down_slab(pe, down_at(n), b_hi[:, n % 3], b_lo[:, n % 3], n == 0, n == MLP_TILES - 1, it, 6)

            for k in range(NT):
                sum_squares(pe, 5, k)
            spread_inv(pe, 5)
            up_tile(0, each=ready(a_ready, 5 * NT)(pe))
            up_tile(1)
            for n in range(3):
                up_tile(n + 2)
                down(n)
            with pe.Fori(0, MLP_TURNS) as it:
                for n in range(3, 6):
                    up_tile(n + 2, it)
                    down(n, it)
            for n in range(3 + 3 * MLP_TURNS, MLP_TILES):
                if n + 2 < MLP_TILES:
                    up_tile(n + 2)
                down(n)
            for k in range(NT):
                sum_squares(pe, 6, k)
            spread_inv(pe, 6)
            pe.wait_ge(res_ready, 7 * NT)
            for q in range(NT // 4):
                for m in range(4 * q, 4 * q + 4):
                    pe.wait_ge(normal_ready, m + 1)
                    for b in range(NB):
                        mm = pe.transpose(ps[:, 2 * q + b, (m % 4) * P:(m % 4 + 1) * P], normal[:, m, b * P:(b + 1) * P], ident)
                mm.then_inc(normal_turned, 1)

        def mlp_act(act):
            act_inv(act, 5)
            mod_act(act, 5)

            def relu_of(n, it=None):
                act.wait_ge(w_used, val(up_at(n) + 1, it, 6))
                if n >= 3:
                    act.wait_ge(hidden_ready, val(n - 2, it, 3))
                act.activation(relu[:, n % 3], ps[:, 4 + n % 3, 0:SEQ], ACT.Relu).then_inc(relu_ready, 1)

            def high(n, it=None):
                act.wait_ge(hidden_ready, val(n + 1, it, 3))
                if n >= 3:
                    act.wait_ge(w_used, val(down_at(n - 3) + 1, it, 6))
                act.activation(b_hi[:, n % 3], hidden[:, n % 3], ACT.Copy).then_inc(hidden_hi, 1)

            def tile(n, it=None):
                hi_ahead(act, up_at(n) + 3, it, 6)
                relu_of(n, it)
                high(n, it)
                if n >= 2:
                    hi_ahead(act, down_at(n - 2) + 3, it, 6)

            for n in range(5):
                tile(n)
            with act.Fori(0, MLP_TURNS - 1) as it:
                for n in range(5, 8):
                    tile(n, it)
            for n in range(2 + 3 * MLP_TURNS, MLP_TILES):
                tile(n)
            for m in range(NT):
                square(act, 6, m)
            act_inv(act, 6)
            for q in range(NT // 4):
                act.wait_ge(normal_turned, q + 1)
                act.activation(result[:, 1, 512 * q:512 * (q + 1)], ps[:, 2 * q + 1, :], ACT.Copy).then_inc(block_1_ready, 1)

        def mlp_vec(dve, step):
            mod_vec(dve, step, 5)

            def hidden_of(n, it=None):
                dve.wait_ge(relu_ready, val(n + 1, it, 3))
                if n >= 3:
                    dve.wait_ge(hidden_operand, val(n - 2, it, 3))
                dve.tensor_tensor(hidden[:, n % 3], relu[:, n % 3], relu[:, n % 3], ALU.mult).then_inc(hidden_ready, 1)

            def low(n, it=None):
                dve.wait_ge(hidden_hi, val(n + 1, it, 3))
                dve.tensor_tensor(b_lo[:, n % 3], hidden[:, n % 3], b_hi[:, n % 3].bitcast(F32), ALU.subtract).then_inc(hidden_operand, 1)

            def tile(n, it=None):
                lo_ahead(dve, up_at(n) + 3, it, 6)
                hidden_of(n, it)
                if n >= 2:
                    lo_ahead(dve, down_at(n - 2) + 3, it, 6)
                low(n, it)

            for n in range(5):
                tile(n)
            with dve.Fori(0, MLP_TURNS - 1) as it:
                for n in range(5, 8):
                    tile(n, it)
            for n in range(2 + 3 * MLP_TURNS, MLP_TILES):
                tile(n)
            dve.wait_ge(w_used, SLABS)
            for m in range(NT):
                dve.scalar_tensor_tensor(out=res[:, m], in0=ps[:, m // 2, (m % 2) * SEQ:(m % 2 + 1) * SEQ],
                                         scalar=mod[:, 5 * NT + m:5 * NT + m + 1], in1=res[:, m],
                                         op0=ALU.mult, op1=ALU.add).then_inc(res_ready, 1)
            vec_inv(dve, step, 6, EPS_B)
            dve.wait_ge(inv_ready, 7)
            for m in range(NT):
                dve.scalar_tensor_tensor(out=normal[:, m], in0=res[:, m], scalar=pcol("final_w", m), in1=inv[:, :],
                                         op0=ALU.mult, op1=ALU.mult).then_inc(normal_ready, 1)
            for q in range(NT // 4):
                dve.wait_ge(normal_turned, q + 1)
                dve.tensor_copy(result[:, 0, 512 * q:512 * (q + 1)], ps[:, 2 * q, :]).then_inc(block_0_ready, 1)
        block = ctx.enter_context(nc.Block())

        @block.sync
        def _(sp):
            sp.dma_start(par[:, :], params).then_inc(small_in, 16)
            sp.dma_start(con[:, :], consts).then_inc(small_in, 16)
            sp.dma_start(x_tok, x.rearrange("(b p) d -> p b d", p=P)).then_inc(x_in, 16)

            def load(s, it=None, ds=0):
                slot = s % RING
                if s >= RING:
                    sp.wait_ge(w_lo_ready, val(s - RING + 1, it, ds))
                src = stream[s] if it is None else stream[bass.ds(it * ds + s, 1)].rearrange("a p n -> (a p) n")
                sp.dma_start(w_raw[:, slot], src).then_inc(w_landed[slot], 16)

            def load_range(a, b):
                turns = (b - a) // RING
                if turns > 1:
                    with sp.Fori(0, turns) as it:
                        for u in range(RING):
                            load(a + u, it, RING)
                    a += turns * RING
                for s in range(a, b):
                    load(s)

            load_range(0, RING)
            load_range(RING, S_FFN0 + RING)
            sp.wait_ge(res_ready, 2 * NT)
            sp.dma_start(cond_row, c_rows).then_inc(cond_in, 16)
            load_range(S_FFN0 + RING, SLABS)
            for q in range(NT // 4):
                sp.wait_ge(block_0_ready, q + 1)
                sp.wait_ge(block_1_ready, q + 1)
                sp.dma_start(out.rearrange("(b p) d -> p b d", p=P)[:, :, 512 * q:512 * (q + 1)],
                             result[:, :, 512 * q:512 * (q + 1)]).then_inc(stored, 16)
            sp.wait_ge(stored, 16 * (NT // 4))

        @block.tensor
        def _(pe):
            attention_pe(pe)
            ffn_pe(pe, 0, S_FFN0, 1)
            retention_pe(pe)
            ffn_pe(pe, 1, S_FFN1, 3)
            ssd_pe(pe)
            mlp_pe(pe)

        @block.scalar
        def _(act):
            attention_act(act)
            ffn_act(act, 0, S_FFN0, 1, "mix_g1")
            retention_act(act)
            ffn_act(act, 1, S_FFN1, 3, None)
            ssd_act(act)
            mlp_act(act)

        @block.gpsimd
        def _(pool):
            modulation_pool(pool, Steps(pool, pool_step))

        @block.vector
        def _(dve):
            step = Steps(dve, vec_step)
            attention_vec(dve, step)
            ffn_vec(dve, step, 0, S_FFN0, 1, "mix_g1")
            retention_vec(dve, step)
            ffn_vec(dve, step, 1, S_FFN1, 3, None)
            ssd_vec(dve, step)
            mlp_vec(dve, step)


def _tiles(w):
    k, m = w.shape
    t = w.reshape(k // P, P, m // P, P).transpose(2, 1, 0, 3)
    return t.reshape(m // P, P, k // SLAB, SLAB).transpose(0, 2, 1, 3).reshape(-1, P, SLAB)


def _rows(w):
    return w.reshape(-1, P, SLAB)


def _wide(w):
    return w.reshape(4, 2, P, 512).transpose(0, 2, 1, 3).reshape(4, P, SLAB)


def _mix(*parts):
    return np.stack(parts, axis=1).reshape(-1, P, SLAB)


def _stream(a):
    out = []
    w = a["a_w_in"][0]
    q, c, qi, ki, wi = np.split(w, [1024, 1152, 1664, 1728], axis=1)
    pad = np.zeros((DM, P - IDX_DIM - HEADS_A), w.dtype)
    out += [_tiles(np.concatenate([c, ki, wi, pad, qi, q], axis=1)), _tiles(a["a_w_out"][0])]

    def ffn(i):
        up, down = a["f_w_up"][i], _rows(a["f_w_down"][i])
        pairs = _mix(_tiles(up[:, :2816]), _tiles(up[:, 2816:]))
        for p in range(FF_PAIRS):
            out.append(pairs[2 * p:2 * p + 2])
            if p:
                out.append(down[p - 1:p])
        out.append(down[-1:])

    ffn(0)
    w = a["b_w_in"][0]
    for h in range(HEADS_B):
        out += [_tiles(w[:, 256 * h:256 * (h + 1)]), _tiles(w[:, DM + 256 * h:DM + 256 * (h + 1)]),
                _wide(w[:, 2 * DM + 512 * h:2 * DM + 512 * (h + 1)]), _tiles(w[:, 4 * DM + 512 * h:4 * DM + 512 * (h + 1)])]
    out.append(_tiles(a["b_w_out"][0]))
    ffn(1)
    z, xs, b, c, dt, u, gates = np.split(a["w_in_2"][0], [2048, 4096, 4608, 5120, 5152, 6176], axis=1)
    out.append(_tiles(np.concatenate([dt, np.zeros((DM, P - SSD_HEADS), dt.dtype)], axis=1)))
    for g in range(GROUPS):
        out.append(_tiles(np.concatenate([
            b[:, P * g:P * (g + 1)], c[:, P * g:P * (g + 1)], xs[:, 512 * g:512 * (g + 1)],
            z[:, 512 * g:512 * (g + 1)], u[:, 256 * g:256 * (g + 1)],
        ], axis=1)))
    out.append(_tiles(gates))
    out.append(a["pool_w_2"][0].reshape(2, 2, 2, P, 2, P).transpose(0, 3, 1, 4, 2, 5).reshape(2, P, SLAB))
    ssd, pool = _tiles(a["w_branch_ssd_2"][0]), _tiles(a["w_branch_pool_2"][0])
    for m in range(NT):
        out += [ssd[2 * m:2 * m + 2], pool[m:m + 1]]
    out.append(_tiles(a["w_out_2"][0]))
    up, down = _tiles(a["w_up_2"][0]), _rows(a["w_down_2"][0])
    out.append(up[:2])
    for j in range(2, MLP_TILES):
        out += [up[j:j + 1], down[j - 2:j - 1]]
    out.append(down[-2:])
    out = np.concatenate(out)
    assert out.shape[0] == SLABS, out.shape
    return out


def _params(a):
    cols = np.zeros((P, PARAMS), np.float32)

    def put(name, rows, at=0):
        rows = np.asarray(rows)
        cols[:rows.shape[-1], COL[name] + at:COL[name] + at + rows.shape[0]] = rows.T

    for i in range(2):
        put(f"mix_g{i}", a["norm_mix_g"][i].reshape(-1, P))
        put(f"ffn_g{i}", a["norm_ffn_g"][i].reshape(-1, P))
        w, b = a["f_conv_w"][i].reshape(3, 2, FF_PAIRS, P), a["f_conv_b"][i].reshape(2, FF_PAIRS, P)
        for p in range(FF_PAIRS):
            put(f"ffn{i}", np.concatenate([w[:, 0, p], w[:, 1, p], b[:, p]]), 8 * p)
    put("q_g", a["a_q_g"])
    put("k_g", a["a_k_g"])
    put("iq_g", np.tile(a["a_iq_g"], 2))
    put("ik_g", np.tile(a["a_ik_g"], 2))
    put("out_g", a["b_out_g"][0].reshape(-1, P))
    put("b_ada", a["b_ada_2"][0].reshape(-1, P))
    put("mix_w", a["norm_mix_w_2"][0].reshape(-1, P))
    cw, cb = a["conv_w_2"][0].reshape(4, 24, P), a["conv_b_2"][0].reshape(1, 24, P)
    skip = np.repeat(a["d_skip_2"][0], SSD_P).reshape(-1, P)
    norm = a["ssd_norm_w_2"][0].reshape(-1, P)
    for g in range(GROUPS):
        for n, t in enumerate([16 + g, 20 + g, *range(4 * g, 4 * g + 4)]):
            put("grp", np.concatenate([cw[:, t], cb[:, t]]), 38 * g + 5 * n)
        put("grp", skip[4 * g:4 * g + 4], 38 * g + 30)
        put("grp", norm[4 * g:4 * g + 4], 38 * g + 34)
    put("dt_bias", a["dt_bias_2"])
    put("a_log", a["a_log_2"])
    put("pool_scale", a["pool_scale_2"][0].reshape(-1, P))
    put("mlp_w", a["norm_mlp_w_2"][0].reshape(-1, P))
    put("final_w", a["norm_final_w_2"].reshape(-1, P))
    return cols


def _consts():
    c = np.zeros((P, CONSTS), np.float32)
    i, t = np.arange(P), np.arange(SEQ)

    def put(name, x):
        c[:x.shape[0], CC[name]:CC[name] + x.shape[1]] = x

    put("ident", np.eye(P))
    put("ones", np.ones((P, P)))
    put("halves", (i[:, None] // IDX_DIM == np.arange(2)[None]).astype(np.float32))
    put("dup", np.tile(np.eye(IDX_DIM), (1, 2)))
    inv = (np.float32(1.0) / np.float32(10000.0) ** (np.arange(0, 256, 2, dtype=np.float32) / np.float32(256))).astype(np.float32)
    ang = (t.astype(np.float32)[None, :] * inv[:, None]).astype(np.float32).astype(np.float64)
    put("cos", np.cos(ang))
    put("sin", np.sin(ang))
    log_gamma = np.log1p(-(2.0 ** (-5.0 - np.arange(HEADS_B))))
    gap = np.concatenate([t[None, :] - i[:, None], t[None, P:] - i[:, None] - P], axis=1)
    for h in range(HEADS_B):
        d = np.where(gap >= 0, np.exp(np.maximum(gap, 0) * log_gamma[h]), 0.0) * 256.0 ** -0.5
        c[:, CC["decay"] + SEEN * h:CC["decay"] + SEEN * (h + 1)] = d
    limit = (t // 64 + 1) * 64
    put("admit", np.concatenate([
        np.where(i[None, :] < limit[:P, None], 0.0, MASKED), np.where(t[None, :] < limit[P:, None], 0.0, MASKED),
    ], axis=1))
    tri = np.where(i[None, :] >= i[:, None], 0.0, -1e30)
    put("tri", np.concatenate([tri, np.zeros((P, P)), tri], axis=1))
    for g in range(4):
        win = 2 ** (g + 1)
        c[:, CC["ramp"] + 16 * g:CC["ramp"] + 16 * (g + 1)] = win / np.minimum(np.arange(16) + 1, win)
    return c


_OUT = (1, SEQ, DM)


def kernel(**inputs):
    import concourse.bacc as _bacc
    from concourse.bass_utils import run_bass_kernel_spmd as _run

    a = {k: np.asarray(v) for k, v in inputs.items()}
    arrays = {"x": a["x"][0], "stream": _stream(a),
              "ada": np.ascontiguousarray(a["w_ada_2"][0].T).reshape(ADA_TILES, P, DM),
              "c_rows": np.broadcast_to(a["c_2"], (P, DM)).copy(), "params": _params(a), "consts": _consts()}
    nc = _bacc.Bacc("TRN2", target_bir_lowering=False, num_devices=1)
    args = {k: nc.dram_tensor(k, v.shape, F32, kind="ExternalInput").ap() for k, v in arrays.items()}
    out = nc.dram_tensor("out", (SEQ, DM), F32, kind="ExternalOutput").ap()
    build(nc, out=out, **args)
    r = _run(nc, [arrays], core_ids=[0])
    return np.asarray(r.results[0]["out"]).reshape(_OUT)
```

```python
from contextlib import ExitStack

import numpy as np

import concourse.bass as bass
from concourse import mybir

F32 = mybir.dt.float32
F32R = mybir.dt.float32r
BF16 = mybir.dt.bfloat16
ALU = mybir.AluOpType
ACT = mybir.ActivationFunctionType
AX = mybir.AxisListType

P = 128
SEQ, DM = 256, 1024
NT = DM // P
NB = SEQ // P
FF_PAIRS = 2816 // P
MLP_TILES = 4 * DM // P
HEADS_A, LAT, IDX_DIM, TOPK = 8, 128, 64, 64
HEADS_B = 4
GROUPS, GROUP_HEADS, SSD_HEADS, SSD_P = 4, 8, 32, 64
EPS_A, EPS_B = 1e-6, 1e-5
MASKED, TAKEN = -3.0e38, -3.3e38
SEEN = 384

ARENA = 9180
RING = 6
SLAB = 8 * P
S_AIN = 0
S_AOUT = S_AIN + 14
S_FFN0 = S_AOUT + NT
S_B = S_FFN0 + 3 * FF_PAIRS
S_BOUT = S_B + 12 * HEADS_B
S_FFN1 = S_BOUT + 2 * NT
S_DT = S_FFN1 + 3 * FF_PAIRS
S_GRP = S_DT + 1
S_GATE = S_GRP + 12 * GROUPS
GATES_FIRST = 12
S_POOL = S_GATE + GATES_FIRST
S_MERGE = S_GATE + 2 * NT + 2
S_WOUT = S_MERGE + 3 * NT
S_MLP = S_WOUT + NT
SLABS = S_MLP + 2 * MLP_TILES
ADA_TILES = 6 * NT

_widths = [
    ("mix_g0", NT), ("ffn_g0", NT), ("mix_g1", NT), ("ffn_g1", NT), ("q_g", 1), ("k_g", 1), ("iq_g", 1), ("ik_g", 1),
    ("ffn0", 8 * FF_PAIRS), ("ffn1", 8 * FF_PAIRS), ("out_g", 16), ("b_ada", 48), ("mix_w", NT),
    ("grp", 38 * GROUPS), ("dt_bias", 1), ("a_log", 1), ("pool_scale", NT), ("mlp_w", NT), ("final_w", NT),
]
COL, PARAMS = {}, 0
for _name, _w in _widths:
    COL[_name] = PARAMS
    PARAMS += _w
_widths = [("ident", P), ("ones", P), ("halves", 2), ("dup", P), ("cos", SEQ), ("sin", SEQ), ("decay", HEADS_B * SEEN),
           ("admit", SEEN), ("tri", SEEN), ("ramp", 4 * 16)]
CC, CONSTS = {}, 0
for _name, _w in _widths:
    CC[_name] = CONSTS
    CONSTS += _w


def val(base, it=None, step=0):
    return base if it is None else it * step + base


class Steps:

    def __init__(self, eng, sem):
        self.eng, self.sem, self.n, self.it, self.per = eng, sem, 0, None, 0

    def __call__(self, ins):
        ins.then_inc(self.sem, 1)
        self.n += 1
        self.eng.wait_ge(self.sem, val(self.n, self.it, self.per))

    def enter(self, it, per):
        self.it, self.per, self.start = it, per, self.n

    def leave(self, turns):
        assert self.n - self.start == self.per, (self.n - self.start, self.per)
        self.n, self.it, self.per = self.start + self.per * turns, None, 0


def build(nc, x, stream, ada, c_rows, params, consts, out):
    ctx = ExitStack()
    with ctx:
        def sb(name, shape, dt=F32):
            return ctx.enter_context(nc.sbuf_tensor(name, shape, dt))

        def sem(name):
            return ctx.enter_context(nc.semaphore(name))

        w_raw = sb("w_raw", [P, RING, SLAB])
        w_hi = sb("w_hi", [P, RING, SLAB], F32R)
        w_lo = sb("w_lo", [P, RING, SLAB], F32R)
        a_hi, a_lo = sb("a_hi", [P, NT, SEQ], F32R), sb("a_lo", [P, NT, SEQ], F32R)
        b_hi, b_lo = sb("b_hi", [P, 2 * NT, SEQ], F32R), sb("b_lo", [P, 2 * NT, SEQ], F32R)
        c_hi, c_lo = sb("c_hi", [P, NT, SEQ], F32R), sb("c_lo", [P, NT, SEQ], F32R)
        res = sb("res", [P, NT, SEQ])
        sq = sb("sq", [P, NT, SEQ])
        inv = sb("inv", [P, SEQ])
        inv_tok = sb("inv_tok", [P, NB])
        par, con = sb("par", [P, PARAMS]), sb("con", [P, CONSTS])
        tri = sb("tri", [P, SEEN], BF16)
        ident_b = sb("ident_b", [P, P], BF16)
        rs_var, rs_root, rs_y, rs_t = (sb(f"rs_{n}", [P, 24]) for n in ("var", "root", "y", "t"))
        table_probe = sb("table_probe", [P, 7])
        diag = sb("diag", [P, 4, P])
        mod = sb("mod", [P, 48])
        eff_scale = sb("eff_scale", [P, 2, NT])
        arena = sb("arena", [P, ARENA])
        ps = ctx.enter_context(nc.psum_tensor("ps", [P, 8, 512], F32))

        top = [0]

        def area(*shape):
            n = int(np.prod(shape))
            piece = arena[:, top[0]:top[0] + n]
            top[0] += n
            assert top[0] <= ARENA, top[0]
            names = " ".join(f"d{i}" for i in range(len(shape)))
            if len(shape) == 1:
                return piece
            return piece.rearrange(f"p ({names}) -> p {names}", **{f"d{i}": s for i, s in enumerate(shape)})

        def const(name, n, rows=P, at=0):
            return con[0:rows, CC[name] + at:CC[name] + at + n]

        def pcol(name, at=0, rows=P, n=1):
            return par[0:rows, COL[name] + at:COL[name] + at + n]

        ident, ones = const("ident", P), const("ones", P)

        small_in, par_in, tables_in, x_in = (sem(n) for n in ("small_in", "par_in", "tables_in", "x_in"))
        w_landed = [sem(f"w_landed{i}") for i in range(RING)]
        w_hi_ready, w_lo_ready = sem("w_hi_ready"), sem("w_lo_ready")
        w_used = sem("w_used")
        turned = sem("turned")
        res_ready = sem("res_ready")
        a_hi_ready, a_ready = sem("a_hi_ready"), sem("a_ready")
        sq_ready, sum_ready = sem("sq_ready"), sem("sum_ready")
        var_ready, root_ready = sem("var_ready"), sem("root_ready")
        diag_ready, spread_ready, inv_ready = sem("diag_ready"), sem("spread_ready"), sem("inv_ready")
        vec_step, act_step = sem("vec_step"), sem("act_step")
        const_ready = sem("const_ready")
        RS = [0, 3, 4, 9, 10, 15, 16]
        RS_KEYS, RS_Q, RS_RET, RS_SSD = 1, 2, 5, 11

        def sum_bank(v):
            return 3 if v % 2 else 7


        def split_hi(act, s, it=None, ds=0):
            act.wait_ge(w_landed[s % RING], val(16 * (s // RING + 1), it, 16 * ds // RING))
            if s >= RING:
                act.wait_ge(w_used, val(s - RING + 1, it, ds))
            act.activation(w_hi[:, s % RING], w_raw[:, s % RING], ACT.Copy).then_inc(w_hi_ready, 1)

        def split_lo(dve, s, it=None, ds=0):
            dve.wait_ge(w_hi_ready, val(s + 1, it, ds))
            dve.tensor_tensor(w_lo[:, s % RING], w_raw[:, s % RING], w_hi[:, s % RING].bitcast(F32),
                              ALU.subtract).then_inc(w_lo_ready, 1)

        def slab_ready(pe, s, it=None, ds=0):
            pe.wait_ge(w_lo_ready, val(s + 1, it, ds))

        def mm3(pe, o, wh, wl, xh, xl, start, stop, shared=False):
            pe.matmul(o, wh, xh, start=start, stop=False, skip_group_check=shared)
            pe.matmul(o, wh, xl, start=False, stop=False, skip_group_check=shared)
            return pe.matmul(o, wl, xh, start=False, stop=stop, skip_group_check=shared)

        def slab_gemm(pe, s, o, hi, lo, it=None, ds=0, first=True, last=True, each=None):
            slab_ready(pe, s, it, ds)
            for k in range(NT):
                if each:
                    each(k)
                t = slice(k * P, (k + 1) * P)
                mm = mm3(pe, o, w_hi[:, s % RING, t], w_lo[:, s % RING, t], hi[:, k], lo[:, k],
                         first and k == 0, last and k == NT - 1)
            mm.then_inc(w_used, 1)

        def down_slab(pe, s, hi, lo, first, last, it=None, ds=0):
            slab_ready(pe, s, it, ds)
            for m in range(NT):
                t = slice(m * P, (m + 1) * P)
                o = ps[:, m // 2, (m % 2) * SEQ:(m % 2 + 1) * SEQ]
                mm = mm3(pe, o, w_hi[:, s % RING, t], w_lo[:, s % RING, t], hi, lo,
                         first and m % 2 == 0, last, shared=True)
            mm.then_inc(w_used, 1)

        def sum_squares(pe, v, k):
            pe.wait_ge(sq_ready, NT * v + k + 1)
            for b in range(NB):
                mm = pe.matmul(ps[:, sum_bank(v), b:b + 1], sq[:, k, b * P:(b + 1) * P], ones[:, 0:1],
                               start=(k == 0 and b == 0), stop=(k == NT - 1), skip_group_check=True)
            if k == NT - 1:
                mm.then_inc(sum_ready, 1)

        def operand_and_sums(pe, v):
            def each(k):
                pe.wait_ge(a_ready, NT * v + k + 1)
                sum_squares(pe, v, k)
            return each

        def spread_inv(pe, v):
            pe.wait_ge(diag_ready, v + 1)
            pe.matmul(ps[:, sum_bank(v), SEQ:2 * SEQ], ones, diag[:, 0:2].rearrange("p b t -> p (b t)"),
                      start=True, stop=True).then_inc(spread_ready, 1)

        def act_root(act, r, n, it=None):
            act.wait_ge(var_ready, val(r + 1, it, 1))
            act.activation(rs_root[:, 0:n], rs_var[:, 0:n], ACT.Sqrt).then_inc(root_ready, 1)

        def rsqrt(dve, step, r, n, o, it=None):
            dve.wait_ge(root_ready, val(r + 1, it, 1))
            step(dve.reciprocal(rs_y[:, 0:n], rs_root[:, 0:n]))
            step(dve.scalar_tensor_tensor(out=rs_t[:, 0:n], in0=rs_y[:, 0:n], scalar=-0.5, in1=rs_y[:, 0:n],
                                          op0=ALU.mult, op1=ALU.mult))
            step(dve.tensor_tensor(rs_t[:, 0:n], rs_t[:, 0:n], rs_var[:, 0:n], ALU.mult))
            step(dve.scalar_tensor_tensor(out=o, in0=rs_t[:, 0:n], scalar=1.5, in1=rs_y[:, 0:n],
                                          op0=ALU.add, op1=ALU.mult))

        def load_root_table(act, v):
            act.activation(table_probe[:, v:v + 1], ones[:, 0:1], ACT.Sqrt).then_inc(act_step, 1)

        def act_inv(act, v):
            act_root(act, RS[v], NB)
            act.wait_ge(spread_ready, v + 1)
            act.activation(inv[:, :], ps[:, sum_bank(v), SEQ:2 * SEQ], ACT.Copy).then_inc(inv_ready, 1)

        def vec_inv(dve, step, v, eps):
            dve.wait_ge(sum_ready, v + 1)
            dve.tensor_scalar(rs_var[:, 0:NB], ps[:, sum_bank(v), 0:NB], 1.0 / DM, eps, ALU.mult, ALU.add).then_inc(var_ready, 1)
            rsqrt(dve, step, RS[v], NB, inv_tok[:, :])
            step(dve.tensor_scalar(diag[:, 0], ident, inv_tok[:, 0:1], None, ALU.mult))
            dve.tensor_scalar(diag[:, 1], ident, inv_tok[:, 1:2], None, ALU.mult).then_inc(diag_ready, 1)

        def act_prep(act, v, m, g):
            act.wait_ge(res_ready, NT * v + m + 1)
            act.activation(a_hi[:, m], res[:, m], ACT.Copy, scale=pcol(g, m)).then_inc(a_hi_ready, 1)
            square(act, v, m)

        def square(act, v, m):
            act.wait_ge(res_ready, NT * v + m + 1)
            act.activation(sq[:, m], res[:, m], ACT.Square).then_inc(sq_ready, 1)

        def vec_prep(dve, v, m, g):
            dve.wait_ge(a_hi_ready, NT * v + m + 1)
            dve.scalar_tensor_tensor(out=a_lo[:, m], in0=res[:, m], scalar=pcol(g, m), in1=a_hi[:, m].bitcast(F32),
                                     op0=ALU.mult, op1=ALU.subtract).then_inc(a_ready, 1)

        def hi_ahead(act, s, it=None, ds=0):
            if s < SLABS:
                split_hi(act, s, it, ds)

        def lo_ahead(dve, s, it=None, ds=0):
            if s < SLABS:
                split_lo(dve, s, it, ds)

        def out_pe(pe, s0, two, hi, lo, taken, base, each=(None, None)):
            for m in range(NT):
                if m >= 4:
                    pe.wait_ge(taken, base + m - 3)
                o = ps[:, 4 + (m + 2) % 4, 0:SEQ]
                if two:
                    slab_gemm(pe, s0 + 2 * m, o, hi, lo, last=False, each=None if m else each[0])
                    slab_gemm(pe, s0 + 2 * m + 1, o, hi[:, NT:2 * NT], lo[:, NT:2 * NT], first=False, each=None if m else each[1])
                else:
                    slab_gemm(pe, s0 + m, o, hi, lo, each=None if m else each[0])

        def out_act(act, s0, per, v, g):
            load_root_table(act, v)
            for m in range(NT):
                for s in range(s0 + per * m, s0 + per * (m + 1)):
                    hi_ahead(act, s + 3)
                act_prep(act, v, m, g)

        def out_vec(dve, s0, per, v, g):
            for m in range(NT):
                for s in range(s0 + per * m, s0 + per * (m + 1)):
                    lo_ahead(dve, s + 3)
                dve.wait_ge(w_used, s0 + per * (m + 1))
                dve.tensor_tensor(res[:, m], res[:, m], ps[:, 4 + (m + 2) % 4, 0:SEQ], ALU.add).then_inc(res_ready, 1)
                if m:
                    vec_prep(dve, v, m - 1, g)
            vec_prep(dve, v, NT - 1, g)

        ADA_PARTS = 4
        top[0] = ARENA - 2 * DM - ADA_PARTS * ADA_TILES
        ada_raw, cond_row, ada_part = area(DM), area(DM), area(ADA_TILES, ADA_PARTS)
        cond_in, cond_ready, mod_ready = sem("cond_in"), sem("cond_ready"), sem("mod_ready")
        ada_landed, pool_step = sem("ada_landed"), sem("pool_step")

        def modulation_pool(pool, step):
            pool.wait_ge(cond_ready, 1)
            pool.dma_start(ada_raw, ada[0]).then_inc(ada_landed, 16)

            def dot(i, it=None):
                pool.wait_ge(ada_landed, val(16 * (i + 1), it, 16))
                step(pool.tensor_tensor(ada_raw, ada_raw, cond_row, ALU.mult))
                n = DM // 2
                while n > ADA_PARTS:
                    step(pool.tensor_tensor(ada_raw[:, 0:n], ada_raw[:, 0:n], ada_raw[:, n:2 * n], ALU.add))
                    n //= 2
                o = ada_part[:, i] if it is None else ada_part[:, bass.ds(it, 1)].rearrange("p a n -> p (a n)")
                step(pool.tensor_tensor(o, ada_raw[:, 0:n], ada_raw[:, n:2 * n], ALU.add))

            with pool.Fori(0, ADA_TILES - 1) as it:
                step.enter(it, 9)
                dot(0, it)
                pool.dma_start(ada_raw, ada[bass.ds(it + 1, 1)].rearrange("a p n -> (a p) n")).then_inc(ada_landed, 16)
            step.leave(ADA_TILES - 1)
            dot(ADA_TILES - 1)
            for n in (2, 1):
                step(pool.tensor_tensor(ada_part[:, :, 0:n], ada_part[:, :, 0:n], ada_part[:, :, n:2 * n], ALU.add))
            pool.tensor_tensor(mod[:, :], ada_part[:, :, 0], pcol("b_ada", n=ADA_TILES), ALU.add).then_inc(mod_ready, 1)

        top[0] = 0
        x_tok = area(NB, DM)
        top[0] = 0
        q_f = area(HEADS_A, SEQ)
        c_f, kw_f, qi_f = area(SEQ), area(SEQ), area(4, SEQ)
        k_n, ki_n, ki_dup, c_tok = area(SEQ), area(SEQ), area(SEQ), area(NB, LAT)
        key_gain = area(2)
        rel = area(2, 512)
        w_idx = area(NB, HEADS_A)
        score, work, pick = area(SEEN), area(SEEN), area(SEEN)
        best = area(NB, 8)
        logit, prob, prob_t = area(2, SEEN), area(2, SEEN), area(2, SEEN)
        peak, low, mass, share = area(2, 2), area(2, 2), area(2, 2), area(2, 2)
        q_scale = area(NB, HEADS_A)
        q_part = [slice(0, P), slice(P, SEEN)]
        best_ready, replaced = sem("best_ready"), sem("replaced")
        a_out_f = sem("a_out_f")
        key_sq, key_sum = sem("key_sq"), sem("key_sum")
        q_sq, q_sum = sem("q_sq"), sem("q_sum")
        key_diag, key_spread, key_norm, dup_done, dup_ready = (sem(n) for n in ("key_diag", "key_spread", "key_norm", "dup_done", "dup_ready"))
        c_turned, c_tok_ready = sem("c_turned"), sem("c_tok_ready")
        idx_ready, rel_ready, rel_used = sem("idx_ready"), sem("rel_ready"), sem("rel_used")
        logit_ready, logit_used, low_ready = sem("logit_ready"), sem("logit_used"), sem("low_ready")
        exp_ready, prob_ready, prob_turned, prob_t_ready = sem("exp_ready"), sem("prob_ready"), sem("prob_turned"), sem("prob_t_ready")
        o_ready, o_hi_ready, o_lo_ready = sem("o_ready"), sem("o_hi_ready"), sem("o_lo_ready")

        IDX = [(1, [0, 2]), (1, [1, 3]), (1, [4, 6]), (1, [5, 7]), (0, [0, 2, 4, 6]), (0, [1, 3, 5, 7])]

        def attention_pe(pe):
            pe.wait_ge(small_in, 16)
            pe.wait_ge(x_in, 16)
            for m in range(NT):
                for b in range(NB):
                    mm = pe.transpose(ps[:, m // 2, (m % 2) * SEQ + b * P:(m % 2) * SEQ + (b + 1) * P],
                                      x_tok[:, b, m * P:(m + 1) * P], ident)
                if m % 2:
                    mm.then_inc(turned, 1)
            pe.wait_ge(res_ready, NT)
            slab_gemm(pe, 0, ps[:, 0, 0:SEQ], a_hi, a_lo, each=operand_and_sums(pe, 0))
            slab_gemm(pe, 1, ps[:, 1, 0:SEQ], a_hi, a_lo)
            spread_inv(pe, 0)
            for s in range(2, 6):
                if s >= 4:
                    pe.wait_ge(a_out_f, s - 3)
                slab_gemm(pe, s, ps[:, s % 4, 0:SEQ], a_hi, a_lo)
            def key_sums(n):
                pe.wait_ge(key_sq, n + 1)
                for b in range(NB):
                    t = slice(b * P, (b + 1) * P)
                    if n == 0:
                        mm = pe.matmul(ps[:, 6, b:b + 1], sq[:, 0, t], ones[:, 0:1], start=True, stop=True)
                    elif n == 1:
                        pe.matmul(ps[:, 6, 2 + b:3 + b], sq[0:IDX_DIM, 1, t], ones[0:IDX_DIM, 0:1], start=True, stop=True)
                        mm = pe.matmul(ps[:, 5, 8 * b:8 + 8 * b], kw_f[64:72, t], con[64:72, CC["ident"] + 64:CC["ident"] + 72],
                                       start=True, stop=True)
                    else:
                        h = 2 * (n - 2)
                        mm = pe.matmul(ps[:, 6, 4 + 8 * b + h:6 + 8 * b + h], sq[:, n, t], const("halves", 2), start=True, stop=True)
                return mm
            for n in range(6):
                mm = key_sums(n)
            mm.then_inc(key_sum, 1)
            pe.wait_ge(a_out_f, 1)
            for b in range(NB):
                mm = pe.transpose(ps[:, 7, b * P:(b + 1) * P], c_f[:, b * P:(b + 1) * P], ident)
            mm.then_inc(c_turned, 1)

            def q_slab(h):
                s = 6 + h
                pe.wait_ge(a_out_f, s - 3)
                slab_gemm(pe, s, ps[:, s % 4, 0:SEQ], a_hi, a_lo)

            def q_sums(h):
                pe.wait_ge(q_sq, h + 1)
                for b in range(NB):
                    mm = pe.matmul(ps[:, 6, 64 + 8 * b + h:65 + 8 * b + h], sq[:, h, b * P:(b + 1) * P], ones[:, 0:1],
                                   start=True, stop=True)
                if h == HEADS_A - 1:
                    mm.then_inc(q_sum, 1)

            def index_batch(n):
                b, heads = IDX[n]
                if n >= 2:
                    pe.wait_ge(rel_ready, n - 1)
                w = 512 // len(heads)
                for i, h in enumerate(heads):
                    r = slice(64 * (h % 2), 64 * (h % 2) + 64)
                    mm = pe.matmul(ps[:, 4 + n % 2, i * w:(i + 1) * w], qi_f[r, h // 2, b * P:(b + 1) * P],
                                   ki_dup[r, 0:w], start=True, stop=True)
                mm.then_inc(idx_ready, 1)

            q_slab(0)
            pe.wait_ge(key_diag, 1)
            pe.matmul(ps[:, 5, :], ones, diag[:, :, :].rearrange("p b t -> p (b t)"), start=True, stop=True).then_inc(key_spread, 1)
            q_slab(1)
            pe.wait_ge(key_norm, 1)
            pe.matmul(ps[:, 4, 0:SEQ], const("dup", P, IDX_DIM), ki_n[0:IDX_DIM, :], start=True, stop=True).then_inc(dup_done, 1)
            pe.wait_ge(dup_ready, 1)
            for n in range(6):
                index_batch(n)
                if n < 5:
                    q_slab(2 + n)
            q_slab(7)
            pe.wait_ge(w_used, 6)
            for h in range(HEADS_A):
                q_sums(h)
            def logits(h):
                if h >= 2:
                    pe.wait_ge(logit_used, 2 * h - 2)
                pe.matmul(ps[:, h % 2, 0:P], q_f[:, h, 0:P], k_n[:, 0:P], start=True, stop=True)
                pe.matmul(ps[:, h % 2, P:SEEN], q_f[:, h, P:SEQ], k_n[:, :], start=True, stop=True).then_inc(logit_ready, 1)

            def turn(h):
                pe.wait_ge(prob_ready, h + 1)
                if h >= 2:
                    pe.wait_ge(prob_t_ready, h - 1)
                for i, c in enumerate([0, 1, 2]):
                    mm = pe.transpose(ps[:, 2 + h % 2, i * P:(i + 1) * P], prob[:, h % 2, c * P:(c + 1) * P], ident)
                mm.then_inc(prob_turned, 1)

            def weigh(h):
                pe.wait_ge(prob_t_ready, h + 1)
                if h >= 2:
                    pe.wait_ge(o_lo_ready, h - 1)
                o = ps[:, 4 + h % 2, :]
                pe.matmul(o[:, 0:P], c_tok[:, 0], prob_t[:, h % 2, 0:P], start=True, stop=True)
                pe.matmul(o[:, P:SEQ], c_tok[:, 0], prob_t[:, h % 2, P:SEQ], start=True, stop=False)
                pe.matmul(o[:, P:SEQ], c_tok[:, 1], prob_t[:, h % 2, SEQ:SEEN], start=False, stop=True).then_inc(o_ready, 1)

            pe.wait_ge(a_out_f, 14)
            pe.wait_ge(c_tok_ready, 1)
            for h in range(HEADS_A + 2):
                if h < HEADS_A:
                    logits(h)
                if 0 <= h - 1 < HEADS_A:
                    turn(h - 1)
                if 0 <= h - 2 < HEADS_A:
                    weigh(h - 2)
            pe.wait_ge(o_lo_ready, HEADS_A)
            out_pe(pe, S_AOUT, False, b_hi, b_lo, res_ready, NT)

        def attention_act(act):
            split_hi(act, 0)
            act.wait_ge(par_in, 16)
            act.wait_ge(small_in, 16)
            load_root_table(act, 0)
            for m in range(NT):
                act_prep(act, 0, m, "mix_g0")
            for s in range(1, 4):
                split_hi(act, s)
            act_root(act, RS[0], NB)
            split_hi(act, 4)
            act.wait_ge(spread_ready, 1)
            act.activation(inv[:, :], ps[:, 7, SEQ:2 * SEQ], ACT.Copy).then_inc(inv_ready, 1)
            for n in range(6):
                split_hi(act, 5 + n)
                act.wait_ge(a_out_f, n + 1)
                if n == 1:
                    act.activation(sq[0:IDX_DIM, 1], kw_f[0:IDX_DIM, :], ACT.Square).then_inc(key_sq, 1)
                else:
                    act.activation(sq[:, n], c_f if n == 0 else qi_f[:, n - 2], ACT.Square).then_inc(key_sq, 1)
            act_root(act, RS_KEYS, 20)
            act.wait_ge(c_turned, 1)
            act.activation(c_tok[:, :, :].rearrange("p b d -> p (b d)"), ps[:, 7, 0:SEQ], ACT.Copy).then_inc(c_tok_ready, 1)

            def q_squares(h):
                act.wait_ge(a_out_f, 7 + h)
                if h == 0:
                    act.wait_ge(key_sum, 1)
                act.activation(sq[:, h], q_f[:, h], ACT.Square).then_inc(q_sq, 1)

            def relu(n):
                act.wait_ge(idx_ready, n + 1)
                if n >= 2:
                    act.wait_ge(rel_used, n - 1)
                act.activation(rel[:, n % 2], ps[:, 4 + n % 2, :], ACT.Relu).then_inc(rel_ready, 1)

            split_hi(act, 11)
            act.wait_ge(dup_done, 1)
            act.activation(ki_dup, ps[:, 4, 0:SEQ], ACT.Copy).then_inc(dup_ready, 1)
            for n in range(6):
                if n < 5:
                    split_hi(act, 12 + n)
                relu(n)
            for h in range(HEADS_A):
                q_squares(h)
            act_root(act, RS_Q, 2 * HEADS_A)

            def exps(h):
                act.wait_ge(low_ready, h + 1)
                if h >= 2:
                    act.wait_ge(prob_turned, h - 1)
                for b in range(NB):
                    act.activation(prob[:, h % 2, q_part[b]], logit[:, h % 2, q_part[b]], ACT.Exp, bias=low[:, h % 2, b:b + 1],
                                   scale=q_scale[:, b, h:h + 1], accum_out=mass[:, h % 2, b:b + 1]).then_inc(exp_ready, 1)

            def turned_copy(h):
                act.wait_ge(prob_turned, h + 1)
                if h >= 2:
                    act.wait_ge(o_ready, h - 1)
                act.activation(prob_t[:, h % 2], ps[:, 2 + h % 2, 0:SEEN], ACT.Copy).then_inc(prob_t_ready, 1)

            def out_hi(h):
                act.wait_ge(o_ready, h + 1)
                act.activation(b_hi[:, h], ps[:, 4 + h % 2, 0:SEQ], ACT.Copy).then_inc(o_hi_ready, 1)

            for h in range(HEADS_A + 2):
                if h < HEADS_A:
                    exps(h)
                if 0 <= h - 1 < HEADS_A:
                    turned_copy(h - 1)
                if 0 <= h - 2 < HEADS_A:
                    out_hi(h - 2)
            out_act(act, S_AOUT, 1, 1, "ffn_g0")
            act.wait_ge(tables_in, 16)
            act.activation(tri[:, :], const("tri", SEEN), ACT.Copy).then_inc(const_ready, 1)
            act.activation(ident_b[:, :], ident, ACT.Copy).then_inc(const_ready, 1)
            act.wait_ge(cond_in, 16)
            act.activation(cond_row, cond_row, ACT.Silu).then_inc(cond_ready, 1)

        def attention_vec(dve, step):
            dve.wait_ge(small_in, 16)
            dve.wait_ge(par_in, 16)
            step(dve.tensor_tensor(key_gain[:, 0:1], pcol("q_g"), pcol("k_g"), ALU.mult))
            step(dve.tensor_tensor(key_gain[:, 1:2], pcol("iq_g"), pcol("ik_g"), ALU.mult))
            for j in range(NT // 2):
                dve.wait_ge(turned, j + 1)
                dve.tensor_copy(res[:, 2 * j:2 * j + 2].rearrange("p m t -> p (m t)"), ps[:, j, :]).then_inc(res_ready, 2)
                if j:
                    vec_prep(dve, 0, 2 * j - 2, "mix_g0")
                    vec_prep(dve, 0, 2 * j - 1, "mix_g0")
                if j == 0:
                    split_lo(dve, 0)
            vec_prep(dve, 0, NT - 2, "mix_g0")
            vec_prep(dve, 0, NT - 1, "mix_g0")
            for s in range(1, 4):
                split_lo(dve, s)
            vec_inv(dve, step, 0, EPS_A)
            split_lo(dve, 4)
            dve.wait_ge(inv_ready, 1)
            tiles = [c_f, kw_f, *(qi_f[:, i] for i in range(4)), *(q_f[:, h] for h in range(HEADS_A))]

            def evict(s):
                dve.wait_ge(w_used, s + 1)
                dve.tensor_tensor(tiles[s], ps[:, s % 4, 0:SEQ], inv[:, :], ALU.mult).then_inc(a_out_f, 1)

            for s in range(6):
                split_lo(dve, 5 + s)
                evict(s)
            dve.wait_ge(key_sum, 1)
            step(dve.tensor_scalar(rs_var[:, 0:2], ps[:, 6, 0:2], 1.0 / LAT, EPS_A, ALU.mult, ALU.add))
            dve.tensor_scalar(rs_var[:, 2:20], ps[:, 6, 2:20], 1.0 / IDX_DIM, EPS_A, ALU.mult, ALU.add).then_inc(var_ready, 1)
            rsqrt(dve, step, RS_KEYS, 20, rs_root[:, 0:20])
            step(dve.scalar_tensor_tensor(
                out=w_idx[:, :, :].rearrange("p b h -> p (b h)"), in0=rs_root[:, 4:20], scalar=float((HEADS_A * IDX_DIM) ** -0.5),
                in1=ps[:, 5, 0:16], op0=ALU.mult, op1=ALU.mult))
            for i in range(3):
                step(dve.tensor_scalar(diag[:, i], ident, rs_root[:, i:i + 1], None, ALU.mult))
            dve.tensor_scalar(diag[:, 3], ident, rs_root[:, 3:4], None, ALU.mult).then_inc(key_diag, 1)
            dve.wait_ge(key_spread, 1)
            step(dve.scalar_tensor_tensor(out=k_n, in0=c_f, scalar=key_gain[:, 0:1], in1=ps[:, 5, 0:SEQ], op0=ALU.mult, op1=ALU.mult))
            dve.scalar_tensor_tensor(out=ki_n[0:IDX_DIM, :], in0=kw_f[0:IDX_DIM, :], scalar=key_gain[0:IDX_DIM, 1:2],
                                     in1=ps[0:IDX_DIM, 5, SEQ:512], op0=ALU.mult, op1=ALU.mult).then_inc(key_norm, 1)
            split_lo(dve, 11)
            evict(6)
            evict(7)
            dve.wait_ge(tables_in, 16)
            for n, (b, heads) in enumerate(IDX):
                if n < 5:
                    split_lo(dve, 12 + n)
                if n < 4:
                    evict(8 + n)
                dve.wait_ge(rel_ready, n + 1)
                w = 512 // len(heads)
                for i, h in enumerate(heads):
                    ins = dve.scalar_tensor_tensor(
                        out=score[:, q_part[b]], in0=rel[:, n % 2, i * w:(i + 1) * w], scalar=w_idx[:, b, h:h + 1],
                        in1=const("admit", SEEN)[:, q_part[b]] if h == 0 else score[:, q_part[b]], op0=ALU.mult, op1=ALU.add)
                    if i < len(heads) - 1:
                        step(ins)
                    else:
                        ins.then_inc(rel_used, 1)
                        dve.wait_ge(rel_used, n + 1)
            evict(12)
            evict(13)
            for r in range(TOPK // 8):
                src = score if r == 0 else work
                for b in range(NB):
                    if r:
                        dve.wait_ge(replaced, NB * r + b - 1)
                    dve.max(best[:, b], src[:, q_part[b]]).then_inc(best_ready, 1)
                for b in range(NB):
                    dve.wait_ge(best_ready, NB * r + b + 1)
                    dve.match_replace(work[:, q_part[b]], best[:, b], src[:, q_part[b]], TAKEN).then_inc(replaced, 1)
            dve.wait_ge(replaced, NB * TOPK // 8)
            step(dve.tensor_scalar(pick, work, (MASKED + TAKEN) / 2, -1e30, ALU.is_gt, ALU.mult))
            dve.wait_ge(q_sum, 1)
            dve.tensor_scalar(rs_var[:, 0:16], ps[:, 6, 64:80], 1.0 / LAT, EPS_A, ALU.mult, ALU.add).then_inc(var_ready, 1)
            rsqrt(dve, step, RS_Q, 16, rs_root[:, 0:16])
            step(dve.tensor_scalar(q_scale[:, :, :].rearrange("p b h -> p (b h)"), rs_root[:, 0:16], float(LAT ** -0.5), None, ALU.mult))

            def maxima(h):
                dve.wait_ge(logit_ready, h + 1)
                for b in range(NB):
                    if h >= 2:
                        dve.wait_ge(exp_ready, 2 * h - 2)
                    dve.tensor_tensor_reduce(logit[:, h % 2, q_part[b]], ps[:, h % 2, q_part[b]], pick[:, q_part[b]], 1.0, -3.4e38,
                                             ALU.add, ALU.max, peak[:, h % 2, b:b + 1]).then_inc(logit_used, 1)
                dve.wait_ge(logit_used, 2 * h + 2)
                dve.scalar_tensor_tensor(out=low[:, h % 2], in0=peak[:, h % 2], scalar=-1.0, in1=q_scale[:, :, h],
                                         op0=ALU.mult, op1=ALU.mult).then_inc(low_ready, 1)

            def shares(h):
                dve.wait_ge(exp_ready, 2 * h + 2)
                step(dve.reciprocal(share[:, h % 2], mass[:, h % 2]))
                step(dve.tensor_scalar(prob[:, h % 2, q_part[0]], prob[:, h % 2, q_part[0]], share[:, h % 2, 0:1], None, ALU.mult))
                dve.tensor_scalar(prob[:, h % 2, q_part[1]], prob[:, h % 2, q_part[1]], share[:, h % 2, 1:2], None, ALU.mult).then_inc(prob_ready, 1)

            def out_lo(h):
                dve.wait_ge(o_hi_ready, h + 1)
                dve.tensor_tensor(b_lo[:, h], ps[:, 4 + h % 2, 0:SEQ], b_hi[:, h].bitcast(F32), ALU.subtract).then_inc(o_lo_ready, 1)

            for h in range(HEADS_A + 2):
                if h < HEADS_A:
                    maxima(h)
                    shares(h)
                if 0 <= h - 2 < HEADS_A:
                    out_lo(h - 2)
            out_vec(dve, S_AOUT, 1, 1, "ffn_g0")

        UNROLL = 4
        LATER = (FF_PAIRS - 4) // UNROLL
        assert (FF_PAIRS - 2) % UNROLL == 0
        top[0] = 0
        up, conv = area(2, 2, SEQ), area(2, 2, SEQ)
        gate, glu = area(2, SEQ), area(2, SEQ)
        ffn_sems = [{n: sem(f"ffn{i}_{n}") for n in ("up_out", "tap", "conv", "gate", "glu", "hi", "operand")} for i in range(2)]

        def ffn_pe(pe, L, s0, v):
            f = ffn_sems[L]

            def up_pair(p, s, it=None, ds=0, each=None):
                for half in range(2):
                    if p >= 2:
                        pe.wait_ge(f["up_out"], val(2 * (p - 2) + half + 1, it, 2 * UNROLL))
                    slab_gemm(pe, s + half, ps[:, 6 - 2 * (p % 2) + half, 0:SEQ], a_hi, a_lo, it, ds, each=each if half == 0 else None)

            def down(p, s, it=None, ds=0):
                pe.wait_ge(f["operand"], val(p + 1, it, UNROLL))
                down_slab(pe, s, b_hi[:, p % 2], b_lo[:, p % 2], p == 0, p == FF_PAIRS - 1, it, ds)

            up_pair(0, s0, each=operand_and_sums(pe, v))
            spread_inv(pe, v)
            up_pair(1, s0 + 2)
            pe.wait_ge(inv_ready, v + 1)
            down(0, s0 + 4)
            with pe.Fori(0, (FF_PAIRS - 2) // UNROLL) as it:
                for u in range(UNROLL):
                    up_pair(2 + u, s0 + 5 + 3 * u, it, 3 * UNROLL)
                    down(1 + u, s0 + 7 + 3 * u, it, 3 * UNROLL)
            down(FF_PAIRS - 1, s0 + 3 * FF_PAIRS - 1)

        def ffn_act(act, L, s0, v, next_gain):
            f = ffn_sems[L]

            def prm(p, j, it):
                c = COL[f"ffn{L}"] + 8 * p + j
                return par[:, c:c + 1] if it is None else par[:, bass.ds(it * 8 * UNROLL + c, 1)]

            def tap(p, half, it=None):
                act.wait_ge(f["up_out"], val(2 * p + half + 1, it, 2 * UNROLL))
                if p >= 2:
                    act.wait_ge(f["glu"], val(p - 1, it, UNROLL))
                act.activation(conv[:, p % 2, half], up[:, p % 2, half], ACT.Identity, bias=prm(p, 6 + half, it),
                               scale=prm(p, 3 * half + 2, it)).then_inc(f["tap"], 1)

            def silu(p, it=None):
                act.wait_ge(f["conv"], val(2 * p + 1, it, 2 * UNROLL))
                act.activation(gate[:, p % 2], conv[:, p % 2, 0], ACT.Silu).then_inc(f["gate"], 1)

            def hi(p, done, it=None):
                act.wait_ge(f["glu"], val(p + 1, it, UNROLL))
                if p >= 2:
                    act.wait_ge(w_used, val(done, it, 3 * UNROLL))
                act.activation(b_hi[:, p % 2], glu[:, p % 2], ACT.Copy).then_inc(f["hi"], 1)

            def pair(p, s, it=None):
                ds = 0 if it is None else 3 * UNROLL
                hi_ahead(act, s + 3, it, ds)
                if p == 0:
                    act_inv(act, v)
                hi_ahead(act, s + 4, it, ds)
                tap(p, 0, it)
                if p:
                    hi_ahead(act, s + 5, it, ds)
                tap(p, 1, it)
                silu(p, it)
                hi(p, s - 6 + 3, it)

            pair(0, s0)
            pair(1, s0 + 2)
            with act.Fori(0, LATER) as it:
                for u in range(UNROLL):
                    pair(2 + u, s0 + 5 + 3 * u, it)
            for p in range(2 + UNROLL * LATER, FF_PAIRS):
                pair(p, s0 + 3 * p - 1)
            hi_ahead(act, s0 + 3 * FF_PAIRS - 1 + 3)
            load_root_table(act, v + 1)
            for m in range(NT):
                if next_gain:
                    act_prep(act, v + 1, m, next_gain)
                else:
                    square(act, v + 1, m)

        def ffn_vec(dve, step, L, s0, v, next_gain):
            f = ffn_sems[L]

            def prm(p, j, it):
                c = COL[f"ffn{L}"] + 8 * p + j
                return par[:, c:c + 1] if it is None else par[:, bass.ds(it * 8 * UNROLL + c, 1)]

            def evict(p, half, s, it, ds):
                dve.wait_ge(w_used, val(s + half + 1, it, ds))
                dve.tensor_tensor(up[:, p % 2, half], ps[:, 6 - 2 * (p % 2) + half, 0:SEQ], inv[:, :], ALU.mult).then_inc(f["up_out"], 1)

            def taps(p, half, it):
                dve.wait_ge(f["tap"], val(2 * p + half + 1, it, 2 * UNROLL))
                t = conv[:, p % 2, half]
                u = up[:, p % 2, half]
                step(dve.scalar_tensor_tensor(out=t[:, 1:SEQ], in0=u[:, 0:SEQ - 1], scalar=prm(p, 3 * half + 1, it),
                                              in1=t[:, 1:SEQ], op0=ALU.mult, op1=ALU.add))
                dve.scalar_tensor_tensor(out=t[:, 2:SEQ], in0=u[:, 0:SEQ - 2], scalar=prm(p, 3 * half, it),
                                         in1=t[:, 2:SEQ], op0=ALU.mult, op1=ALU.add).then_inc(f["conv"], 1)

            def pair(p, s, it=None):
                ds = 0 if it is None else 3 * UNROLL
                lo_ahead(dve, s + 3, it, ds)
                if p == 0:
                    vec_inv(dve, step, v, EPS_A)
                    dve.wait_ge(inv_ready, v + 1)
                evict(p, 0, s, it, ds)
                lo_ahead(dve, s + 4, it, ds)
                taps(p, 0, it)
                evict(p, 1, s, it, ds)
                taps(p, 1, it)
                dve.wait_ge(f["conv"], val(2 * p + 2, it, 2 * UNROLL))
                dve.wait_ge(f["gate"], val(p + 1, it, UNROLL))
                dve.tensor_tensor(glu[:, p % 2], gate[:, p % 2], conv[:, p % 2, 1], ALU.mult).then_inc(f["glu"], 1)
                if p:
                    lo_ahead(dve, s + 5, it, ds)
                dve.wait_ge(f["hi"], val(p + 1, it, UNROLL))
                dve.tensor_tensor(b_lo[:, p % 2], glu[:, p % 2], b_hi[:, p % 2].bitcast(F32), ALU.subtract).then_inc(f["operand"], 1)

            pair(0, s0)
            pair(1, s0 + 2)
            with dve.Fori(0, LATER) as it:
                step.enter(it, 2 * UNROLL)
                for u in range(UNROLL):
                    pair(2 + u, s0 + 5 + 3 * u, it)
            step.leave(LATER)
            for p in range(2 + UNROLL * LATER, FF_PAIRS):
                pair(p, s0 + 3 * p - 1)
            lo_ahead(dve, s0 + 3 * FF_PAIRS - 1 + 3)
            add_down(dve, s0 + 3 * FF_PAIRS, v + 1, next_gain)

        def add_down(dve, used, v, g):
            dve.wait_ge(w_used, used)
            for j in range(NT // 2):
                dve.tensor_tensor(res[:, 2 * j:2 * j + 2].rearrange("p m t -> p (m t)"), res[:, 2 * j:2 * j + 2].rearrange("p m t -> p (m t)"),
                                  ps[:, j, :], ALU.add).then_inc(res_ready, 2)
                if g and j:
                    vec_prep(dve, v, 2 * j - 2, g)
                    vec_prep(dve, v, 2 * j - 1, g)
            if g:
                vec_prep(dve, v, NT - 2, g)
                vec_prep(dve, v, NT - 1, g)

        HEAD = 12
        top[0] = 0
        cos_i, sin_i = area(SEQ), area(SEQ)
        q_rot, k_rot = area(2, SEQ), area(2, SEQ)
        v_tok = area(NB, 512)
        g_b = area(4, SEQ)
        decayed = area(SEEN)
        turn_t = area(4, SEQ)
        inv_r = area(SEQ)
        y_n, y_b = area(2, SEQ), area(4, SEQ)
        g_taken, ret_taken = sem("g_taken"), sem("ret_taken")
        rot_ready, qk_ready, decayed_ready, v_ready = (sem(n) for n in ("rot_ready", "qk_ready", "decayed_ready", "v_ready"))
        ret_ready, ret_sq, ret_sum, ret_diag, ret_spread, ret_inv = (sem(n) for n in ("ret_ready", "ret_sq", "ret_sum", "ret_diag", "ret_spread", "ret_inv"))
        g_silu, y_ready, y_hi, y_operand = sem("g_silu"), sem("y_ready"), sem("y_hi"), sem("y_operand")

        def retention_pe(pe):
            def v_slab(s, i, it):
                slab_ready(pe, s, it, HEAD)
                for kk in range(2):
                    k = 2 * i + kk
                    w = slice(kk * 512, (kk + 1) * 512)
                    for b in range(NB):
                        t = slice(b * P, (b + 1) * P)
                        mm = mm3(pe, ps[:, 4 + b, :], a_hi[:, k, t], a_lo[:, k, t], w_hi[:, s % RING, w], w_lo[:, s % RING, w],
                                 k == 0, k == NT - 1)
                mm.then_inc(w_used, 1)

            def scores(it):
                pe.wait_ge(rot_ready, val(2, it, 2))
                for b in range(NB):
                    for d in range(2):
                        mm = pe.matmul(ps[:, 7, b * SEQ:b * SEQ + SEQ - b * P], k_rot[:, d, b * P:(b + 1) * P], q_rot[:, d, b * P:SEQ],
                                       start=(d == 0), stop=(d == 1))
                mm.then_inc(qk_ready, 1)

            def weigh(it):
                pe.wait_ge(decayed_ready, val(1, it, 1))
                pe.wait_ge(v_ready, val(2, it, 2))
                for e in range(4):
                    o = ps[:, 4 + e // 2, (e % 2) * SEQ:(e % 2 + 1) * SEQ]
                    c = slice(e * P, (e + 1) * P)
                    pe.matmul(o[:, 0:P], v_tok[:, 0, c], decayed[:, 0:P], start=True, stop=True)
                    pe.matmul(o[:, P:SEQ], v_tok[:, 0, c], decayed[:, P:SEQ], start=True, stop=False)
                    pe.matmul(o[:, P:SEQ], v_tok[:, 1, c], decayed[:, SEQ:SEEN], start=False, stop=True).then_inc(ret_ready, 1)

            def sums(it):
                pe.wait_ge(ret_sq, val(2, it, 2))
                for b in range(NB):
                    for e in range(4):
                        mm = pe.matmul(ps[:, 7, 400 + b:401 + b], sq[:, e, b * P:(b + 1) * P], ones[:, 0:1], start=(e == 0), stop=(e == 3))
                mm.then_inc(ret_sum, 1)

            def head(it, s=S_B):
                for j in range(12):
                    own = s + j
                    if j == 0:
                        pe.wait_ge(g_taken, val(1, it, 4))
                    if j == 4:
                        pe.wait_ge(ret_taken, val(1, it, 4))
                    if 4 <= j < 8:
                        v_slab(own, j - 4, it)
                    else:
                        slab_gemm(pe, own, ps[:, j % 4, 0:SEQ], a_hi, a_lo, it, HEAD)
                    if j == 6:
                        scores(it)
                    if j == 8:
                        weigh(it)
                    if j == 9:
                        sums(it)
                pe.wait_ge(ret_diag, val(1, it, 1))
                pe.matmul(ps[:, 7, 0:SEQ], ones, diag[:, 2:4].rearrange("p b t -> p (b t)"), start=True, stop=True).then_inc(ret_spread, 1)

            for k in range(NT):
                sum_squares(pe, 2, k)
            spread_inv(pe, 2)
            pe.wait_ge(a_ready, NT * 3)
            with pe.Fori(0, HEADS_B) as it:
                head(it)

            def tile_of(n):
                def each(k):
                    pe.wait_ge(y_operand, n + k + 1)
                return each
            out_pe(pe, S_BOUT, True, b_hi, b_lo, res_ready, 3 * NT, (tile_of(0), tile_of(NT)))

        def retention_act(act):
            act_inv(act, 2)
            with act.Fori(0, HEADS_B) as it:
                def silu(n):
                    act.wait_ge(g_taken, val(2 + n, it, 4))
                    act.activation(g_b[:, n], g_b[:, n], ACT.Silu).then_inc(g_silu, 1)

                for j in range(12):
                    s = S_B + j
                    split_hi(act, s + 3, it, HEAD)
                    if j == 7:
                        act.wait_ge(w_used, val(s + 1, it, HEAD))
                        for b in range(NB):
                            act.activation(v_tok[:, b], ps[:, 4 + b, :], ACT.Copy, scale=inv_tok[:, b:b + 1]).then_inc(v_ready, 1)
                    if j == 9:
                        for i in range(2):
                            act.wait_ge(ret_ready, val(2 * i + 2, it, 4))
                            act.activation(sq[:, 2 * i:2 * i + 2].rearrange("p m t -> p (m t)"), ps[:, 4 + i, :], ACT.Square).then_inc(ret_sq, 1)
                    if j == 10:
                        act_root(act, RS_RET, NB, it)
                for n in range(4):
                    silu(n)
                act.wait_ge(ret_spread, val(1, it, 1))
                act.activation(inv_r, ps[:, 7, 0:SEQ], ACT.Copy).then_inc(ret_inv, 1)
                for e in range(4):
                    act.wait_ge(y_ready, val(e + 1, it, 4))
                    act.activation(b_hi[:, bass.ds(it * 4 + e, 1)].rearrange("p a t -> p (a t)"), y_b[:, e], ACT.Copy).then_inc(y_hi, 1)
            out_act(act, S_BOUT, 2, 3, "ffn_g1")

        def retention_vec(dve, step):
            vec_inv(dve, step, 2, EPS_A)
            dve.wait_ge(inv_ready, 3)
            dve.tensor_tensor(cos_i, const("cos", SEQ), inv[:, :], ALU.mult).then_inc(g_taken, 1)
            dve.tensor_tensor(sin_i, const("sin", SEQ), inv[:, :], ALU.mult).then_inc(ret_taken, 1)
            dve.wait_ge(ret_taken, 1)
            with dve.Fori(0, HEADS_B) as it:
                step.enter(it, 9)

                def rotary(o, bank, used):
                    dve.wait_ge(w_used, val(used, it, HEAD))
                    for n, (x_h, table) in enumerate([(0, cos_i), (1, sin_i), (0, sin_i), (1, cos_i)]):
                        ins = dve.tensor_tensor(turn_t[:, n], ps[:, bank + x_h, 0:SEQ], table, ALU.mult)
                    step(ins)
                    step(dve.tensor_tensor(o[:, 0], turn_t[:, 0], turn_t[:, 1], ALU.subtract))
                    dve.tensor_tensor(o[:, 1], turn_t[:, 2], turn_t[:, 3], ALU.add).then_inc(rot_ready, 1)

                for j in range(12):
                    s = S_B + j
                    split_lo(dve, s + 3, it, HEAD)
                    if j == 1:
                        rotary(q_rot, 0, s + 1)
                    if j == 3:
                        dve.wait_ge(rot_ready, val(1, it, 2))
                        rotary(k_rot, 2, s + 1)
                    if j == 7:
                        dve.wait_ge(qk_ready, val(1, it, 1))
                        dve.tensor_tensor(decayed, ps[:, 7, 0:SEEN], con[:, bass.ds(it * SEEN + CC["decay"], SEEN)],
                                          ALU.mult).then_inc(decayed_ready, 1)
                    if j == 10:
                        dve.wait_ge(ret_sum, val(1, it, 1))
                        dve.tensor_scalar(rs_var[:, 0:NB], ps[:, 7, 400:402], 1.0 / 512, EPS_A, ALU.mult, ALU.add).then_inc(var_ready, 1)
                        rsqrt(dve, step, RS_RET, NB, rs_root[:, 0:NB], it)
                        step(dve.tensor_scalar(diag[:, 2], ident, rs_root[:, 0:1], None, ALU.mult))
                        dve.tensor_scalar(diag[:, 3], ident, rs_root[:, 1:2], None, ALU.mult).then_inc(ret_diag, 1)
                    if j >= 8:
                        dve.wait_ge(w_used, val(s + 1, it, HEAD))
                        dve.tensor_tensor(g_b[:, j - 8], ps[:, j - 8, 0:SEQ], inv[:, :], ALU.mult).then_inc(g_taken, 1)
                dve.wait_ge(ret_inv, val(1, it, 1))

                def y_lo(e):
                    dve.wait_ge(y_hi, val(e + 1, it, 4))
                    o = bass.ds(it * 4 + e, 1)
                    dve.tensor_tensor(b_lo[:, o].rearrange("p a t -> p (a t)"), y_b[:, e],
                                      b_hi[:, o].bitcast(F32).rearrange("p a t -> p (a t)"), ALU.subtract).then_inc(y_operand, 1)

                for e in range(4):
                    dve.scalar_tensor_tensor(out=y_n[:, e % 2], in0=ps[:, 4 + e // 2, (e % 2) * SEQ:(e % 2 + 1) * SEQ],
                                             scalar=par[:, bass.ds(it * 4 + COL["out_g"] + e, 1)], in1=inv_r,
                                             op0=ALU.mult, op1=ALU.mult).then_inc(ret_taken, 1)
                    dve.wait_ge(ret_taken, val(2 + e, it, 4))
                    dve.wait_ge(g_silu, val(e + 1, it, 4))
                    dve.tensor_tensor(y_b[:, e], y_n[:, e % 2], g_b[:, e], ALU.mult).then_inc(y_ready, 1)
                    if e:
                        y_lo(e - 1)
                y_lo(3)
            step.leave(HEADS_B)
            out_vec(dve, S_BOUT, 2, 3, "ffn_g1")

        top[0] = ARENA - 4 * SEQ
        scaled, normed = area(2, SEQ), area(2, SEQ)
        scaled_ready, normed_ready = sem("scaled_ready"), sem("normed_ready")
        MOD = {4: ("mix_w", 0), 5: ("mlp_w", 3 * NT)}

        def mod_act(act, v):
            act.wait_ge(mod_ready, 1)
            for m in range(NT):
                n = NT * (v - 4) + m
                act.wait_ge(scaled_ready, n + 1)
                if m >= 2:
                    act.wait_ge(a_ready, NT * v + m - 1)
                act.activation(normed[:, m % 2], scaled[:, m % 2], ACT.Identity, bias=mod[:, MOD[v][1] + m:MOD[v][1] + m + 1],
                               scale=eff_scale[:, v - 4, m:m + 1]).then_inc(normed_ready, 1)
                act.wait_ge(normed_ready, n + 1)
                act.activation(a_hi[:, m], normed[:, m % 2], ACT.Copy).then_inc(a_hi_ready, 1)

        def mod_vec(dve, step, v):
            gain, col = MOD[v]
            dve.wait_ge(mod_ready, 1)
            step(dve.scalar_tensor_tensor(out=eff_scale[:, v - 4], in0=mod[:, col + NT:col + 2 * NT], scalar=1.0, in1=pcol(gain, n=NT),
                                          op0=ALU.add, op1=ALU.mult))
            vec_inv(dve, step, v, EPS_B)
            dve.wait_ge(inv_ready, v + 1)

            def low(m):
                dve.wait_ge(a_hi_ready, NT * v + m + 1)
                dve.tensor_tensor(a_lo[:, m], normed[:, m % 2], a_hi[:, m].bitcast(F32), ALU.subtract).then_inc(a_ready, 1)

            for m in range(NT):
                dve.tensor_tensor(scaled[:, m % 2], res[:, m], inv[:, :], ALU.mult).then_inc(scaled_ready, 1)
                if m:
                    low(m - 1)
            low(NT - 1)

        def ready(s, base):
            def wait_on(pe):
                def each(k):
                    pe.wait_ge(s, base + k + 1)
                return each
            return wait_on

        GRP = 12
        top[0] = 0
        u_f = area(NT, SEQ)
        cv = area(6, SEQ)
        z_s = area(4, SEQ)
        inv_s = area(SEQ)
        tail = top[0]
        x_tok2 = area(NB, 512)
        y_f = area(4, SEQ)
        c_flat = [t[:, :, :].rearrange("p m t -> p (m t)") for t in (c_hi, c_lo)]
        cum_hi, cum_lo = (t[0:SSD_HEADS, 0:SEEN] for t in c_flat)
        pick_h = c_flat[0][0:SSD_HEADS, DM:2 * DM].rearrange("p (h n) -> p h n", n=P)
        seen = area(2, SEEN)
        cb = area(SEEN)
        cum = area(SEEN)
        dt_f = area(SEQ)
        dt_tok, neg_cum = area(NB, GROUP_HEADS), area(NB, GROUP_HEADS)
        root_s = area(NB)
        neg_a = area(1)
        end = top[0]
        top[0] = tail + 2 * 512
        dt_x, dt_e, dt_z = area(SEQ), area(SEQ), area(SEQ)
        assert top[0] <= tail + 1024 + 4 * SEQ
        top[0] = tail
        gates = area(2 * NT, SEQ)
        top[0] = 0
        merged = area(2, SEQ)
        part = area(2, 2, SEQ)
        win = [cv[:, 0:2], cv[:, 2:4]]

        dt_x_ready, dt_e_ready, decay_a, dt_ready = sem("dt_x_ready"), sem("dt_e_ready"), sem("decay_a"), sem("dt_ready")
        tap_done, conv_done, act_done, z_done, u_done = (sem(n) for n in ("tap_done", "conv_done", "act_done", "z_done", "u_done"))
        cb_ready, cb_copied, own_ready, own_copied = sem("cb_ready"), sem("cb_copied"), sem("own_ready"), sem("own_copied")
        pick_ready, x_turned, x_tok_ready = sem("pick_ready"), sem("x_turned"), sem("x_tok_ready")
        cum_ready, exp_done, seen_ready, y_done = sem("cum_ready"), sem("exp_done"), sem("seen_ready"), sem("y_done")
        yz_ready, ysq_ready, ysum_ready, ydiag_ready, yspread_ready, inv_s_ready = (
            sem(n) for n in ("yz_ready", "ysq_ready", "ysum_ready", "ydiag_ready", "yspread_ready", "inv_s_ready"))
        z_silu, cum_split, yn_ready, yhi_ready, yssd_ready = sem("z_silu"), sem("cum_split"), sem("yn_ready"), sem("yhi_ready"), sem("yssd_ready")
        gate_ready, pooled_ready, pooled_hi, pooled_operand = (sem(n) for n in ("gate_ready", "pooled_ready", "pooled_hi", "pooled_operand"))
        pw_ready, pw_hi, pw_operand = sem("pw_ready"), sem("pw_hi"), sem("pw_operand")
        parts_ready, merged_ready, merged_hi, merged_operand = (sem(n) for n in ("parts_ready", "merged_ready", "merged_hi", "merged_operand"))

        POOL_AT = (1, 4, 6, 9)

        def gate_at(m):
            return S_GATE + m + (2 if m >= GATES_FIRST else 0)

        def in_group(n, per, g, it):
            return val(n + per * g, it, per)

        def ssd_pe(pe):
            for k in range(NT):
                sum_squares(pe, 4, k)
            spread_inv(pe, 4)
            slab_gemm(pe, S_DT, ps[:, 4, 0:SEQ], a_hi, a_lo, each=ready(a_ready, 4 * NT)(pe))

            def slab(j, g, it):
                if j < 2 and g:
                    pe.wait_ge(z_done, in_group(j + 3, 4, g - 1, it))
                elif 2 <= j < 4 and g:
                    pe.wait_ge(u_done, in_group(j - 1, 2, g - 1, it))
                elif 4 <= j < 10:
                    pe.wait_ge(conv_done, in_group(j - 3, 6, g, it))
                elif j >= 10:
                    pe.wait_ge(z_done, in_group(j - 9, 4, g, it))
                slab_gemm(pe, S_GRP + GRP * g + j, ps[:, j % 4, 0:SEQ], a_hi, a_lo, it, GRP)

            def tail_sums(g, it):
                pe.wait_ge(ysq_ready, in_group(1, 1, g, it))
                for b in range(NB):
                    for t in range(4):
                        mm = pe.matmul(ps[:, 5, b:b + 1], sq[:, t, b * P:(b + 1) * P], ones[:, 0:1], start=(t == 0), stop=(t == 3))
                mm.then_inc(ysum_ready, 1)

            def tail_spread(g, it):
                pe.wait_ge(ydiag_ready, in_group(1, 1, g, it))
                pe.matmul(ps[:, 6, 0:SEQ], ones, diag[:, 2:4].rearrange("p b t -> p (b t)"), start=True, stop=True).then_inc(yspread_ready, 1)

            def group(g, it=None):
                def products():
                    if g:
                        pe.wait_ge(yz_ready, in_group(1, 1, g - 1, it))
                    else:
                        pe.wait_ge(dt_x_ready, 1)
                    pe.wait_ge(act_done, in_group(2, 6, g, it))
                    for b in range(NB):
                        mm = pe.matmul(ps[:, 4, b * SEQ:b * SEQ + SEQ - b * P], cv[:, 0, b * P:(b + 1) * P], cv[:, 1, b * P:SEQ],
                                       start=True, stop=True)
                    mm.then_inc(cb_ready, 1)

                def own():
                    pe.wait_ge(cb_copied, in_group(1, 1, g, it))
                    pe.wait_ge(dt_ready, 2)
                    at = CC["ident"] + g * GROUP_HEADS
                    sel = con[0:SSD_HEADS, at:at + GROUP_HEADS] if it is None else con[0:SSD_HEADS, bass.ds(it * GROUP_HEADS + at, GROUP_HEADS)]
                    for n, src in enumerate([dt_f, cum]):
                        for b in range(NB):
                            c = 400 + GROUP_HEADS * (2 * n + b)
                            mm = pe.matmul(ps[:, 4, c:c + GROUP_HEADS], src[0:SSD_HEADS, b * P:(b + 1) * P], sel, start=True, stop=True)
                    mm.then_inc(own_ready, 1)

                def turn():
                    pe.wait_ge(act_done, in_group(6, 6, g, it))
                    if g:
                        pe.wait_ge(inv_s_ready, in_group(1, 1, g - 1, it))
                    for b in range(NB):
                        for t in range(4):
                            mm = pe.transpose(ps[:, 5 + b, t * P:(t + 1) * P], cv[:, 2 + t, b * P:(b + 1) * P], ident)
                        mm.then_inc(x_turned, 1)

                def spread_cum(j):
                    if j == 0:
                        pe.wait_ge(pick_ready, in_group(1, 1, g, it))
                        pe.wait_ge(cum_split, 2)
                    if j < 2:
                        pe.wait_ge(x_tok_ready, in_group(j + 1, 2, g, it))
                    else:
                        pe.wait_ge(exp_done, in_group(2 * j - 2, 16, g, it))
                    o = ps[:, 5 + j % 2, 0:SEEN]
                    pe.matmul(o, ident_b[:, :], tri[:, :], start=True, stop=False)
                    pe.matmul(o, pick_h[:, j], cum_hi, start=False, stop=False)
                    pe.matmul(o, pick_h[:, j], cum_lo, start=False, stop=True).then_inc(cum_ready, 1)

                def head(j):
                    pe.wait_ge(seen_ready, in_group(j + 1, 8, g, it))
                    if j == 4:
                        pe.wait_ge(own_copied, in_group(1, 1, g, it))
                    o = ps[SSD_P * (j % 2):SSD_P * (j % 2) + SSD_P, 7 if j < 4 else 4, (j // 2 % 2) * SEQ:(j // 2 % 2 + 1) * SEQ]
                    c = slice(j * SSD_P, (j + 1) * SSD_P)
                    pe.matmul(o[:, 0:P], x_tok2[:, 0, c], seen[:, j % 2, 0:P], start=True, stop=True)
                    pe.matmul(o[:, P:SEQ], x_tok2[:, 0, c], seen[:, j % 2, P:SEQ], start=True, stop=False)
                    pe.matmul(o[:, P:SEQ], x_tok2[:, 1, c], seen[:, j % 2, SEQ:SEEN], start=False, stop=True).then_inc(y_done, 1)

                for j in range(GRP):
                    slab(j, g, it)
                    if j == 1 and g:
                        tail_sums(g - 1, it)
                    if j == 3 and g:
                        tail_spread(g - 1, it)
                    if j == 4:
                        products()
                    if j == 5:
                        own()
                    if j == 6:
                        turn()
                    if j == 7:
                        spread_cum(0)
                        spread_cum(1)
                    if j >= 8:
                        for k in (2 * (j - 8), 2 * (j - 8) + 1):
                            head(k)
                            if k + 2 < GROUP_HEADS:
                                spread_cum(k + 2)

            group(0)
            with pe.Fori(0, GROUPS - 1) as it:
                group(1, it)

            def pools():
                pe.wait_ge(pooled_operand, GROUPS)
                pe.wait_ge(yssd_ready, GROUPS)
                for a in range(2):
                    s = S_POOL + a
                    slab_ready(pe, s)
                    for n in range(4):
                        for k in range(2):
                            t = slice((2 * n + k) * P, (2 * n + k + 1) * P)
                            i = 4 * a + 2 * (n // 2) + k
                            mm = mm3(pe, ps[:, 4 + 2 * a + n // 2, (n % 2) * SEQ:(n % 2 + 1) * SEQ], w_hi[:, s % RING, t], w_lo[:, s % RING, t],
                                     c_hi[:, i], c_lo[:, i], k == 0, k == 1)
                    mm.then_inc(w_used, 1)

            for m in range(2 * NT):
                if m == GATES_FIRST:
                    pools()
                if m < 2:
                    pe.wait_ge(z_done, 4 * GROUPS)
                elif m < 4:
                    pe.wait_ge(u_done, 2 * GROUPS)
                else:
                    pe.wait_ge(gate_ready, m - 3)
                slab_gemm(pe, gate_at(m), ps[:, m % 4, 0:SEQ], a_hi, a_lo)
                if m == 1:
                    tail_sums(GROUPS - 1, None)
                if m == 3:
                    tail_spread(GROUPS - 1, None)
            pe.wait_ge(gate_ready, 2 * NT)
            pe.wait_ge(pw_operand, NT)
            pe.sem_inc(parts_ready, 2)
            with pe.Fori(0, NT // 2) as it:
                for u in range(2):
                    pe.wait_ge(parts_ready, val(u + 1, it, 2))
                    s = S_MERGE + 3 * u
                    slab_gemm(pe, s, ps[:, 2 * u, 0:SEQ], b_hi, b_lo, it, 6, last=False)
                    slab_gemm(pe, s + 1, ps[:, 2 * u, 0:SEQ], b_hi[:, NT:2 * NT], b_lo[:, NT:2 * NT], it, 6, first=False)
                    slab_gemm(pe, s + 2, ps[:, 2 * u + 1, 0:SEQ], c_hi, c_lo, it, 6)
            out_pe(pe, S_WOUT, False, a_hi, a_lo, res_ready, 5 * NT, (ready(merged_operand, 0)(pe),))

        def ssd_act(act):
            act_inv(act, 4)
            mod_act(act, 4)
            hi_ahead(act, S_DT + 3)
            act.wait_ge(dt_x_ready, 1)
            act.activation(dt_e[0:SSD_HEADS, :], dt_e[0:SSD_HEADS, :], ACT.Exp, scale=-1.0).then_inc(dt_e_ready, 1)
            act.activation(neg_a[0:SSD_HEADS, :], pcol("a_log", 0, SSD_HEADS), ACT.Exp).then_inc(decay_a, 1)
            def tail(j, g, it):
                if j == 0:
                    act.wait_ge(z_done, in_group(4, 4, g, it))
                    act.activation(z_s, z_s, ACT.Silu).then_inc(z_silu, 1)
                if j == 1:
                    act.wait_ge(yz_ready, in_group(1, 1, g, it))
                    act.activation(sq[:, 0:4], z_s, ACT.Square).then_inc(ysq_ready, 1)
                if j == 3:
                    act.wait_ge(var_ready, in_group(RS_SSD + 1, 1, g, it))
                    act.activation(rs_root[:, 0:NB], rs_var[:, 0:NB], ACT.Sqrt).then_inc(root_ready, 1)
                if j == 5:
                    act.wait_ge(yspread_ready, in_group(1, 1, g, it))
                    act.activation(inv_s, ps[:, 6, 0:SEQ], ACT.Copy).then_inc(inv_s_ready, 1)
                if j == 6:
                    act.wait_ge(yn_ready, in_group(1, 1, g, it))
                    o = slice(4 * g, 4 * g + 4) if it is None else bass.ds(it * 4 + 4 * g, 4)
                    act.activation(b_hi[:, o], y_f, ACT.Copy).then_inc(yhi_ready, 1)

            def group(g, it=None):
                def prm(t, j):
                    c = COL["grp"] + 38 * g + 5 * t + j
                    return par[:, c:c + 1] if it is None else par[:, bass.ds(it * 38 + c, 1)]

                def used(j):
                    act.wait_ge(w_used, val(S_GRP + GRP * g + j + 1, it, GRP))

                def exps(j):
                    act.wait_ge(cum_ready, in_group(j + 1, 8, g, it))
                    if j == 0:
                        act.wait_ge(own_copied, in_group(1, 1, g, it))
                    if j >= 2:
                        act.wait_ge(y_done, in_group(j - 1, 8, g, it))
                    for b in range(NB):
                        c = slice(0, SEQ) if b == 0 else slice(SEQ, SEEN)
                        act.activation(seen[:, j % 2, c], ps[:, 5 + j % 2, c], ACT.Exp, bias=neg_cum[:, b, j:j + 1]).then_inc(exp_done, 1)

                for j in range(GRP):
                    if g:
                        tail(j, g - 1, it)
                    split_hi(act, S_GRP + GRP * g + j + 3, it, GRP)
                    if j == 5:
                        act.wait_ge(cb_ready, in_group(1, 1, g, it))
                        act.activation(cb, ps[:, 4, 0:SEEN], ACT.Copy).then_inc(cb_copied, 1)
                    if j == 5 and g == 0:
                        act.wait_ge(dt_ready, 2)
                        act.activation(cum_hi, cum[0:SSD_HEADS, :], ACT.Copy).then_inc(cum_split, 1)
                    if j >= 8:
                        exps(2 * (j - 8))
                        exps(2 * (j - 8) + 1)
                    used(j)
                    if j < 6:
                        act.activation(cv[:, j], ps[:, j % 4, 0:SEQ], ACT.Identity, bias=prm(j, 4), scale=prm(j, 3)).then_inc(tap_done, 1)
                    elif j < 10:
                        act.activation(z_s[:, j - 6], ps[:, j % 4, 0:SEQ], ACT.Copy).then_inc(z_done, 1)
                    else:
                        o = u_f[:, 2 * g + j - 10] if it is None else u_f[:, bass.ds(it * 2 + 2 * g + j - 10, 1)].rearrange("p a t -> p (a t)")
                        act.activation(o, ps[:, j % 4, 0:SEQ], ACT.Copy).then_inc(u_done, 1)
                    if 1 <= j < 7:
                        act.wait_ge(conv_done, in_group(j, 6, g, it))
                        act.activation(cv[:, j - 1], cv[:, j - 1], ACT.Silu).then_inc(act_done, 1)

            group(0)
            with act.Fori(0, GROUPS - 1) as it:
                group(1, it)

            def pools():
                for a in range(2):
                    hi_ahead(act, S_POOL + a + 3)
                    act.wait_ge(w_used, S_POOL + a + 1)
                    for n in range(4):
                        act.activation(sq[:, 4 * a + n], ps[:, 4 + 2 * a + n // 2, (n % 2) * SEQ:(n % 2 + 1) * SEQ], ACT.Copy,
                                       scale=pcol("pool_scale", 4 * a + n)).then_inc(pw_ready, 1)
                    act.wait_ge(pw_ready, 4 * a + 4)
                    act.activation(c_hi[:, 4 * a:4 * a + 4], sq[:, 4 * a:4 * a + 4], ACT.Copy).then_inc(pw_hi, 1)

            for m in range(2 * NT):
                if m == GATES_FIRST:
                    pools()
                tail(m, GROUPS - 1, None)
                hi_ahead(act, gate_at(m) + 3)
                act.wait_ge(w_used, gate_at(m) + 1)
                if m == NT:
                    act.wait_ge(yssd_ready, GROUPS)
                act.activation(gates[:, (m + NT) % (2 * NT)], ps[:, m % 4, 0:SEQ], ACT.Sigmoid).then_inc(gate_ready, 1)
                if m - 1 in POOL_AT:
                    g = POOL_AT.index(m - 1)
                    act.wait_ge(pooled_ready, g + 1)
                    act.activation(c_hi[:, 2 * g:2 * g + 2], win_of(g), ACT.Copy).then_inc(pooled_hi, 1)
            with act.Fori(0, NT // 2) as it:
                for u in range(2):
                    for n in range(3):
                        split_hi(act, S_MERGE + 3 * u + n + 3, it, 6)
                    act.wait_ge(merged_ready, val(u + 1, it, 2))
                    act.activation(a_hi[:, bass.ds(it * 2 + u, 1)].rearrange("p a t -> p (a t)"), merged[:, u], ACT.Copy).then_inc(merged_hi, 1)
            load_root_table(act, 5)
            for m in range(NT):
                hi_ahead(act, S_WOUT + m + 3)
                square(act, 5, m)

        def win_of(g):
            return win[g % 2]

        def ssd_vec(dve, step):
            mod_vec(dve, step, 4)
            lo_ahead(dve, S_DT + 3)
            h = slice(0, SSD_HEADS)
            dve.wait_ge(w_used, S_DT + 1)
            step(dve.tensor_scalar(dt_x[h], ps[h, 4, 0:SEQ], pcol("dt_bias", 0, SSD_HEADS), None, ALU.add))
            dve.scalar_tensor_tensor(out=dt_e[h], in0=dt_x[h], scalar=-1.0, in1=dt_x[h], op0=ALU.mult, op1=ALU.max).then_inc(dt_x_ready, 1)

            def softplus_series():
                dve.wait_ge(dt_e_ready, 1)
                step(dve.tensor_scalar(dt_z[h], dt_e[h], 2.0, None, ALU.add))
                step(dve.reciprocal(dt_z[h], dt_z[h]))
                step(dve.tensor_tensor(dt_z[h], dt_z[h], dt_e[h], ALU.mult))
                step(dve.tensor_tensor(dt_e[h], dt_z[h], dt_z[h], ALU.mult))
                step(dve.tensor_scalar(dt_f[h], dt_e[h], 1.0 / 15, None, ALU.mult))
                for n in range(13, 1, -2):
                    step(dve.scalar_tensor_tensor(out=dt_f[h], in0=dt_f[h], scalar=1.0 / n, in1=dt_e[h], op0=ALU.add, op1=ALU.mult))

            def softplus_and_cum():
                step(dve.scalar_tensor_tensor(out=dt_f[h], in0=dt_f[h], scalar=1.0, in1=dt_z[h], op0=ALU.add, op1=ALU.mult))
                step(dve.tensor_scalar(dt_f[h], dt_f[h], 2.0, None, ALU.mult))
                step(dve.scalar_tensor_tensor(out=dt_f[h], in0=dt_x[h], scalar=0.0, in1=dt_f[h], op0=ALU.max, op1=ALU.add))
                dve.wait_ge(decay_a, 1)
                step(dve.tensor_scalar(dt_x[h], dt_f[h], neg_a[h, 0:1], -1.0, ALU.mult, ALU.mult))
                step(dve.memset(dt_e[h], 1.0))
                dve.tensor_tensor_scan(cum[h, 0:SEQ], dt_e[h], dt_x[h], 0.0, ALU.mult, ALU.add).then_inc(dt_ready, 1)
                dve.wait_ge(dt_ready, 1)
                dve.tensor_copy(cum[h, SEQ:SEEN], cum[h, P:SEQ]).then_inc(dt_ready, 1)
                dve.wait_ge(dt_ready, 2)

            def split_cum():
                dve.wait_ge(cum_split, 1)
                dve.tensor_tensor(cum_lo, cum[h, :], cum_hi.bitcast(F32), ALU.subtract).then_inc(cum_split, 1)

            def prm(c, g, it):
                c += COL["grp"] + 38 * g
                return par[:, c:c + 1] if it is None else par[:, bass.ds(it * 38 + c, 1)]

            def skip(t, g, it):
                dve.wait_ge(y_done, in_group(4 * (t // 2) + 4, 8, g, it))
                step(dve.scalar_tensor_tensor(out=cv[:, 2 + t], in0=cv[:, 2 + t], scalar=prm(30 + t, g, it),
                                              in1=ps[:, 4 if t // 2 else 7, (t % 2) * SEQ:(t % 2 + 1) * SEQ], op0=ALU.mult, op1=ALU.add))

            def tail(j, g, it):
                if j == 0:
                    skip(2, g, it)
                    skip(3, g, it)
                    dve.wait_ge(z_silu, in_group(1, 1, g, it))
                    dve.tensor_tensor(z_s, cv[:, 2:6], z_s, ALU.mult).then_inc(yz_ready, 1)
                if j == 2:
                    dve.wait_ge(ysum_ready, in_group(1, 1, g, it))
                    dve.tensor_scalar(rs_var[:, 0:NB], ps[:, 5, 0:NB], 1.0 / 512, EPS_B, ALU.mult, ALU.add).then_inc(var_ready, 1)
                if j == 3:
                    rsqrt(dve, step, RS_SSD + g, NB, root_s, it)
                    step(dve.tensor_scalar(diag[:, 2], ident, root_s[:, 0:1], None, ALU.mult))
                    dve.tensor_scalar(diag[:, 3], ident, root_s[:, 1:2], None, ALU.mult).then_inc(ydiag_ready, 1)
                if j == 5:
                    dve.wait_ge(inv_s_ready, in_group(1, 1, g, it))
                    for t in range(4):
                        ins = dve.scalar_tensor_tensor(out=y_f[:, t], in0=z_s[:, t], scalar=prm(34 + t, g, it), in1=inv_s,
                                                       op0=ALU.mult, op1=ALU.mult)
                    ins.then_inc(yn_ready, 1)
                if j == 7:
                    dve.wait_ge(yhi_ready, in_group(1, 1, g, it))
                    o = slice(4 * g, 4 * g + 4) if it is None else bass.ds(it * 4 + 4 * g, 4)
                    dve.tensor_tensor(b_lo[:, o], y_f, b_hi[:, o].bitcast(F32), ALU.subtract).then_inc(yssd_ready, 1)

            def group(g, it=None):
                at = CC["ident"] + g * GROUP_HEADS
                own = con[h, at:at + GROUP_HEADS] if it is None else con[h, bass.ds(it * GROUP_HEADS + at, GROUP_HEADS)]
                for j in range(GRP):
                    if g:
                        tail(j, g - 1, it)
                    elif j in (0, 1, 6):
                        {0: softplus_series, 1: softplus_and_cum, 6: split_cum}[j]()
                    split_lo(dve, S_GRP + GRP * g + j + 3, it, GRP)
                    if j == 0:
                        dve.tensor_copy(pick_h, own.unsqueeze(2).broadcast_to((SSD_HEADS, GROUP_HEADS, P))).then_inc(pick_ready, 1)
                    if j < 6:
                        dve.wait_ge(tap_done, in_group(j + 1, 6, g, it))
                        for n in range(1, 4):
                            ins = dve.scalar_tensor_tensor(out=cv[:, j, n:SEQ], in0=ps[:, j % 4, 0:SEQ - n], scalar=prm(5 * j + 3 - n, g, it),
                                                           in1=cv[:, j, n:SEQ], op0=ALU.mult, op1=ALU.add)
                            if n < 3:
                                step(ins)
                        ins.then_inc(conv_done, 1)
                    if j == 6:
                        dve.wait_ge(own_ready, in_group(1, 1, g, it))
                        step(dve.tensor_copy(dt_tok.rearrange("p b h -> p (b h)"), ps[:, 4, 400:416]))
                        dve.tensor_scalar(neg_cum.rearrange("p b h -> p (b h)"), ps[:, 4, 416:432], -1.0, None, ALU.mult).then_inc(own_copied, 1)
                    if j == 7:
                        for b in range(NB):
                            dve.wait_ge(x_turned, in_group(b + 1, 2, g, it))
                            dve.tensor_tensor(x_tok2[:, b].rearrange("p (h d) -> p h d", h=GROUP_HEADS),
                                              ps[:, 5 + b, :].rearrange("p (h d) -> p h d", h=GROUP_HEADS),
                                              dt_tok[:, b].unsqueeze(2).broadcast_to((P, GROUP_HEADS, SSD_P)), ALU.mult).then_inc(x_tok_ready, 1)
                    if j >= 8:
                        for k in (2 * (j - 8), 2 * (j - 8) + 1):
                            dve.wait_ge(exp_done, in_group(2 * k + 2, 16, g, it))
                            dve.tensor_tensor(seen[:, k % 2], seen[:, k % 2], cb, ALU.mult).then_inc(seen_ready, 1)
                    if j == 11:
                        skip(0, g, it)
                        skip(1, g, it)

            group(0)
            with dve.Fori(0, GROUPS - 1) as it:
                step.enter(it, 22)
                group(1, it)
            step.leave(GROUPS - 1)
            dve.wait_ge(u_done, 2 * GROUPS)

            def pool(g):
                u = u_f[:, 2 * g:2 * g + 2]
                cur = u
                for i in range(g + 1):
                    nxt = win[i % 2]
                    dve.tensor_copy(nxt[:, :, 0:2 ** i], cur[:, :, 0:2 ** i])
                    step(dve.tensor_tensor(nxt[:, :, 2 ** i:SEQ], cur[:, :, 2 ** i:SEQ], cur[:, :, 0:SEQ - 2 ** i], ALU.add))
                    cur = nxt
                for t in range(2):
                    ins = dve.tensor_tensor(cur[:, t, 0:16], cur[:, t, 0:16], const("ramp", 16, at=16 * g), ALU.mult)
                step(ins)
                dve.scalar_tensor_tensor(out=cur, in0=cur, scalar=0.5 ** (g + 1), in1=u, op0=ALU.mult, op1=ALU.subtract).then_inc(pooled_ready, 1)
                dve.wait_ge(pooled_ready, g + 1)

            def pooled_lo(g):
                dve.wait_ge(pooled_hi, g + 1)
                dve.tensor_tensor(c_lo[:, 2 * g:2 * g + 2], win_of(g), c_hi[:, 2 * g:2 * g + 2].bitcast(F32), ALU.subtract).then_inc(pooled_operand, 1)
                dve.wait_ge(pooled_operand, g + 1)

            def pools():
                for a in range(2):
                    lo_ahead(dve, S_POOL + a + 3)
                    dve.wait_ge(pw_hi, a + 1)
                    dve.tensor_tensor(c_lo[:, 4 * a:4 * a + 4], sq[:, 4 * a:4 * a + 4], c_hi[:, 4 * a:4 * a + 4].bitcast(F32),
                                      ALU.subtract).then_inc(pw_operand, 4)

            for m in range(2 * NT):
                if m == GATES_FIRST:
                    pools()
                tail(m, GROUPS - 1, None)
                lo_ahead(dve, gate_at(m) + 3)
                if m in POOL_AT:
                    pool(POOL_AT.index(m))
                if m - 1 in POOL_AT:
                    pooled_lo(POOL_AT.index(m - 1))
            with dve.Fori(0, NT // 2) as it:
                step.enter(it, 0)
                for u in range(2):
                    for n in range(3):
                        split_lo(dve, S_MERGE + 3 * u + n + 3, it, 6)
                    dve.wait_ge(w_used, val(S_MERGE + 3 * u + 3, it, 6))
                    dve.tensor_tensor(part[:, u, 0], ps[:, 2 * u, 0:SEQ], gates[:, bass.ds(it * 2 + NT + u, 1)].rearrange("p a t -> p (a t)"), ALU.mult)
                    dve.tensor_tensor(part[:, u, 1], ps[:, 2 * u + 1, 0:SEQ], gates[:, bass.ds(it * 2 + u, 1)].rearrange("p a t -> p (a t)"),
                                      ALU.mult).then_inc(parts_ready, 1)
                    dve.wait_ge(parts_ready, val(u + 3, it, 2))
                    dve.tensor_tensor(merged[:, u], part[:, u, 0], part[:, u, 1], ALU.add).then_inc(merged_ready, 1)
                    dve.wait_ge(merged_hi, val(u + 1, it, 2))
                    o = bass.ds(it * 2 + u, 1)
                    dve.tensor_tensor(a_lo[:, o].rearrange("p a t -> p (a t)"), merged[:, u], a_hi[:, o].bitcast(F32).rearrange("p a t -> p (a t)"),
                                      ALU.subtract).then_inc(merged_operand, 1)
            step.leave(NT // 2)
            for m in range(NT):
                lo_ahead(dve, S_WOUT + m + 3)
                dve.wait_ge(w_used, S_WOUT + m + 1)
                dve.scalar_tensor_tensor(out=res[:, m], in0=ps[:, 4 + (m + 2) % 4, 0:SEQ], scalar=mod[:, 2 * NT + m:2 * NT + m + 1], in1=res[:, m],
                                         op0=ALU.mult, op1=ALU.add).then_inc(res_ready, 1)

        top[0] = 0
        relu, hidden = area(3, SEQ), area(3, SEQ)
        normal = area(NT, SEQ)
        result = area(NB, DM)
        relu_ready, hidden_ready, hidden_hi, hidden_operand = (
            sem(n) for n in ("relu_ready", "hidden_ready", "hidden_hi", "hidden_operand"))
        normal_ready, normal_turned, block_0_ready, block_1_ready, stored = (
            sem(n) for n in ("normal_ready", "normal_turned", "block_0_ready", "block_1_ready", "stored"))
        MLP_TURNS = (MLP_TILES - 5) // 3

        def up_at(n):
            return S_MLP + (n if n < 2 else 2 * n - 2)

        def down_at(n):
            return S_MLP + (2 * n + 3 if n < MLP_TILES - 2 else MLP_TILES + n)

        def mlp_pe(pe):
            def up_tile(n, it=None, each=None):
                slab_gemm(pe, up_at(n), ps[:, 4 + n % 3, 0:SEQ], a_hi, a_lo, it, 6, each=each)

            def down(n, it=None):
                pe.wait_ge(hidden_operand, val(n + 1, it, 3))
                down_slab(pe, down_at(n), b_hi[:, n % 3], b_lo[:, n % 3], n == 0, n == MLP_TILES - 1, it, 6)

            for k in range(NT):
                sum_squares(pe, 5, k)
            spread_inv(pe, 5)
            up_tile(0, each=ready(a_ready, 5 * NT)(pe))
            up_tile(1)
            for n in range(3):
                up_tile(n + 2)
                down(n)
            with pe.Fori(0, MLP_TURNS) as it:
                for n in range(3, 6):
                    up_tile(n + 2, it)
                    down(n, it)
            for n in range(3 + 3 * MLP_TURNS, MLP_TILES):
                if n + 2 < MLP_TILES:
                    up_tile(n + 2)
                down(n)
            for k in range(NT):
                sum_squares(pe, 6, k)
            spread_inv(pe, 6)
            pe.wait_ge(res_ready, 7 * NT)
            for q in range(NT // 4):
                for m in range(4 * q, 4 * q + 4):
                    pe.wait_ge(normal_ready, m + 1)
                    for b in range(NB):
                        mm = pe.transpose(ps[:, 2 * q + b, (m % 4) * P:(m % 4 + 1) * P], normal[:, m, b * P:(b + 1) * P], ident)
                mm.then_inc(normal_turned, 1)

        def mlp_act(act):
            act_inv(act, 5)
            mod_act(act, 5)

            def relu_of(n, it=None):
                act.wait_ge(w_used, val(up_at(n) + 1, it, 6))
                if n >= 3:
                    act.wait_ge(hidden_ready, val(n - 2, it, 3))
                act.activation(relu[:, n % 3], ps[:, 4 + n % 3, 0:SEQ], ACT.Relu).then_inc(relu_ready, 1)

            def high(n, it=None):
                act.wait_ge(hidden_ready, val(n + 1, it, 3))
                if n >= 3:
                    act.wait_ge(w_used, val(down_at(n - 3) + 1, it, 6))
                act.activation(b_hi[:, n % 3], hidden[:, n % 3], ACT.Copy).then_inc(hidden_hi, 1)

            def tile(n, it=None):
                hi_ahead(act, up_at(n) + 3, it, 6)
                relu_of(n, it)
                high(n, it)
                if n >= 2:
                    hi_ahead(act, down_at(n - 2) + 3, it, 6)

            for n in range(5):
                tile(n)
            with act.Fori(0, MLP_TURNS - 1) as it:
                for n in range(5, 8):
                    tile(n, it)
            for n in range(2 + 3 * MLP_TURNS, MLP_TILES):
                tile(n)
            load_root_table(act, 6)
            for m in range(NT):
                square(act, 6, m)
            act_inv(act, 6)
            for q in range(NT // 4):
                act.wait_ge(normal_turned, q + 1)
                act.activation(result[:, 1, 512 * q:512 * (q + 1)], ps[:, 2 * q + 1, :], ACT.Copy).then_inc(block_1_ready, 1)

        def mlp_vec(dve, step):
            mod_vec(dve, step, 5)

            def hidden_of(n, it=None):
                dve.wait_ge(relu_ready, val(n + 1, it, 3))
                if n >= 3:
                    dve.wait_ge(hidden_operand, val(n - 2, it, 3))
                dve.tensor_tensor(hidden[:, n % 3], relu[:, n % 3], relu[:, n % 3], ALU.mult).then_inc(hidden_ready, 1)

            def low(n, it=None):
                dve.wait_ge(hidden_hi, val(n + 1, it, 3))
                dve.tensor_tensor(b_lo[:, n % 3], hidden[:, n % 3], b_hi[:, n % 3].bitcast(F32), ALU.subtract).then_inc(hidden_operand, 1)

            def tile(n, it=None):
                lo_ahead(dve, up_at(n) + 3, it, 6)
                hidden_of(n, it)
                if n >= 2:
                    lo_ahead(dve, down_at(n - 2) + 3, it, 6)
                low(n, it)

            for n in range(5):
                tile(n)
            with dve.Fori(0, MLP_TURNS - 1) as it:
                for n in range(5, 8):
                    tile(n, it)
            for n in range(2 + 3 * MLP_TURNS, MLP_TILES):
                tile(n)
            dve.wait_ge(w_used, SLABS)
            for m in range(NT):
                dve.scalar_tensor_tensor(out=res[:, m], in0=ps[:, m // 2, (m % 2) * SEQ:(m % 2 + 1) * SEQ],
                                         scalar=mod[:, 5 * NT + m:5 * NT + m + 1], in1=res[:, m],
                                         op0=ALU.mult, op1=ALU.add).then_inc(res_ready, 1)
            vec_inv(dve, step, 6, EPS_B)
            dve.wait_ge(inv_ready, 7)
            for m in range(NT):
                dve.scalar_tensor_tensor(out=normal[:, m], in0=res[:, m], scalar=pcol("final_w", m), in1=inv[:, :],
                                         op0=ALU.mult, op1=ALU.mult).then_inc(normal_ready, 1)
            for q in range(NT // 4):
                dve.wait_ge(normal_turned, q + 1)
                dve.tensor_copy(result[:, 0, 512 * q:512 * (q + 1)], ps[:, 2 * q, :]).then_inc(block_0_ready, 1)
        block = ctx.enter_context(nc.Block())

        @block.sync
        def _(sp):
            sp.dma_start(con[:, 0:CC["cos"]], consts[:, 0:CC["cos"]]).then_inc(small_in, 16)
            sp.dma_start(x_tok, x.rearrange("(b p) d -> p b d", p=P)).then_inc(x_in, 16)
            sp.dma_start(par[:, :], params).then_inc(par_in, 16)

            def load(s, it=None, ds=0):
                slot = s % RING
                if s >= RING:
                    sp.wait_ge(w_lo_ready, val(s - RING + 1, it, ds))
                src = stream[s] if it is None else stream[bass.ds(it * ds + s, 1)].rearrange("a p n -> (a p) n")
                sp.dma_start(w_raw[:, slot], src).then_inc(w_landed[slot], 16)

            def load_range(a, b):
                turns = (b - a) // RING
                if turns > 1:
                    with sp.Fori(0, turns) as it:
                        for u in range(RING):
                            load(a + u, it, RING)
                    a += turns * RING
                for s in range(a, b):
                    load(s)

            load_range(0, RING)
            sp.dma_start(con[:, CC["cos"]:CONSTS], consts[:, CC["cos"]:CONSTS]).then_inc(tables_in, 16)
            load_range(RING, S_FFN0 + RING)
            sp.wait_ge(res_ready, 2 * NT)
            sp.dma_start(cond_row, c_rows).then_inc(cond_in, 16)
            load_range(S_FFN0 + RING, SLABS)
            for q in range(NT // 4):
                sp.wait_ge(block_0_ready, q + 1)
                sp.wait_ge(block_1_ready, q + 1)
                sp.dma_start(out.rearrange("(b p) d -> p b d", p=P)[:, :, 512 * q:512 * (q + 1)],
                             result[:, :, 512 * q:512 * (q + 1)]).then_inc(stored, 16)
            sp.wait_ge(stored, 16 * (NT // 4))

        @block.tensor
        def _(pe):
            attention_pe(pe)
            ffn_pe(pe, 0, S_FFN0, 1)
            retention_pe(pe)
            ffn_pe(pe, 1, S_FFN1, 3)
            ssd_pe(pe)
            mlp_pe(pe)

        @block.scalar
        def _(act):
            attention_act(act)
            ffn_act(act, 0, S_FFN0, 1, "mix_g1")
            retention_act(act)
            ffn_act(act, 1, S_FFN1, 3, None)
            ssd_act(act)
            mlp_act(act)

        @block.gpsimd
        def _(pool):
            modulation_pool(pool, Steps(pool, pool_step))

        @block.vector
        def _(dve):
            step = Steps(dve, vec_step)
            attention_vec(dve, step)
            ffn_vec(dve, step, 0, S_FFN0, 1, "mix_g1")
            retention_vec(dve, step)
            ffn_vec(dve, step, 1, S_FFN1, 3, None)
            ssd_vec(dve, step)
            mlp_vec(dve, step)


def _tiles(w):
    k, m = w.shape
    t = w.reshape(k // P, P, m // P, P).transpose(2, 1, 0, 3)
    return t.reshape(m // P, P, k // SLAB, SLAB).transpose(0, 2, 1, 3).reshape(-1, P, SLAB)


def _rows(w):
    return w.reshape(-1, P, SLAB)


def _wide(w):
    return w.reshape(4, 2, P, 512).transpose(0, 2, 1, 3).reshape(4, P, SLAB)


def _mix(*parts):
    return np.stack(parts, axis=1).reshape(-1, P, SLAB)


def _stream(a):
    out = []
    w = a["a_w_in"][0]
    q, c, qi, ki, wi = np.split(w, [1024, 1152, 1664, 1728], axis=1)
    pad = np.zeros((DM, P - IDX_DIM - HEADS_A), w.dtype)
    out += [_tiles(np.concatenate([c, ki, wi, pad, qi, q], axis=1)), _tiles(a["a_w_out"][0])]

    def ffn(i):
        up, down = a["f_w_up"][i], _rows(a["f_w_down"][i])
        pairs = _mix(_tiles(up[:, :2816]), _tiles(up[:, 2816:]))
        for p in range(FF_PAIRS):
            out.append(pairs[2 * p:2 * p + 2])
            if p:
                out.append(down[p - 1:p])
        out.append(down[-1:])

    ffn(0)
    w = a["b_w_in"][0]
    for h in range(HEADS_B):
        out += [_tiles(w[:, 256 * h:256 * (h + 1)]), _tiles(w[:, DM + 256 * h:DM + 256 * (h + 1)]),
                _wide(w[:, 2 * DM + 512 * h:2 * DM + 512 * (h + 1)]), _tiles(w[:, 4 * DM + 512 * h:4 * DM + 512 * (h + 1)])]
    out.append(_tiles(a["b_w_out"][0]))
    ffn(1)
    z, xs, b, c, dt, u, gates = np.split(a["w_in_2"][0], [2048, 4096, 4608, 5120, 5152, 6176], axis=1)
    out.append(_tiles(np.concatenate([dt, np.zeros((DM, P - SSD_HEADS), dt.dtype)], axis=1)))
    for g in range(GROUPS):
        out.append(_tiles(np.concatenate([
            b[:, P * g:P * (g + 1)], c[:, P * g:P * (g + 1)], xs[:, 512 * g:512 * (g + 1)],
            z[:, 512 * g:512 * (g + 1)], u[:, 256 * g:256 * (g + 1)],
        ], axis=1)))
    gates = _tiles(gates)
    out.append(gates[:GATES_FIRST])
    out.append(a["pool_w_2"][0].reshape(2, 2, 2, P, 2, P).transpose(0, 3, 1, 4, 2, 5).reshape(2, P, SLAB))
    out.append(gates[GATES_FIRST:])
    ssd, pool = _tiles(a["w_branch_ssd_2"][0]), _tiles(a["w_branch_pool_2"][0])
    for m in range(NT):
        out += [ssd[2 * m:2 * m + 2], pool[m:m + 1]]
    out.append(_tiles(a["w_out_2"][0]))
    up, down = _tiles(a["w_up_2"][0]), _rows(a["w_down_2"][0])
    out.append(up[:2])
    for j in range(2, MLP_TILES):
        out += [up[j:j + 1], down[j - 2:j - 1]]
    out.append(down[-2:])
    out = np.concatenate(out)
    assert out.shape[0] == SLABS, out.shape
    return out


def _params(a):
    cols = np.zeros((P, PARAMS), np.float32)

    def put(name, rows, at=0):
        rows = np.asarray(rows)
        cols[:rows.shape[-1], COL[name] + at:COL[name] + at + rows.shape[0]] = rows.T

    for i in range(2):
        put(f"mix_g{i}", a["norm_mix_g"][i].reshape(-1, P))
        put(f"ffn_g{i}", a["norm_ffn_g"][i].reshape(-1, P))
        w, b = a["f_conv_w"][i].reshape(3, 2, FF_PAIRS, P), a["f_conv_b"][i].reshape(2, FF_PAIRS, P)
        for p in range(FF_PAIRS):
            put(f"ffn{i}", np.concatenate([w[:, 0, p], w[:, 1, p], b[:, p]]), 8 * p)
    put("q_g", a["a_q_g"])
    put("k_g", a["a_k_g"])
    put("iq_g", np.tile(a["a_iq_g"], 2))
    put("ik_g", np.tile(a["a_ik_g"], 2))
    put("out_g", a["b_out_g"][0].reshape(-1, P))
    put("b_ada", a["b_ada_2"][0].reshape(-1, P))
    put("mix_w", a["norm_mix_w_2"][0].reshape(-1, P))
    cw, cb = a["conv_w_2"][0].reshape(4, 24, P), a["conv_b_2"][0].reshape(1, 24, P)
    skip = np.repeat(a["d_skip_2"][0], SSD_P).reshape(-1, P)
    norm = a["ssd_norm_w_2"][0].reshape(-1, P)
    for g in range(GROUPS):
        for n, t in enumerate([16 + g, 20 + g, *range(4 * g, 4 * g + 4)]):
            put("grp", np.concatenate([cw[:, t], cb[:, t]]), 38 * g + 5 * n)
        put("grp", skip[4 * g:4 * g + 4], 38 * g + 30)
        put("grp", norm[4 * g:4 * g + 4], 38 * g + 34)
    put("dt_bias", a["dt_bias_2"])
    put("a_log", a["a_log_2"])
    put("pool_scale", a["pool_scale_2"][0].reshape(-1, P))
    put("mlp_w", a["norm_mlp_w_2"][0].reshape(-1, P))
    put("final_w", a["norm_final_w_2"].reshape(-1, P))
    return cols


def _consts():
    c = np.zeros((P, CONSTS), np.float32)
    i, t = np.arange(P), np.arange(SEQ)

    def put(name, x):
        c[:x.shape[0], CC[name]:CC[name] + x.shape[1]] = x

    put("ident", np.eye(P))
    put("ones", np.ones((P, P)))
    put("halves", (i[:, None] // IDX_DIM == np.arange(2)[None]).astype(np.float32))
    put("dup", np.tile(np.eye(IDX_DIM), (1, 2)))
    inv = (np.float32(1.0) / np.float32(10000.0) ** (np.arange(0, 256, 2, dtype=np.float32) / np.float32(256))).astype(np.float32)
    ang = (t.astype(np.float32)[None, :] * inv[:, None]).astype(np.float32).astype(np.float64)
    put("cos", np.cos(ang))
    put("sin", np.sin(ang))
    log_gamma = np.log1p(-(2.0 ** (-5.0 - np.arange(HEADS_B))))
    gap = np.concatenate([t[None, :] - i[:, None], t[None, P:] - i[:, None] - P], axis=1)
    for h in range(HEADS_B):
        d = np.where(gap >= 0, np.exp(np.maximum(gap, 0) * log_gamma[h]), 0.0) * 256.0 ** -0.5
        c[:, CC["decay"] + SEEN * h:CC["decay"] + SEEN * (h + 1)] = d
    limit = (t // 64 + 1) * 64
    put("admit", np.concatenate([
        np.where(i[None, :] < limit[:P, None], 0.0, MASKED), np.where(t[None, :] < limit[P:, None], 0.0, MASKED),
    ], axis=1))
    tri = np.where(i[None, :] >= i[:, None], 0.0, -1e30)
    put("tri", np.concatenate([tri, np.zeros((P, P)), tri], axis=1))
    for g in range(4):
        win = 2 ** (g + 1)
        c[:, CC["ramp"] + 16 * g:CC["ramp"] + 16 * (g + 1)] = win / np.minimum(np.arange(16) + 1, win)
    return c


_OUT = (1, SEQ, DM)


def kernel(**inputs):
    import concourse.bacc as _bacc
    from concourse.bass_utils import run_bass_kernel_spmd as _run

    a = {k: np.asarray(v) for k, v in inputs.items()}
    arrays = {"x": a["x"][0], "stream": _stream(a),
              "ada": np.ascontiguousarray(a["w_ada_2"][0].T).reshape(ADA_TILES, P, DM),
              "c_rows": np.broadcast_to(a["c_2"], (P, DM)).copy(), "params": _params(a), "consts": _consts()}
    nc = _bacc.Bacc("TRN2", target_bir_lowering=False, num_devices=1)
    args = {k: nc.dram_tensor(k, v.shape, F32, kind="ExternalInput").ap() for k, v in arrays.items()}
    out = nc.dram_tensor("out", (SEQ, DM), F32, kind="ExternalOutput").ap()
    build(nc, out=out, **args)
    r = _run(nc, [arrays], core_ids=[0])
    return np.asarray(r.results[0]["out"]).reshape(_OUT)
```
